# Optimizing a Trainium2 kernel written in Bass

```python
import math
import jax, jax.numpy as jnp
from jax import lax
import numpy as np

D_MODEL = 1024
BATCH = 1
SEQ = 512
DEPTH = 2

N_A_LAYERS = DEPTH // 2
N_B_LAYERS = DEPTH - N_A_LAYERS
CONV_WIDTH = 2 * D_MODEL
CONV_KERNEL = 31
N_HEADS = 16
QK_NOPE_DIM = 128
QK_ROPE_DIM = 64
V_HEAD_DIM = 128
KV_LORA_RANK = D_MODEL // 4
Q_LORA_RANK = D_MODEL // 2
ROPE_THETA = 10000.0
Q_BLOCK = 128
LN_EPS = 1e-5
RMS_EPS = 1e-6
MASK_VALUE = -1e30

kernel_name = "yoco_conformer_conv_mla_deepnorm"

def layer_norm(x, g, b):
    xf = x.astype(jnp.float32)
    mu = jnp.mean(xf, axis=-1, keepdims=True)
    var = jnp.mean(jnp.square(xf - mu), axis=-1, keepdims=True)
    return ((xf - mu) * lax.rsqrt(var + LN_EPS)).astype(x.dtype) * g + b

def rms_norm(x, g):
    xf = x.astype(jnp.float32)
    ms = jnp.mean(jnp.square(xf), axis=-1, keepdims=True)
    return (xf * lax.rsqrt(ms + RMS_EPS)).astype(x.dtype) * g

def rope_tables(positions, dtype):
    freqs = ROPE_THETA ** (-jnp.arange(0, QK_ROPE_DIM, 2, dtype=jnp.float32) / QK_ROPE_DIM)
    ang = positions.astype(jnp.float32)[..., None] * freqs
    return jnp.cos(ang).astype(dtype), jnp.sin(ang).astype(dtype)

def apply_rope(x, cos, sin):
    x1, x2 = jnp.split(x, 2, axis=-1)
    return jnp.concatenate([x1 * cos - x2 * sin, x2 * cos + x1 * sin], axis=-1)

def conformer_conv_branch(h, w_in, b_in, conv_w, conv_b, norm_g, norm_b, w_out, b_out):
    proj = h @ w_in + b_in
    val, glu_gate, z = jnp.split(proj, 3, axis=-1)
    u = val * jax.nn.sigmoid(glu_gate)
    u = lax.conv_general_dilated(
        u, conv_w[:, None, :], window_strides=(1,), padding=[(CONV_KERNEL - 1, 0)],
        dimension_numbers=('NWC', 'WIO', 'NWC'), feature_group_count=CONV_WIDTH) + conv_b
    u = jax.nn.silu(layer_norm(u, norm_g, norm_b))
    u = u * jax.nn.silu(z)
    return u @ w_out + b_out

def shared_latent_kv(h, w_down, kv_norm_g, w_uk, w_uv, cos, sin):
    ckv_kr = h @ w_down
    c_kv, k_rope = jnp.split(ckv_kr, [KV_LORA_RANK], axis=-1)
    c_kv = rms_norm(c_kv, kv_norm_g)
    k_nope = jnp.einsum('bsr,rhd->bshd', c_kv, w_uk)
    v = jnp.einsum('bsr,rhd->bshd', c_kv, w_uv)
    k_rope = apply_rope(k_rope, cos, sin)
    return k_nope, k_rope, v

def causal_mla_attention(q_nope, q_rope, k_nope, k_rope, v):
    scale = 1.0 / math.sqrt(QK_NOPE_DIM + QK_ROPE_DIM)
    seq = q_nope.shape[1]
    outs = []
    for blk in range(seq // Q_BLOCK):
        q0 = blk * Q_BLOCK
        kend = q0 + Q_BLOCK
        s = (jnp.einsum('bqhd,bkhd->bhqk', q_nope[:, q0:kend], k_nope[:, :kend])
             + jnp.einsum('bqhr,bkr->bhqk', q_rope[:, q0:kend], k_rope[:, :kend]))
        s = s.astype(jnp.float32) * scale
        mask = jnp.arange(kend)[None, :] <= (q0 + jnp.arange(Q_BLOCK))[:, None]
        s = jnp.where(mask, s, MASK_VALUE)
        p = jax.nn.softmax(s, axis=-1).astype(v.dtype)
        outs.append(jnp.einsum('bhqk,bkhd->bqhd', p, v[:, :kend]))
    return jnp.concatenate(outs, axis=1)

def mla_branch(h, k_nope, k_rope, v, w_in, q_norm_g, w_uq, w_out, cos, sin):
    bsz, seq, _ = h.shape
    proj = h @ w_in
    c_q, z = jnp.split(proj, [Q_LORA_RANK], axis=-1)
    q = jnp.einsum('bsr,rhd->bshd', rms_norm(c_q, q_norm_g), w_uq)
    q_nope, q_rope = jnp.split(q, [QK_NOPE_DIM], axis=-1)
    q_rope = apply_rope(q_rope, cos[:, :, None, :], sin[:, :, None, :])
    o = causal_mla_attention(q_nope, q_rope, k_nope, k_rope, v)
    o = o.reshape(bsz, seq, N_HEADS * V_HEAD_DIM) * jax.nn.silu(z)
    return o @ w_out

def setup_inputs(seed: int = 0) -> dict:
    key = jax.random.key(seed)
    ks = jax.random.split(key, 20)
    f32 = jnp.float32
    beta = (8.0 * DEPTH) ** -0.25
    E = CONV_WIDTH
    HV = N_HEADS * V_HEAD_DIM

    def dense(k, shape, fan_in, scale=1.0):
        return jax.random.normal(k, shape, f32) * (scale * fan_in ** -0.5)

    def gain(k, shape):
        return 1.0 + 0.02 * jax.random.normal(k, shape, f32)

    def small(k, shape):
        return 0.02 * jax.random.normal(k, shape, f32)

    return {
        "x": jax.random.normal(ks[0], (BATCH, SEQ, D_MODEL), f32),
        "positions": jnp.broadcast_to(jnp.arange(SEQ, dtype=jnp.int32), (BATCH, SEQ)),
        "ln_g": gain(ks[1], (DEPTH, D_MODEL)),
        "ln_b": small(ks[2], (DEPTH, D_MODEL)),
        "a_w_in": dense(ks[3], (N_A_LAYERS, D_MODEL, 3 * E), D_MODEL),
        "a_b_in": small(ks[4], (N_A_LAYERS, 3 * E)),
        "a_conv_w": dense(ks[5], (N_A_LAYERS, CONV_KERNEL, E), CONV_KERNEL),
        "a_conv_b": small(ks[6], (N_A_LAYERS, E)),
        "a_norm_g": gain(ks[7], (N_A_LAYERS, E)),
        "a_norm_b": small(ks[8], (N_A_LAYERS, E)),
        "a_w_out": dense(ks[9], (N_A_LAYERS, E, D_MODEL), E, beta),
        "a_b_out": small(ks[10], (N_A_LAYERS, D_MODEL)),
        "kv_w_down": dense(ks[11], (D_MODEL, KV_LORA_RANK + QK_ROPE_DIM), D_MODEL),
        "kv_norm_g": gain(ks[12], (KV_LORA_RANK,)),
        "kv_w_uk": dense(ks[13], (KV_LORA_RANK, N_HEADS, QK_NOPE_DIM), KV_LORA_RANK),
        "kv_w_uv": dense(ks[14], (KV_LORA_RANK, N_HEADS, V_HEAD_DIM), KV_LORA_RANK),
        "b_w_in": dense(ks[15], (N_B_LAYERS, D_MODEL, Q_LORA_RANK + HV), D_MODEL),
        "b_q_norm_g": gain(ks[16], (N_B_LAYERS, Q_LORA_RANK)),
        "b_w_uq": dense(ks[17], (N_B_LAYERS, Q_LORA_RANK, N_HEADS, QK_NOPE_DIM + QK_ROPE_DIM), Q_LORA_RANK),
        "b_w_out": dense(ks[18], (N_B_LAYERS, HV, D_MODEL), HV, beta),
    }

def reference(x, positions, ln_g, ln_b, a_w_in, a_b_in, a_conv_w, a_conv_b, a_norm_g, a_norm_b,
              a_w_out, a_b_out, kv_w_down, kv_norm_g, kv_w_uk, kv_w_uv, b_w_in, b_q_norm_g,
              b_w_uq, b_w_out):
    alpha = (2.0 * DEPTH) ** 0.25
    cos, sin = rope_tables(positions, x.dtype)
    h = x
    k_nope = k_rope = v = None
    for layer in range(DEPTH):
        if layer < N_A_LAYERS:
            i = layer
            y = conformer_conv_branch(h, a_w_in[i], a_b_in[i], a_conv_w[i], a_conv_b[i],
                                      a_norm_g[i], a_norm_b[i], a_w_out[i], a_b_out[i])
        else:
            if layer == N_A_LAYERS:
                k_nope, k_rope, v = shared_latent_kv(h, kv_w_down, kv_norm_g, kv_w_uk, kv_w_uv, cos, sin)
            j = layer - N_A_LAYERS
            y = mla_branch(h, k_nope, k_rope, v, b_w_in[j], b_q_norm_g[j], b_w_uq[j], b_w_out[j], cos, sin)
        h = layer_norm(alpha * h + y, ln_g[layer], ln_b[layer])
    return h


_drawn_inputs = setup_inputs


def setup_inputs(seed=0):
    import zlib

    import numpy as np

    out = dict(_drawn_inputs(seed))
    spreads = {}
    factors = {'a_b_in': 8.0,
     'a_conv_b': 8.0,
     'a_norm_g': 8.0,
     'a_norm_b': 8.0,
     'a_b_out': 4.085,
     'kv_norm_g': 8.0,
     'b_q_norm_g': 8.0}
    for name, (base, spread) in spreads.items():
        noise = np.random.default_rng([zlib.crc32(name.encode()), seed]).standard_normal(out[name].shape)
        drawn = base * np.exp(spread * noise) if base else spread * noise
        out[name] = __import__('jax').numpy.asarray(drawn.astype(out[name].dtype))
    for name, factor in factors.items():
        out[name] = (out[name] * factor).astype(out[name].dtype)
    return out
```

```python
from contextlib import ExitStack

import numpy as np

import concourse.bass as bass
from concourse import mybir

F32 = mybir.dt.float32
F32R = mybir.dt.float32r
I32 = mybir.dt.int32
ALU = mybir.AluOpType
ACT = mybir.ActivationFunctionType

P = 128
BANK = 512
DEPTH = 2
D_MODEL = 1024
SEQ = 512
CONV_WIDTH = 2 * D_MODEL
TAPS = 31
PAD = TAPS - 1
N_HEADS = 16
NOPE = 128
ROPE = 64
V_DIM = 128
KV_RANK = D_MODEL // 4
Q_RANK = D_MODEL // 2
ALPHA = (2.0 * DEPTH) ** 0.25
LN_EPS = 1e-5
RMS_EPS = 1e-6
MASK_VALUE = -1e30
MAX_START = -3e38
SM_SCALE = float((NOPE + ROPE) ** -0.5)
ROPE_THETA = 10000.0

KD = D_MODEL // P
CT = CONV_WIDTH // P
RT = SEQ // P
KQ = Q_RANK // P
KV = KV_RANK // P
PAIRS = N_HEADS // 2
HALVES = D_MODEL // BANK

ROUND = 4
ROUNDS = CT // ROUND

CHUNK = KD * P
Z0 = 2 * CT
OUT0 = Z0 + CT
LAT0 = OUT0 + CT
LATENTS = KV + 1 + KQ
ROPE_CHUNK = LAT0 + KV
BZ0 = LAT0 + LATENTS
FIN0 = BZ0 + N_HEADS
RAW_SLOTS = 2
SLOTS = 4
RESIDENT = SLOTS

UK, UV, QN, QR = 0, KV * 2 * NOPE, 2 * KV * 2 * NOPE, 2 * KV * 2 * NOPE + KQ * 2 * NOPE
BUNDLE = QR + KQ * 2 * ROPE

V_BIN = 0
V_CONVB = V_BIN + 3 * CT
V_NG = V_CONVB + CT
V_NB = V_NG + CT
V_KVG = V_NB + CT
V_QG = V_KVG + KV
V_ALL = V_QG + KQ

TWO_PI = 2.0 * np.pi
PI_A = 6.28125
PI_B = float(np.float32(np.floor((TWO_PI - PI_A) * 2.0 ** 20) / 2.0 ** 20))
PI_C = float(np.float32(TWO_PI - PI_A - PI_B))
ROUNDER = 1.5 * 2.0 ** 23
PI_SAFE = 3.1415925


def wait(eng, semaphore, value):
    if not isinstance(value, int) or value > 0:
        eng.wait_ge(semaphore, value)


def trunk_kernel(nc, x, positions, ln_g, ln_b, a_w_in, a_b_in, a_conv_w, a_conv_b, a_norm_g,
                 a_norm_b, a_w_out, a_b_out, kv_w_down, kv_norm_g, kv_w_uk, kv_w_uv, b_w_in,
                 b_q_norm_g, b_w_uq, b_w_out, rope_freq, out, only_a=False):
    x_rows = x.rearrange("b (r p) d -> p (b r) d", p=P)
    out_rows = out.rearrange("b (r p) d -> p (b r) d", p=P)
    w_in_a = a_w_in.rearrange("a (k p) n -> p (a k) n", p=P)
    w_out_a = a_w_out.rearrange("a (k p) n -> (a k) p n", p=P)
    w_down = kv_w_down.rearrange("(k p) n -> p k n", p=P)
    w_in_b = b_w_in.rearrange("a (k p) n -> p (a k) n", p=P)
    w_out_b = b_w_out.rearrange("a (k p) n -> (a k) p n", p=P)
    w_uk = kv_w_uk.rearrange("(k p) h d -> p k (h d)", p=P)
    w_uv = kv_w_uv.rearrange("(k p) h d -> p k (h d)", p=P)
    w_uq = b_w_uq.rearrange("a (k p) h d -> p (a k) h d", p=P)

    with ExitStack() as ctx:
        def sem(name):
            return ctx.enter_context(nc.semaphore(name))

        place = [-(-nc.sbuf_base // 32) * 32]

        def region(words):
            at = place[0]
            place[0] = at + -(-words * 4 // 32) * 32
            assert place[0] <= nc.sbuf_usable_end
            return at

        def at(name, base, offset_words, shape, dtype=F32):
            return nc.alloc_sbuf_tensor_at(name, shape, dtype, offset=base + 4 * offset_words)

        def own(name, shape, dtype=F32):
            words = 1
            for n in shape[1:]:
                words *= n
            return at(name, region(words), 0, shape, dtype)

        TILE = SEQ
        reg_x = region(8 * TILE)
        reg_xt = region(16 * TILE)
        reg_u = region(CT * (SEQ + PAD))
        reg_acc = region(CT * TILE)
        reg_z = region(CT * TILE)
        reg_w = region((RAW_SLOTS + 2 * SLOTS) * CHUNK)
        reg_e = region(4 * TILE)

        ident = own("ident", [P, P])
        ones = own("ones", [P, P])
        conv_w = own("conv_w", [P, CT * TAPS])
        conv_w_hi = own("conv_w_hi", [P, CT * TAPS], F32R)
        conv_w_lo = own("conv_w_lo", [P, CT * TAPS], F32R)
        vec = own("vec", [P, V_ALL])
        cos = own("cos", [P, SEQ])
        sin = own("sin", [P, SEQ])
        mask = own("mask", [P, SEQ])
        freq = own("freq", [P, 2])
        bn = own("bn", [P, HALVES, 6])
        mean_var = own("mean_var", [P, 2])
        rstd_row = own("rstd_row", [P, 2])
        minus_half = own("minus_half", [P, 1])
        top = own("top", [P, RT])
        neg_top = own("neg_top", [P, RT])
        denom = own("denom", [P, RT])
        waited = own("waited", [P, RT])
        inv_denom = own("inv_denom", [P, RT])

        w_raw = [at(f"w_raw{i}", reg_w, i * CHUNK, [P, CHUNK]) for i in range(RAW_SLOTS)]
        w_hi = [at(f"w_hi{i}", reg_w, (RAW_SLOTS + i) * CHUNK, [P, CHUNK], F32R) for i in range(SLOTS)]
        w_lo = [at(f"w_lo{i}", reg_w, (RAW_SLOTS + SLOTS + i) * CHUNK, [P, CHUNK], F32R)
                for i in range(SLOTS)]

        x_in = at("x_in", reg_x, 0, [P, RT, D_MODEL])
        val = [at(f"val{i}", reg_x, i * TILE, [P, SEQ]) for i in range(2)]
        sig = [at(f"sig{i}", reg_x, (2 + i) * TILE, [P, SEQ]) for i in range(2)]
        cu_hi = at("cu_hi", reg_x, 4 * TILE, [P, SEQ + PAD], F32R)
        cu_lo = at("cu_lo", reg_x, 4 * TILE + 544, [P, SEQ + PAD], F32R)
        sq = [at(f"sq{i}", reg_x, i * TILE, [P, SEQ]) for i in range(2)]
        var_a = at("var_a", reg_x, 2 * TILE, [P, SEQ])
        std_a = at("std_a", reg_x, 3 * TILE, [P, SEQ])
        rstd_a = at("rstd_a", reg_x, 4 * TILE, [P, SEQ])
        newton_a = at("newton_a", reg_x, 6 * TILE, [P, SEQ])
        xt_hi = at("xt_hi", reg_xt, 0, [P, KD, SEQ], F32R)
        xt_lo = at("xt_lo", reg_xt, KD * SEQ, [P, KD, SEQ], F32R)
        u = at("u", reg_u, 0, [P, CT, SEQ + PAD])
        taps_raw = at("taps_raw", reg_acc, 0, [TAPS, CONV_WIDTH])
        vec_raw = at("vec_raw", reg_acc, 4 * TILE, [V_ALL, P])
        pos_int = at("pos_int", reg_acc, 5 * TILE, [P, SEQ], I32)
        pos = at("pos", reg_acc, 6 * TILE, [P, SEQ])
        angle = at("angle", reg_acc, 7 * TILE, [P, SEQ])
        turns = at("turns", reg_acc, 8 * TILE, [P, SEQ])
        angle_c = at("angle_c", reg_acc, 9 * TILE, [P, SEQ])
        acc = at("acc", reg_acc, 0, [P, CT, SEQ])
        diag_hi = at("diag_hi", reg_z, 0, [P, TAPS, P], F32R)
        diag_lo = at("diag_lo", reg_z, TAPS * P, [P, TAPS, P], F32R)
        z_a = at("z_a", reg_z, 0, [P, CT, SEQ])
        g_hi = at("g_hi", reg_u, 0, [P, CT, SEQ], F32R)
        g_lo = at("g_lo", reg_z, 0, [P, CT, SEQ], F32R)
        csum = at("csum", reg_e, 0, [P, SEQ])
        vsum = at("vsum", reg_e, TILE, [P, SEQ])

        res = at("res", reg_xt, 0, [P, RT, D_MODEL])
        ln_rows = at("ln_rows", reg_xt, 8 * TILE, [P, 3, D_MODEL])
        ln_rows_b = at("ln_rows_b", reg_x, 0, [P, 2, D_MODEL])

        ht_hi = at("ht_hi", reg_acc, 0, [P, KD, SEQ], F32R)
        ht_lo = at("ht_lo", reg_acc, KD * SEQ, [P, KD, SEQ], F32R)
        lat = at("lat", reg_x, 0, [P, LATENTS, SEQ])
        k_swap = at("k_swap", reg_x, LATENTS * TILE, [P, SEQ])
        b_sq = at("b_sq", reg_xt, 8 * TILE, [P, SEQ])
        b_sum = at("b_sum", reg_xt, 9 * TILE, [P, 2, SEQ])
        b_var = at("b_var", reg_xt, 11 * TILE, [P, 2, SEQ])
        b_std = at("b_std", reg_xt, 13 * TILE, [P, 2, SEQ])
        b_newton = at("b_newton", reg_xt, 15 * TILE, [P, SEQ])
        b_rstd = at("b_rstd", reg_e, 0, [P, 2, SEQ])
        cq_hi = at("cq_hi", reg_u, 0, [P, KQ, SEQ], F32R)
        cq_lo = at("cq_lo", reg_u, 4 * TILE, [P, KQ, SEQ], F32R)
        ckv_hi = at("ckv_hi", reg_u, 8 * TILE, [P, KV, SEQ], F32R)
        ckv_lo = at("ckv_lo", reg_u, 10 * TILE, [P, KV, SEQ], F32R)
        kr_hi = at("kr_hi", reg_u, 12 * TILE, [P, SEQ], F32R)
        kr_lo = at("kr_lo", reg_u, 13 * TILE, [P, SEQ], F32R)
        qr_raw = at("qr_raw", reg_u, 14 * TILE, [P, SEQ])
        qr_swap = at("qr_swap", reg_u, 15 * TILE, [P, SEQ])
        gate = at("gate", reg_z, 0, [P, N_HEADS, SEQ])
        k_hi = [at(f"k_hi{i}", reg_acc, (0 + i) * TILE, [P, SEQ], F32R) for i in range(2)]
        k_lo = [at(f"k_lo{i}", reg_acc, (2 + i) * TILE, [P, SEQ], F32R) for i in range(2)]
        q_hi = [at(f"q_hi{i}", reg_acc, (4 + i) * TILE, [P, SEQ], F32R) for i in range(2)]
        q_lo = [at(f"q_lo{i}", reg_acc, (6 + i) * TILE, [P, SEQ], F32R) for i in range(2)]
        v_hi = [at(f"v_hi{i}", reg_acc, (8 + 2 * i) * TILE, [P, RT, 2 * V_DIM], F32R) for i in range(2)]
        v_lo = [at(f"v_lo{i}", reg_acc, (12 + 2 * i) * TILE, [P, RT, 2 * V_DIM], F32R) for i in range(2)]
        qr_hi = [at(f"qr_hi{i}", reg_e, i * TILE, [P, SEQ], F32R) for i in range(2)]
        qr_lo = [at(f"qr_lo{i}", reg_e, (2 + i) * TILE, [P, SEQ], F32R) for i in range(2)]
        bundle_raw = at("bundle_raw", reg_xt, 8 * TILE, [P, BUNDLE])
        bundle_hi = [at(f"bundle_hi{i}", reg_w, i * BUNDLE, [P, BUNDLE], F32R) for i in range(2)]
        bundle_lo = [at(f"bundle_lo{i}", reg_w, (2 + i) * BUNDLE, [P, BUNDLE], F32R) for i in range(2)]
        prob_at = [0, 1, 3, 6]
        prob = at("prob", reg_xt, 8 * TILE + BUNDLE, [P, 10 * P])
        pt_hi = at("pt_hi", reg_x, 0, [P, RT, SEQ], F32R)
        pt_lo = at("pt_lo", reg_x, 4 * TILE, [P, RT, SEQ], F32R)
        fg_hi = [at(f"fg_hi{i}", reg_u, i * TILE, [P, SEQ], F32R) for i in range(4)]
        fg_lo = [at(f"fg_lo{i}", reg_u, (4 + i) * TILE, [P, SEQ], F32R) for i in range(4)]

        bank = [ctx.enter_context(nc.psum_tensor(f"bank{i}", [P, BANK], F32)) for i in range(8)]

        x_landed = [sem(f"x_landed{r}") for r in range(RT)]
        small_landed = sem("small_landed")
        w_landed = [sem(f"w_landed{i}") for i in range(RAW_SLOTS)]
        w_hi_ready, w_lo_ready, w_used = sem("w_hi_ready"), sem("w_lo_ready"), sem("w_used")
        consts_ready = sem("consts_ready")
        vec_turned, taps_turned, vec_ready = sem("vec_turned"), sem("taps_turned"), sem("vec_ready")
        taps_hi_ready, taps_lo_ready, taps_ready = sem("taps_hi_ready"), sem("taps_lo_ready"), sem("taps_ready")
        x_turned, xt_hi_ready, xt_lo_ready = sem("x_turned"), sem("xt_hi_ready"), sem("xt_lo_ready")
        table_step, angles_ready, rope_ready = sem("table_step"), sem("angles_ready"), sem("rope_ready")
        evacuated = sem("evacuated")
        u_ready, pad_ready = sem("u_ready"), sem("pad_ready")
        diag_hi_ready, diag_lo_ready = sem("diag_hi_ready"), sem("diag_lo_ready")
        cu_hi_ready, cu_lo_ready = sem("cu_hi_ready"), sem("cu_lo_ready")
        pe_conv_done, pe_conv_kept = sem("pe_conv_done"), sem("pe_conv_kept")
        tap_done, csum_done, sums_cleared = sem("tap_done"), sem("csum_done"), sem("sums_cleared")
        mean_done, centered, squared, vsum_done, var_done = (
            sem("mean_done"), sem("centered"), sem("squared"), sem("vsum_done"), sem("var_done"))
        var_ready, std_ready, stat_step, rstd_ready = (
            sem("var_ready"), sem("std_ready"), sem("stat_step"), sem("rstd_ready"))
        scaled, silu_done, gated, g_hi_ready, g_lo_ready = (
            sem("scaled"), sem("silu_done"), sem("gated"), sem("g_hi_ready"), sem("g_lo_ready"))
        res_landed, res_scaled, res_ready = sem("res_landed"), sem("res_scaled"), sem("res_ready")
        y_done, y_step, var_row_ready, rstd_row_ready, rstd_step, row_scaled, row_ready = (
            sem("y_done"), sem("y_step"), sem("var_row_ready"), sem("rstd_row_ready"),
            sem("rstd_step"), sem("row_scaled"), sem("row_ready"))
        h_turned, ht_hi_ready, ht_lo_ready = sem("h_turned"), sem("ht_hi_ready"), sem("ht_lo_ready")
        b_step, b_sum_done, b_var_ready, b_std_ready, b_rstd_ready = (
            sem("b_step"), sem("b_sum_done"), sem("b_var_ready"),
            sem("b_std_ready"), sem("b_rstd_ready"))
        lat_scaled, lat_hi_ready, lat_lo_ready = sem("lat_scaled"), sem("lat_hi_ready"), sem("lat_lo_ready")
        k_swapped = sem("k_swapped")
        bundle_landed, bundle_hi_ready, bundle_lo_ready = (
            sem("bundle_landed"), sem("bundle_hi_ready"), sem("bundle_lo_ready"))
        proj_done, proj_hi_ready, proj_lo_ready = sem("proj_done"), sem("proj_hi_ready"), sem("proj_lo_ready")
        q_swapped, rope_step, qr_rotated, qr_hi_ready, qr_lo_ready = (
            sem("q_swapped"), sem("rope_step"), sem("qr_rotated"), sem("qr_hi_ready"), sem("qr_lo_ready"))
        scores_done, masked, neg_top_ready, exp_done, inv_ready, prob_ready = (
            sem("scores_done"), sem("masked"), sem("neg_top_ready"), sem("exp_done"),
            sem("inv_ready"), sem("prob_ready"))
        prob_turned, pt_hi_ready, pt_lo_ready, pv_done, gate_ready = (
            sem("prob_turned"), sem("pt_hi_ready"), sem("pt_lo_ready"), sem("pv_done"), sem("gate_ready"))
        ln_rows_landed = sem("ln_rows_landed")
        stored = sem("stored")

        SMALL_DMAS = 9
        PROJ_BANK = (5, 6, 7, 5, 6, 7, 5)
        SQUARE_STEPS = (2 * KV - 1, 2 * KV - 1 + 2 * KQ - 1)

        def landed_value(c):
            extra = 16 if isinstance(c, int) and c >= ROPE_CHUNK and (c - ROPE_CHUNK) % RAW_SLOTS == 0 else 0
            return 16 * (c // RAW_SLOTS + 1) + extra

        def heads_loop(eng, step):
            with eng.Fori(0, ROUNDS - 1) as g:
                for s in range(1, ROUND + 1):
                    step(g, s)
            for s in range(1, ROUND):
                step(ROUNDS - 1, s)

        block = ctx.enter_context(nc.Block())

        @block.sync
        def _(sp):
            for r in range(RT):
                sp.dma_start(x_in[:, r, :], x_rows[:, r, :]).then_inc(x_landed[r], 16)
                if r == 0:
                    sp.dma_start(taps_raw[:], a_conv_w[0]).then_inc(small_landed, 16)
                    for row, vector, n in ((V_BIN, a_b_in, 3 * CT), (V_CONVB, a_conv_b, CT),
                                           (V_NG, a_norm_g, CT), (V_NB, a_norm_b, CT),
                                           (V_QG, b_q_norm_g, KQ)):
                        sp.dma_start(vec_raw[row:row + n, :], vector.rearrange("a (n p) -> (a n) p", p=P)
                                     ).then_inc(small_landed, 16)
                    sp.dma_start(vec_raw[V_KVG:V_KVG + KV, :], kv_norm_g.rearrange("(n p) -> n p", p=P)
                                 ).then_inc(small_landed, 16)
                    sp.dma_start(freq[:], rope_freq).then_inc(small_landed, 16)
                    sp.dma_start(pos_int[:], positions.broadcast_to([P, SEQ])).then_inc(small_landed, 16)

            def raw_free(c):
                wait(sp, w_hi_ready, c - RAW_SLOTS + 1)
                wait(sp, w_lo_ready, c - RAW_SLOTS + 1)

            def load_columns(c, slot, source, column, n=P):
                sp.dma_start(w_raw[slot][:].rearrange("p (k m) -> p k m", m=P),
                             source[:, :, bass.ds(column, P)]).then_inc(w_landed[slot], 16)

            def load_value_gate(j):
                for s in range(ROUND):
                    for w in range(2):
                        raw_free(2 * ROUND * j + 2 * s + w)
                        load_columns(None, w, w_in_a, w * CONV_WIDTH + (ROUND * j + s) * P)

            load_value_gate(0)
            with sp.Fori(1, ROUNDS) as j:
                load_value_gate(j)
            with sp.Fori(0, ROUNDS) as j:
                for s in range(ROUND):
                    raw_free(Z0 + ROUND * j + s)
                    load_columns(None, s % 2, w_in_a, 2 * CONV_WIDTH + (ROUND * j + s) * P)

            sp.wait_ge(w_used, OUT0)
            sp.dma_start(res[:], x_rows).then_inc(res_landed, 16)
            sp.dma_start(ln_rows[:, 0, :], ln_g[0:1, :].broadcast_to([P, D_MODEL])).then_inc(res_landed, 16)
            sp.dma_start(ln_rows[:, 1, :], ln_b[0:1, :].broadcast_to([P, D_MODEL])).then_inc(res_landed, 16)
            sp.dma_start(ln_rows[:, 2, :], a_b_out.broadcast_to([P, D_MODEL])).then_inc(res_landed, 16)
            for k in range(CT):
                raw_free(OUT0 + k)
                sp.dma_start(w_raw[k % 2][:], w_out_a[k]).then_inc(w_landed[k % 2], 16)
            if only_a:
                for r in range(RT):
                    sp.wait_ge(row_ready, r + 1)
                    sp.dma_start(out_rows[:, r, :], res[:, r, :]).then_inc(stored, 16)
                sp.wait_ge(stored, 16 * RT)
                return

            for n in range(LATENTS):
                c = LAT0 + n
                raw_free(c)
                if n < KV:
                    load_columns(c, c % 2, w_down, n * P)
                elif n == KV:
                    halves = w_raw[c % 2][:].rearrange("p (k b m) -> p b k m", b=2, m=ROPE)
                    for b in range(2):
                        sp.dma_start(halves[:, b], w_down[:, :, KV_RANK:KV_RANK + ROPE]
                                     ).then_inc(w_landed[c % 2], 16)
                else:
                    load_columns(c, c % 2, w_in_b, (n - KV - 1) * P)
            for i in range(ROUND):
                raw_free(BZ0 + i)
                load_columns(None, (BZ0 + i) % 2, w_in_b, Q_RANK + i * P)
            sp.wait_ge(evacuated, OUT0 + KV + 1)
            for b in range(4):
                sp.dma_start(k_swap[32 * b:32 * b + 32, :], lat[32 * (b ^ 1):32 * (b ^ 1) + 32, KV, :]
                             ).then_inc(k_swapped, 16)
            with sp.Fori(1, ROUNDS) as j:
                for s in range(ROUND):
                    raw_free(BZ0 + ROUND * j + s)
                    load_columns(None, (BZ0 + s) % 2, w_in_b, Q_RANK + (ROUND * j + s) * P)

            def load_bundle(p):
                wait(sp, bundle_hi_ready, 2 * p)
                wait(sp, bundle_lo_ready, 2 * p)
                for off, source in ((UK, w_uk), (UV, w_uv)):
                    sp.dma_start(bundle_raw[:, off:off + KV * 2 * NOPE].rearrange("p (k m) -> p k m", k=KV),
                                 source[:, :, bass.ds(p * 2 * NOPE, 2 * NOPE)]).then_inc(bundle_landed, 16)
                for e in range(2):
                    qn = bundle_raw[:, QN:QR].rearrange("p (k e m) -> p e k m", k=KQ, e=2)
                    qr = bundle_raw[:, QR:BUNDLE].rearrange("p (k e m) -> p e k m", k=KQ, e=2)
                    sp.dma_start(qn[:, e], w_uq[:, :, bass.ds(2 * p + e, 1), 0:NOPE].rearrange("p k o m -> p k (o m)")
                                 ).then_inc(bundle_landed, 16)
                    sp.dma_start(qr[:, e], w_uq[:, :, bass.ds(2 * p + e, 1), NOPE:NOPE + ROPE].rearrange("p k o m -> p k (o m)")
                                 ).then_inc(bundle_landed, 16)

            def swap_rotary(p):
                sp.wait_ge(proj_hi_ready, 7 * p + 3)
                for b in range(4):
                    sp.dma_start(qr_swap[32 * b:32 * b + 32, :], qr_raw[32 * (b ^ 1):32 * (b ^ 1) + 32, :]
                                 ).then_inc(q_swapped, 16)

            sp.wait_ge(lat_scaled, LATENTS)
            load_bundle(0)
            swap_rotary(0)
            load_bundle(1)
            with sp.Fori(1, PAIRS - 1) as p:
                swap_rotary(p)
                load_bundle(p + 1)
            swap_rotary(PAIRS - 1)

            sp.wait_ge(proj_done, 7 * PAIRS)
            for k in range(CT):
                c = FIN0 + k
                raw_free(c)
                sp.dma_start(w_raw[c % 2][:], w_out_b[k]).then_inc(w_landed[c % 2], 16)
                if k == 1:
                    sp.wait_ge(pv_done, N_HEADS)
                    sp.dma_start(ln_rows_b[:, 0, :], ln_g[1:2, :].broadcast_to([P, D_MODEL])
                                 ).then_inc(ln_rows_landed, 16)
                    sp.dma_start(ln_rows_b[:, 1, :], ln_b[1:2, :].broadcast_to([P, D_MODEL])
                                 ).then_inc(ln_rows_landed, 16)
            for r in range(RT):
                sp.wait_ge(row_ready, RT + r + 1)
                sp.dma_start(out_rows[:, r, :], res[:, r, :]).then_inc(stored, 16)
            sp.wait_ge(stored, 16 * RT)

        @block.gpsimd
        def _(pool):
            nc.gpsimd.memset(ident[:], 0.0).then_inc(consts_ready, 1)
            nc.gpsimd.memset(mask[:], 0.0).then_inc(consts_ready, 1)
            nc.gpsimd.memset(ones[:], 1.0).then_inc(consts_ready, 1)
            nc.gpsimd.memset(minus_half[:], -0.5).then_inc(consts_ready, 1)
            pool.wait_ge(consts_ready, 4)
            nc.gpsimd.affine_select(out=ident[:], in_=ident[:], compare_op=ALU.not_equal, fill=1.0, base=0,
                                    pattern=[[-1, P]], channel_multiplier=1).then_inc(consts_ready, 1)
            nc.gpsimd.affine_select(out=mask[:], in_=mask[:], compare_op=ALU.is_ge, fill=MASK_VALUE,
                                    base=SEQ - P, pattern=[[-1, SEQ]], channel_multiplier=1
                                    ).then_inc(consts_ready, 1)
            nc.gpsimd.memset(u[:, :, 0:PAD], 0.0).then_inc(pad_ready, 1)

            def split_lo(c, raw, slot):
                pool.wait_ge(w_hi_ready, c + 1)
                wait(pool, w_used, c - SLOTS + 1)
                nc.gpsimd.tensor_tensor(w_lo[slot][:], w_raw[raw][:], w_hi[slot][:].bitcast(F32),
                                        ALU.subtract).then_inc(w_lo_ready, 1)

            def glu(t, slot):
                pool.wait_ge(evacuated, 2 * t + 2)
                nc.gpsimd.tensor_tensor(u[:, bass.ds(t, 1), PAD:].rearrange("p o n -> p (o n)"), val[slot][:], sig[slot][:],
                                        ALU.mult).then_inc(u_ready, 1)

            def value_gate(j):
                for s in range(ROUND):
                    t = ROUND * j + s
                    for w in range(2):
                        split_lo(2 * t + w, w, (2 * s + w) % SLOTS)
                    if not isinstance(t, int) or t > 0:
                        glu(t - 1, (s - 1) % 2)
                    if s < 2:
                        wait(pool, pe_conv_done, j)
                        if s == 0:
                            pool.wait_ge(taps_hi_ready, 1)
                        lo, hi = (0, TAPS // 2) if s == 0 else (TAPS // 2, TAPS)
                        n = hi - lo
                        taps = conv_w_hi[:, bass.ds(j * (ROUND * TAPS) + lo, n)].bitcast(F32)
                        nc.gpsimd.tensor_tensor(diag_hi[:, lo:hi, :],
                                                ident[:].unsqueeze(1).broadcast_to([P, n, P]),
                                                taps.unsqueeze(2).broadcast_to([P, n, P]),
                                                ALU.mult).then_inc(diag_hi_ready, 1)
                    if s == 2:
                        pool.wait_ge(cu_hi_ready, j + 1)
                        nc.gpsimd.tensor_tensor(cu_lo[:], u[:, bass.ds(ROUND * j, 1), :].rearrange("p o n -> p (o n)"),
                                                cu_hi[:].bitcast(F32), ALU.subtract).then_inc(cu_lo_ready, 1)

            pool.wait_ge(x_turned, 2 * RT)
            value_gate(0)
            with pool.Fori(1, ROUNDS) as j:
                value_gate(j)
            split_lo(Z0, 0, 0)
            glu(CT - 1, (CT - 1) % 2)
            for c in range(Z0 + 1, OUT0):
                split_lo(c, c % 2, c % SLOTS)

            def rstd_of_row(n):
                pool.wait_ge(var_row_ready, n + 1)
                nc.gpsimd.tensor_scalar(rstd_row[:, 0:1], mean_var[:, 1:2], LN_EPS, None, ALU.add
                                        ).then_inc(rstd_step, 1)
                pool.wait_ge(rstd_step, n + 1)
                nc.gpsimd.tensor_tensor(rstd_row[:, 1:2], rstd_row[:, 0:1], minus_half[:], ALU.pow
                                        ).then_inc(rstd_row_ready, 1)

            def add_ln_bias(n, r, rows):
                pool.wait_ge(row_scaled, n + 1)
                nc.gpsimd.tensor_tensor(res[:, r, :], res[:, r, :], rows[:, 1, :], ALU.add
                                        ).then_inc(row_ready, 1)

            for k in range(CT):
                c = OUT0 + k
                split_lo(c, c % 2, c % SLOTS)
                if 4 <= k < 4 + RT:
                    r = k - 4
                    pool.wait_ge(res_scaled, r + 1)
                    nc.gpsimd.tensor_tensor(res[:, r, :], res[:, r, :], ln_rows[:, 2, :], ALU.add
                                            ).then_inc(res_ready, 1)
            for r in range(RT):
                rstd_of_row(r)
                if r > 0:
                    add_ln_bias(r - 1, r - 1, ln_rows)
            if not only_a:
                split_lo(LAT0, LAT0 % 2, LAT0 % SLOTS)
                split_lo(LAT0 + 1, (LAT0 + 1) % 2, (LAT0 + 1) % SLOTS)
            add_ln_bias(RT - 1, RT - 1, ln_rows)
            if only_a:
                return
            for c in range(LAT0 + 2, BZ0 + N_HEADS):
                split_lo(c, c % 2, c % SLOTS)

            def split_bundle_lo(p, slot):
                for part, (lo, hi) in enumerate(((0, QN), (QN, BUNDLE))):
                    pool.wait_ge(bundle_hi_ready, 2 * p + part + 1)
                    nc.gpsimd.tensor_tensor(bundle_lo[slot][:, lo:hi], bundle_raw[:, lo:hi],
                                            bundle_hi[slot][:, lo:hi].bitcast(F32), ALU.subtract
                                            ).then_inc(bundle_lo_ready, 1)

            def rotate(p, slot):
                pool.wait_ge(q_swapped, 64 * (p + 1))
                nc.gpsimd.tensor_tensor(qr_raw[:], qr_raw[:], cos[:], ALU.mult).then_inc(rope_step, 1)
                nc.gpsimd.tensor_tensor(qr_swap[:], qr_swap[:], sin[:], ALU.mult).then_inc(rope_step, 1)
                pool.wait_ge(rope_step, 2 * p + 2)
                nc.gpsimd.tensor_tensor(qr_raw[:], qr_raw[:], qr_swap[:], ALU.add).then_inc(qr_rotated, 1)
                pool.wait_ge(qr_hi_ready, p + 1)
                nc.gpsimd.tensor_tensor(qr_lo[slot][:], qr_raw[:], qr_hi[slot][:].bitcast(F32), ALU.subtract
                                        ).then_inc(qr_lo_ready, 1)

            split_bundle_lo(0, 0)
            rotate(0, 0)
            split_bundle_lo(1, 1)
            with pool.Fori(0, PAIRS // 2 - 1) as i:
                for e in range(2):
                    rotate(2 * i + e + 1, (e + 1) % 2)
                    split_bundle_lo(2 * i + e + 2, e)
            rotate(PAIRS - 1, (PAIRS - 1) % 2)

            pool.wait_ge(proj_done, 7 * PAIRS)
            for k in range(CT):
                c = FIN0 + k
                split_lo(c, c % 2, c % SLOTS)
            for r in range(RT):
                rstd_of_row(RT + r)
                if r > 0:
                    add_ln_bias(RT + r - 1, r - 1, ln_rows_b)
            add_ln_bias(2 * RT - 1, RT - 1, ln_rows_b)

        @block.scalar
        def _(act):
            for q in range(2 * RT):
                r, half = q // 2, q % 2
                act.wait_ge(x_turned, q + 1)
                nc.scalar.activation(xt_hi[:, 4 * half:4 * half + 4, r * P:(r + 1) * P],
                                     bank[q % 4][:].rearrange("p (k n) -> p k n", k=4), ACT.Copy
                                     ).then_inc(xt_hi_ready, 1)
                if q == 1:
                    act.wait_ge(taps_turned, 1)
                    nc.scalar.activation(conv_w_hi[:], bank[4][:, 0:CT * TAPS], ACT.Copy
                                         ).then_inc(taps_hi_ready, 1)
                    act.wait_ge(vec_turned, 1)
                    nc.scalar.activation(vec[:], bank[5][:, 0:V_ALL], ACT.Copy).then_inc(vec_ready, 1)

            def split_hi(c, raw, slot, landed):
                act.wait_ge(w_landed[raw], landed)
                wait(act, w_used, c - SLOTS + 1)
                nc.scalar.activation(w_hi[slot][:], w_raw[raw][:], ACT.Copy).then_inc(w_hi_ready, 1)

            def keep_value_gate(t, s):
                wait(act, u_ready, t - 1)
                act.wait_ge(w_used, 2 * t + 1)
                nc.scalar.activation(val[s % 2][:], bank[2 * s % 4][:], ACT.Identity,
                                     bias=vec[:, bass.ds(V_BIN + t, 1)]).then_inc(evacuated, 1)
                act.wait_ge(w_used, 2 * t + 2)
                nc.scalar.activation(sig[s % 2][:], bank[(2 * s + 1) % 4][:], ACT.Sigmoid,
                                     bias=vec[:, bass.ds(V_BIN + CT + t, 1)]).then_inc(evacuated, 1)

            def value_gate(j):
                for s in range(ROUND):
                    t = ROUND * j + s
                    for w in range(2):
                        split_hi(2 * t + w, w, (2 * s + w) % SLOTS, 16 * (t + 1))
                    if not isinstance(t, int) or t > 0:
                        keep_value_gate(t - 1, s - 1)
                    if s < 2:
                        if s == 0:
                            act.wait_ge(taps_lo_ready, 1)
                            wait(act, pe_conv_done, j)
                        lo, hi = (0, TAPS // 2) if s == 0 else (TAPS // 2, TAPS)
                        for k in range(lo, hi):
                            nc.scalar.activation(
                                diag_lo[:, k, :], ident[:], ACT.Copy,
                                scale=conv_w_lo[:, bass.ds(j * (ROUND * TAPS) + k, 1)].bitcast(F32)
                            ).then_inc(diag_lo_ready, 1)
                    if s == 2:
                        act.wait_ge(u_ready, ROUND * j + 1)
                        if isinstance(j, int):
                            act.wait_ge(pad_ready, 1)
                        nc.scalar.activation(cu_hi[:], u[:, bass.ds(ROUND * j, 1), :].rearrange("p o n -> p (o n)"),
                                             ACT.Copy).then_inc(cu_hi_ready, 1)
                    if s == 3:
                        act.wait_ge(pe_conv_done, j + 1)
                        if isinstance(j, int):
                            act.wait_ge(rope_ready, 2)
                        nc.scalar.activation(acc[:, bass.ds(ROUND * j, 1), :].rearrange("p o n -> p (o n)"), bank[6][:],
                                             ACT.Identity, bias=vec[:, bass.ds(V_CONVB + ROUND * j, 1)]
                                             ).then_inc(pe_conv_kept, 1)

            act.wait_ge(angles_ready, 1)
            nc.scalar.activation(sin[:], angle[:], ACT.Sin).then_inc(rope_ready, 1)
            nc.scalar.activation(cos[:], angle_c[:], ACT.Sin).then_inc(rope_ready, 1)

            act.wait_ge(x_turned, 2 * RT)
            value_gate(0)
            with act.Fori(1, ROUNDS) as j:
                value_gate(j)

            def keep_z(i):
                act.wait_ge(w_used, Z0 + i + 1)
                if i == 0:
                    act.wait_ge(pe_conv_done, ROUNDS)
                nc.scalar.activation(z_a[:, i, :], bank[i % 4][:], ACT.Silu,
                                     bias=vec[:, V_BIN + 2 * CT + i:V_BIN + 2 * CT + i + 1]
                                     ).then_inc(evacuated, 1)

            def z_split(i):
                c = Z0 + i
                split_hi(c, c % 2, c % SLOTS, landed_value(c))

            def square(t):
                act.wait_ge(centered, t + 1)
                wait(act, vsum_done, t - 1)
                nc.scalar.activation(sq[t % 2][:], acc[:, t, :], ACT.Square).then_inc(squared, 1)

            def branch_silu(t):
                act.wait_ge(scaled, t + 1)
                nc.scalar.activation(acc[:, t, :], acc[:, t, :], ACT.Silu,
                                     bias=vec[:, V_NB + t:V_NB + t + 1], scale=vec[:, V_NG + t:V_NG + t + 1]
                                     ).then_inc(silu_done, 1)

            for i in range(CT):
                z_split(i)
                if i == 0:
                    keep_value_gate(CT - 1, CT - 1)
                if i >= 3:
                    keep_z(i - 3)
                if i in (10, 11):
                    for t in range(8 * (i - 10), 8 * (i - 10) + 8):
                        square(t)
                if i == 14:
                    act.wait_ge(var_ready, 1)
                    nc.scalar.activation(std_a[:], var_a[:], ACT.Sqrt).then_inc(std_ready, 1)
                if i == 15:
                    for t in range(4):
                        branch_silu(t)
            def branch_hi(k):
                act.wait_ge(gated, k + 1)
                nc.scalar.activation(g_hi[:, k, :], acc[:, k, :], ACT.Copy).then_inc(g_hi_ready, 1)

            for i in range(CT - 3, CT):
                keep_z(i)
                for t in range(4 * (i - CT + 4), 4 * (i - CT + 4) + 4):
                    branch_silu(t)
                if i < CT - 1:
                    for k in range(4 * (i - CT + 3), 4 * (i - CT + 3) + 4):
                        branch_hi(k)
            for k in range(CT):
                c = OUT0 + k
                split_hi(c, c % 2, c % SLOTS, landed_value(c))
                if k < CT - 8:
                    branch_hi(8 + k)
                if 3 <= k < 3 + RT:
                    r = k - 3
                    act.wait_ge(res_landed, 64)
                    nc.scalar.activation(res[:, r, :], res[:, r, :], ACT.Copy, scale=ALPHA
                                         ).then_inc(res_scaled, 1)
            if only_a:
                return

            act.wait_ge(g_lo_ready, CT)
            for q in range(2 * RT):
                r, half = q // 2, q % 2
                act.wait_ge(h_turned, q + 1)
                nc.scalar.activation(ht_hi[:, 4 * half:4 * half + 4, r * P:(r + 1) * P],
                                     bank[q][:].rearrange("p (k n) -> p k n", k=4), ACT.Copy
                                     ).then_inc(ht_hi_ready, 1)
                if q in (4, 5):
                    c = LAT0 + q - 4
                    split_hi(c, c % 2, c % SLOTS, landed_value(c))

            def keep_latent(n):
                act.wait_ge(w_used, LAT0 + n + 1)
                nc.scalar.activation(lat[:, n, :], bank[n % 4][:], ACT.Copy).then_inc(evacuated, 1)

            def keep_gate(i):
                act.wait_ge(w_used, BZ0 + i + 1)
                nc.scalar.activation(gate[:, i, :], bank[(LATENTS + i) % 4][:], ACT.Silu).then_inc(evacuated, 1)

            def latent_hi(m, out_ap, in_ap):
                act.wait_ge(lat_scaled, m + 1)
                nc.scalar.activation(out_ap, in_ap, ACT.Copy).then_inc(lat_hi_ready, 1)

            for n in range(2, LATENTS + N_HEADS):
                c = LAT0 + n
                if n >= SLOTS:
                    m = n - SLOTS
                    if m < LATENTS:
                        keep_latent(m)
                    else:
                        keep_gate(m - LATENTS)
                split_hi(c, c % 2, c % SLOTS, landed_value(c))
                if n == LATENTS + 7:
                    act.wait_ge(b_var_ready, 2)
                    nc.scalar.activation(b_std[:], b_var[:], ACT.Sqrt).then_inc(b_std_ready, 1)
                if n == LATENTS + 10:
                    for k in range(KV):
                        latent_hi(k, ckv_hi[:, k, :], lat[:, k, :])
                    latent_hi(KV, kr_hi[:], lat[:, KV, :])
                if n == LATENTS + 11:
                    for k in range(KQ):
                        latent_hi(KV + 1 + k, cq_hi[:, k, :], lat[:, KV + 1 + k, :])
            for i in range(N_HEADS - 4, N_HEADS):
                keep_gate(i)

            def split_bundle_hi(p, slot):
                act.wait_ge(bundle_landed, 96 * (p + 1))
                wait(act, proj_done, 7 * (p - 1))
                for lo, hi in ((0, QN), (QN, BUNDLE)):
                    nc.scalar.activation(bundle_hi[slot][:, lo:hi], bundle_raw[:, lo:hi], ACT.Copy
                                         ).then_inc(bundle_hi_ready, 1)

            def keep_projection(p, e, slot):
                if e == 0:
                    for half in range(2):
                        act.wait_ge(proj_done, 7 * p + half + 1)
                        nc.scalar.activation(v_hi[slot][:, 2 * half:2 * half + 2, :],
                                             bank[5 + half][:].rearrange("p (t n) -> p t n", t=2), ACT.Copy
                                             ).then_inc(proj_hi_ready, 1)
                    act.wait_ge(proj_done, 7 * p + 3)
                    wait(act, qr_lo_ready, p)
                    nc.scalar.activation(qr_raw[:], bank[7][:], ACT.Copy).then_inc(proj_hi_ready, 1)
                for n, tile in ((0, k_hi), (1, q_hi)):
                    act.wait_ge(proj_done, 7 * p + 3 + 2 * e + n + 1)
                    nc.scalar.activation(tile[e][:], bank[PROJ_BANK[3 + 2 * e + n]][:], ACT.Copy
                                         ).then_inc(proj_hi_ready, 1)

            def rotary_hi(p, slot):
                act.wait_ge(qr_rotated, p + 1)
                nc.scalar.activation(qr_hi[slot][:], qr_raw[:], ACT.Copy).then_inc(qr_hi_ready, 1)

            def exps(h):
                act.wait_ge(neg_top_ready, h + 1)
                for b in range(RT):
                    n = (b + 1) * P
                    block_ = prob[:, prob_at[b] * P:prob_at[b] * P + n]
                    nc.scalar.activation(block_, block_, ACT.Exp, bias=neg_top[:, b:b + 1], scale=SM_SCALE,
                                         accum_out=denom[:, b:b + 1]).then_inc(exp_done, 1)

            def transposed_hi(h):
                for b in range(RT):
                    act.wait_ge(prob_turned, RT * h + b + 1)
                    nc.scalar.activation(pt_hi[:, 0:b + 1, b * P:(b + 1) * P],
                                         bank[2 + b % 2][:, 0:(b + 1) * P].rearrange("p (k n) -> p k n", k=b + 1),
                                         ACT.Copy).then_inc(pt_hi_ready, 1)

            act.wait_ge(w_used, FIN0)
            split_bundle_hi(0, 0)
            keep_projection(0, 0, 0)
            rotary_hi(0, 0)
            split_bundle_hi(1, 1)
            exps(0)
            keep_projection(0, 1, 0)
            transposed_hi(0)

            def head(g, s):
                h = ROUND * g + s
                exps(h)
                last = isinstance(h, int) and h == N_HEADS - 1
                if not last:
                    p = 2 * g + (s + 1) // 2
                    slot = ((s + 1) // 2) % 2
                    keep_projection(p, (s + 1) % 2, slot)
                    if s % 2 == 1:
                        rotary_hi(p, slot)
                        if not (isinstance(p, int) and p == PAIRS - 1):
                            split_bundle_hi(p + 1, 1 - slot)
                transposed_hi(h)

            heads_loop(act, head)

            act.wait_ge(proj_done, 7 * PAIRS)
            for k in range(CT):
                c = FIN0 + k
                split_hi(c, c % 2, c % SLOTS, landed_value(c))
                act.wait_ge(gate_ready, k + 1)
                wait(act, w_used, c - SLOTS + 1)
                nc.scalar.activation(fg_hi[k % 4][:], gate[:, k, :], ACT.Copy).then_inc(g_hi_ready, 1)

        @block.vector
        def _(dve):
            nc.vector.memset(csum[:], 0.0).then_inc(sums_cleared, 1)
            nc.vector.memset(vsum[:], 0.0).then_inc(sums_cleared, 1)
            steps = [0]

            def chained(instruction):
                instruction.then_inc(table_step, 1)
                steps[0] += 1
                dve.wait_ge(table_step, steps[0])

            dve.wait_ge(small_landed, 16 * SMALL_DMAS)
            chained(nc.vector.tensor_copy(pos[:], pos_int[:]))
            chained(nc.vector.tensor_scalar(angle[:], pos[:], freq[:, 0:1], None, ALU.mult))
            chained(nc.vector.tensor_scalar(turns[:], angle[:], 1.0 / TWO_PI, ROUNDER, ALU.mult, ALU.add))
            chained(nc.vector.tensor_scalar(turns[:], turns[:], -ROUNDER, None, ALU.add))
            for part in (PI_A, PI_B, PI_C):
                chained(nc.vector.scalar_tensor_tensor(out=angle[:], in0=turns[:], scalar=-part, in1=angle[:],
                                                       op0=ALU.mult, op1=ALU.add))
            chained(nc.vector.tensor_scalar(angle_c[:], angle[:], 0.5 * np.pi, None, ALU.add))
            chained(nc.vector.tensor_scalar(turns[:], angle_c[:], PI_SAFE, -TWO_PI, ALU.is_gt, ALU.mult))
            chained(nc.vector.tensor_tensor(angle_c[:], angle_c[:], turns[:], ALU.add))
            chained(nc.vector.tensor_scalar(angle_c[:], angle_c[:], PI_SAFE, -PI_SAFE, ALU.min, ALU.max))
            chained(nc.vector.tensor_scalar(angle[:], angle[:], PI_SAFE, -PI_SAFE, ALU.min, ALU.max))
            nc.vector.tensor_scalar(angle[:], angle[:], freq[:, 1:2], None, ALU.mult).then_inc(angles_ready, 1)

            for q in range(2 * RT):
                r, half = q // 2, q % 2
                dve.wait_ge(xt_hi_ready, q + 1)
                cut = (slice(None), slice(4 * half, 4 * half + 4), slice(r * P, (r + 1) * P))
                nc.vector.tensor_tensor(xt_lo[cut], bank[q % 4][:].rearrange("p (k n) -> p k n", k=4),
                                        xt_hi[cut].bitcast(F32), ALU.subtract).then_inc(xt_lo_ready, 1)
                if q == 1:
                    dve.wait_ge(taps_hi_ready, 1)
                    nc.vector.tensor_copy(conv_w[:], bank[4][:, 0:CT * TAPS]).then_inc(taps_ready, 1)
                    nc.vector.tensor_tensor(conv_w_lo[:], bank[4][:, 0:CT * TAPS], conv_w_hi[:].bitcast(F32),
                                            ALU.subtract).then_inc(taps_lo_ready, 1)

            DVE_TILES = ROUND - 1

            def convolve(j):
                dve.wait_ge(u_ready, ROUND * (j + 1))
                for k in range(TAPS):
                    for i in range(DVE_TILES):
                        t = ROUND * j + i + 1
                        n = DVE_TILES * TAPS * j + DVE_TILES * k + i
                        shifted = u[:, bass.ds(t, 1), k:k + SEQ].rearrange("p o n -> p (o n)")
                        acc_t = acc[:, bass.ds(t, 1), :].rearrange("p o n -> p (o n)")
                        tap = conv_w[:, bass.ds(t * TAPS + k, 1)]
                        if k == 0:
                            nc.vector.tensor_scalar(acc_t, shifted, tap, vec[:, bass.ds(V_CONVB + t, 1)],
                                                    ALU.mult, ALU.add).then_inc(tap_done, 1)
                        else:
                            dve.wait_ge(tap_done, n - DVE_TILES + 1)
                            nc.vector.scalar_tensor_tensor(out=acc_t, in0=shifted, scalar=tap, in1=acc_t,
                                                           op0=ALU.mult, op1=ALU.add).then_inc(tap_done, 1)
                for i in (1, 2, 3, 0):
                    n = ROUND * j + (i - 1) % ROUND
                    if i:
                        dve.wait_ge(tap_done, DVE_TILES * TAPS * (j + 1) - DVE_TILES + i)
                    else:
                        dve.wait_ge(pe_conv_kept, j + 1)
                    wait(dve, csum_done, n)
                    nc.vector.tensor_tensor(csum[:], csum[:],
                                            acc[:, bass.ds(ROUND * j + i, 1), :].rearrange("p o n -> p (o n)"),
                                            ALU.add).then_inc(csum_done, 1)

            dve.wait_ge(sums_cleared, 2)
            dve.wait_ge(vec_ready, 1)
            dve.wait_ge(taps_ready, 1)
            dve.wait_ge(pad_ready, 1)
            dve.wait_ge(rope_ready, 2)
            convolve(0)
            with dve.Fori(1, ROUNDS) as j:
                convolve(j)

            dve.wait_ge(mean_done, 1)
            for t in range(CT + 2):
                if t < CT:
                    nc.vector.scalar_tensor_tensor(out=acc[:, t, :], in0=bank[7][:], scalar=-1.0 / CONV_WIDTH,
                                                   in1=acc[:, t, :], op0=ALU.mult, op1=ALU.add
                                                   ).then_inc(centered, 1)
                if t >= 2:
                    dve.wait_ge(squared, t - 1)
                    wait(dve, vsum_done, t - 2)
                    nc.vector.tensor_tensor(vsum[:], vsum[:], sq[t % 2][:], ALU.add).then_inc(vsum_done, 1)

            stat_count = [0]

            def stat(instruction):
                instruction.then_inc(stat_step, 1)
                stat_count[0] += 1
                dve.wait_ge(stat_step, stat_count[0])

            def refined_rstd(var, std, t, rstd, ready):
                stat(nc.vector.reciprocal(rstd, std))
                stat(nc.vector.tensor_tensor(t, rstd, rstd, ALU.mult))
                stat(nc.vector.tensor_tensor(t, t, var, ALU.mult))
                stat(nc.vector.tensor_scalar(t, t, -0.5, 1.5, ALU.mult, ALU.add))
                nc.vector.tensor_tensor(rstd, rstd, t, ALU.mult).then_inc(ready, 1)

            dve.wait_ge(var_done, 1)
            nc.vector.tensor_scalar(var_a[:], bank[7][:], 1.0 / CONV_WIDTH, LN_EPS, ALU.mult, ALU.add
                                    ).then_inc(var_ready, 1)
            dve.wait_ge(std_ready, 1)
            refined_rstd(var_a[:], std_a[:], newton_a[:], rstd_a[:], rstd_ready)
            dve.wait_ge(rstd_ready, 1)
            dve.wait_ge(centered, CT)

            def gate_branch(t):
                dve.wait_ge(silu_done, t + 1)
                dve.wait_ge(evacuated, Z0 + t + 1)
                nc.vector.tensor_tensor(acc[:, t, :], acc[:, t, :], z_a[:, t, :], ALU.mult).then_inc(gated, 1)

            def branch_lo(t):
                dve.wait_ge(g_hi_ready, t + 1)
                nc.vector.tensor_tensor(g_lo[:, t, :], acc[:, t, :], g_hi[:, t, :].bitcast(F32), ALU.subtract
                                        ).then_inc(g_lo_ready, 1)

            for t in range(CT + 8):
                if t < CT:
                    nc.vector.tensor_tensor(acc[:, t, :], acc[:, t, :], rstd_a[:], ALU.mult).then_inc(scaled, 1)
                if 3 <= t < CT + 3:
                    gate_branch(t - 3)
                if t >= 8:
                    branch_lo(t - 8)

            def row_norm(n, r, rows, scale):
                dve.wait_ge(y_done, n + 1)
                for half in range(HALVES):
                    cut = res[:, r, half * BANK:(half + 1) * BANK]
                    nc.vector.scalar_tensor_tensor(out=cut, in0=cut, scalar=scale, in1=bank[2 * r + half][:],
                                                   op0=ALU.mult, op1=ALU.add).then_inc(y_step, 1)
                wait(dve, row_scaled, n)
                for half in range(HALVES):
                    dve.wait_ge(y_step, 5 * n + half + 1)
                    nc.vector.bn_stats(bn[:, half, :], res[:, r, half * BANK:(half + 1) * BANK]
                                       ).then_inc(y_step, 1)
                dve.wait_ge(y_step, 5 * n + 4)
                nc.vector.bn_aggr(mean_var[:], bn[:].rearrange("p a b -> p (a b)")).then_inc(var_row_ready, 1)
                dve.wait_ge(rstd_row_ready, n + 1)
                nc.vector.tensor_scalar(res[:, r, :], res[:, r, :], mean_var[:, 0:1], rstd_row[:, 1:2],
                                        ALU.subtract, ALU.mult).then_inc(y_step, 1)
                dve.wait_ge(y_step, 5 * n + 5)
                nc.vector.tensor_tensor(res[:, r, :], res[:, r, :], rows[:, 0, :], ALU.mult
                                        ).then_inc(row_scaled, 1)

            def turned_lo(q):
                r, half = q // 2, q % 2
                cut = (slice(None), slice(4 * half, 4 * half + 4), slice(r * P, (r + 1) * P))
                dve.wait_ge(ht_hi_ready, q + 1)
                nc.vector.tensor_tensor(ht_lo[cut], bank[q][:].rearrange("p (k n) -> p k n", k=4),
                                        ht_hi[cut].bitcast(F32), ALU.subtract).then_inc(ht_lo_ready, 1)

            dve.wait_ge(res_ready, RT)
            for r in range(RT):
                row_norm(r, r, ln_rows, 1.0)
                if r > 0 and not only_a:
                    turned_lo(2 * r - 2)
                    turned_lo(2 * r - 1)
            if only_a:
                return
            turned_lo(2 * RT - 2)
            turned_lo(2 * RT - 1)

            bcount = [0]

            def b_next(instruction):
                instruction.then_inc(b_step, 1)
                bcount[0] += 1
                dve.wait_ge(b_step, bcount[0])

            dve.wait_ge(row_ready, RT)
            for which, tiles in ((0, range(KV)), (1, range(KV + 1, LATENTS))):
                for m in tiles:
                    dve.wait_ge(evacuated, OUT0 + m + 1)
                    if m == tiles[0]:
                        b_next(nc.vector.tensor_tensor(b_sum[:, which, :], lat[:, m, :], lat[:, m, :], ALU.mult))
                    else:
                        b_next(nc.vector.tensor_tensor(b_sq[:], lat[:, m, :], lat[:, m, :], ALU.mult))
                        b_next(nc.vector.tensor_tensor(b_sum[:, which, :], b_sum[:, which, :], b_sq[:], ALU.add))
            dve.wait_ge(k_swapped, 64)
            dve.wait_ge(rope_ready, 2)
            b_next(nc.vector.tensor_tensor(lat[:, KV, :], lat[:, KV, :], cos[:], ALU.mult))
            b_next(nc.vector.tensor_tensor(k_swap[:], k_swap[:], sin[:], ALU.mult))
            for which, rank in ((0, KV_RANK), (1, Q_RANK)):
                dve.wait_ge(b_sum_done, which + 1)
                nc.vector.tensor_scalar(b_var[:, which, :], bank[4 + which][:], 1.0 / rank, RMS_EPS,
                                        ALU.mult, ALU.add).then_inc(b_var_ready, 1)
            dve.wait_ge(b_std_ready, 1)
            dve.wait_ge(b_var_ready, 2)
            for which in range(2):
                refined_rstd(b_var[:, which, :], b_std[:, which, :], b_newton[:], b_rstd[:, which, :], b_rstd_ready)
                dve.wait_ge(b_rstd_ready, which + 1)
            for m in range(LATENTS):
                if m == KV:
                    nc.vector.tensor_tensor(lat[:, KV, :], lat[:, KV, :], k_swap[:], ALU.add).then_inc(lat_scaled, 1)
                    continue
                gain = V_KVG + m if m < KV else V_QG + m - KV - 1
                nc.vector.scalar_tensor_tensor(out=lat[:, m, :], in0=lat[:, m, :], scalar=vec[:, gain:gain + 1],
                                               in1=b_rstd[:, 0 if m < KV else 1, :], op0=ALU.mult, op1=ALU.mult
                                               ).then_inc(lat_scaled, 1)
            for m in range(LATENTS):
                dve.wait_ge(lat_hi_ready, m + 1)
                hi, lo = ((ckv_hi[:, m, :], ckv_lo[:, m, :]) if m < KV else (kr_hi[:], kr_lo[:]) if m == KV
                          else (cq_hi[:, m - KV - 1, :], cq_lo[:, m - KV - 1, :]))
                nc.vector.tensor_tensor(lo, lat[:, m, :], hi.bitcast(F32), ALU.subtract).then_inc(lat_lo_ready, 1)

            def mask_scores(h):
                for b in range(RT):
                    n = (b + 1) * P
                    dve.wait_ge(scores_done, RT * h + b + 1)
                    nc.vector.memset(waited[:, b:b + 1], 0.0)
                    nc.vector.tensor_tensor_reduce(prob[:, prob_at[b] * P:prob_at[b] * P + n], bank[b % 2][:, 0:n],
                                                   mask[:, SEQ - n:SEQ], 1.0, MAX_START, ALU.add, ALU.max,
                                                   top[:, b:b + 1]).then_inc(masked, 1)
                dve.wait_ge(masked, RT * h + RT)
                nc.vector.tensor_scalar(neg_top[:], top[:], -SM_SCALE, None, ALU.mult).then_inc(neg_top_ready, 1)

            def normalise(h):
                dve.wait_ge(exp_done, RT * (h + 1))
                nc.vector.reciprocal(inv_denom[:], denom[:]).then_inc(inv_ready, 1)
                dve.wait_ge(inv_ready, h + 1)
                for b in range(RT):
                    block_ = prob[:, prob_at[b] * P:(prob_at[b] + b + 1) * P]
                    nc.vector.tensor_scalar(block_, block_, inv_denom[:, b:b + 1], None, ALU.mult
                                            ).then_inc(prob_ready, 1)

            def projection_lo_pair(p, slot):
                for half in range(2):
                    dve.wait_ge(proj_hi_ready, 7 * p + half + 1)
                    cut = (slice(None), slice(2 * half, 2 * half + 2), slice(None))
                    nc.vector.tensor_tensor(v_lo[slot][cut], bank[5 + half][:].rearrange("p (t n) -> p t n", t=2),
                                            v_hi[slot][cut].bitcast(F32), ALU.subtract).then_inc(proj_lo_ready, 1)

            def projection_lo(p, e):
                for n, (hi, lo) in enumerate(((k_hi, k_lo), (q_hi, q_lo))):
                    dve.wait_ge(proj_hi_ready, 7 * p + 3 + 2 * e + n + 1)
                    nc.vector.tensor_tensor(lo[e][:], bank[PROJ_BANK[3 + 2 * e + n]][:], hi[e][:].bitcast(F32),
                                            ALU.subtract).then_inc(proj_lo_ready, 1)

            def transposed_lo(h):
                for b in range(RT):
                    dve.wait_ge(pt_hi_ready, RT * h + b + 1)
                    cut = (slice(None), slice(0, b + 1), slice(b * P, (b + 1) * P))
                    nc.vector.tensor_tensor(pt_lo[cut], bank[2 + b % 2][:, 0:(b + 1) * P].rearrange(
                        "p (k n) -> p k n", k=b + 1), pt_hi[cut].bitcast(F32), ALU.subtract
                    ).then_inc(pt_lo_ready, 1)

            def gate_head(h):
                dve.wait_ge(pv_done, h + 1)
                tile = gate[:, bass.ds(h, 1), :].rearrange("p o n -> p (o n)")
                nc.vector.tensor_tensor(tile, bank[4][:], tile, ALU.mult).then_inc(gate_ready, 1)

            dve.wait_ge(consts_ready, 6)
            dve.wait_ge(w_used, FIN0)
            projection_lo_pair(0, 0)
            projection_lo(0, 0)
            mask_scores(0)
            normalise(0)
            projection_lo(0, 1)
            transposed_lo(0)

            def head(g, s):
                h = ROUND * g + s
                mask_scores(h)
                gate_head(h - 1)
                last = isinstance(h, int) and h == N_HEADS - 1
                p = 2 * g + (s + 1) // 2
                if not last and s % 2 == 1:
                    projection_lo_pair(p, ((s + 1) // 2) % 2)
                normalise(h)
                if not last:
                    projection_lo(p, (s + 1) % 2)
                transposed_lo(h)

            dve.wait_ge(evacuated, OUT0 + LATENTS + N_HEADS)
            heads_loop(dve, head)
            gate_head(N_HEADS - 1)

            for k in range(CT):
                dve.wait_ge(g_hi_ready, CT + k + 1)
                nc.vector.tensor_tensor(fg_lo[k % 4][:], gate[:, k, :], fg_hi[k % 4][:].bitcast(F32), ALU.subtract
                                        ).then_inc(g_lo_ready, 1)
            dve.wait_ge(ln_rows_landed, 32)
            for r in range(RT):
                row_norm(RT + r, r, ln_rows_b, ALPHA)

        @block.tensor
        def _(pe):
            def product(out_ap, parts, start, stop):
                last = None
                for n, (s_hi, s_lo, m_hi, m_lo) in enumerate(parts):
                    for m, (a, b) in enumerate(((s_lo, m_hi), (s_hi, m_lo), (s_hi, m_hi))):
                        last = nc.tensor.matmul(out_ap, a, b, start=(start and n == 0 and m == 0),
                                                stop=(stop and n == len(parts) - 1 and m == 2))
                return last

            pe.wait_ge(consts_ready, 6)
            for r in range(RT):
                pe.wait_ge(x_landed[r], 16)
                for half in range(2):
                    q = 2 * r + half
                    wait(pe, xt_lo_ready, q - 3)
                    for k in range(4):
                        last = nc.tensor.transpose(bank[q % 4][:, k * P:(k + 1) * P],
                                                   x_in[:, r, (4 * half + k) * P:(4 * half + k + 1) * P], ident[:])
                    last.then_inc(x_turned, 1)
                if r == 0:
                    pe.wait_ge(small_landed, 16 * SMALL_DMAS)
                    for t in range(CT):
                        last = nc.tensor.transpose(bank[4][:, t * TAPS:(t + 1) * TAPS],
                                                   taps_raw[:, t * P:(t + 1) * P], ident[0:TAPS, 0:TAPS])
                    last.then_inc(taps_turned, 1)
                    nc.tensor.transpose(bank[5][:, 0:V_ALL], vec_raw[:], ident[0:V_ALL, 0:V_ALL]
                                        ).then_inc(vec_turned, 1)

            def columns(c, slot, out_bank, bank_free, hi, lo):
                pe.wait_ge(w_hi_ready, c + 1)
                pe.wait_ge(w_lo_ready, c + 1)
                wait(pe, evacuated, bank_free)
                parts = [(w_hi[slot][:, k * P:(k + 1) * P], w_lo[slot][:, k * P:(k + 1) * P],
                          hi[:, k, :], lo[:, k, :]) for k in range(KD)]
                product(bank[out_bank][:], parts, True, True).then_inc(w_used, 1)

            def value_gate(j):
                for s in range(ROUND):
                    for w in range(2):
                        c = 2 * ROUND * j + 2 * s + w
                        columns(c, (2 * s + w) % SLOTS, (2 * s + w) % 4, c - 3, xt_hi, xt_lo)
                    if s == 2:
                        pe.wait_ge(diag_hi_ready, 2 * j + 2)
                        pe.wait_ge(diag_lo_ready, TAPS * (j + 1))
                        pe.wait_ge(cu_lo_ready, j + 1)
                        wait(pe, pe_conv_kept, j)
                        parts = [(diag_hi[:, k, :], diag_lo[:, k, :], cu_hi[:, k:k + SEQ], cu_lo[:, k:k + SEQ])
                                 for k in range(TAPS)]
                        product(bank[6][:], parts, True, True).then_inc(pe_conv_done, 1)

            pe.wait_ge(xt_lo_ready, 2 * RT)
            value_gate(0)
            with pe.Fori(1, ROUNDS) as j:
                value_gate(j)

            def z_round(j):
                for s in range(ROUND):
                    c = Z0 + ROUND * j + s
                    columns(c, s % SLOTS, s % 4, c - 3, xt_hi, xt_lo)

            with pe.Fori(0, ROUNDS - 2) as j:
                z_round(j)
            pe.wait_ge(csum_done, CT)
            nc.tensor.matmul(bank[7][:], ones[:], csum[:], start=True, stop=True).then_inc(mean_done, 1)
            z_round(ROUNDS - 2)
            pe.wait_ge(vsum_done, CT)
            nc.tensor.matmul(bank[7][:], ones[:], vsum[:], start=True, stop=True).then_inc(var_done, 1)
            z_round(ROUNDS - 1)

            def output_projection(c0, hi_ready, lo_ready, hi, lo, ring):
                def tile(k, r):
                    c = c0 + k
                    cut = slice(r * P, (r + 1) * P)
                    for half in range(HALVES):
                        cols = slice(half * BANK, (half + 1) * BANK)
                        last = product(bank[2 * r + half][:],
                                       [(hi(k)[:, cut], lo(k)[:, cut], w_hi[c % SLOTS][:, cols], w_lo[c % SLOTS][:, cols])],
                                       k == 0, k == CT - 1)
                    return last

                def arrive(k):
                    pe.wait_ge(w_hi_ready, c0 + k + 1)
                    pe.wait_ge(w_lo_ready, c0 + k + 1)
                    pe.wait_ge(g_lo_ready, ring * CT + k + 1)

                for k in range(CT - RESIDENT):
                    arrive(k)
                    for r in range(RT):
                        last = tile(k, r)
                    last.then_inc(w_used, 1)
                for r in range(RT):
                    for k in range(CT - RESIDENT, CT):
                        if r == 0:
                            arrive(k)
                        last = tile(k, r)
                        if r == RT - 1 and k < CT - 1:
                            last.then_inc(w_used, 1)
                    last.then_inc(y_done, 1)

            pe.wait_ge(evacuated, OUT0)
            pe.wait_ge(var_ready, 1)
            output_projection(OUT0, None, None, lambda k: g_hi[:, k, :], lambda k: g_lo[:, k, :], 0)
            if only_a:
                return

            for q in range(2 * RT):
                r, half = q // 2, q % 2
                pe.wait_ge(row_ready, r + 1)
                for k in range(4):
                    last = nc.tensor.transpose(bank[q][:, k * P:(k + 1) * P],
                                               res[:, r, (4 * half + k) * P:(4 * half + k + 1) * P], ident[:])
                    if q == k == 0:
                        last.then_inc(w_used, 1)
                last.then_inc(h_turned, 1)
            pe.wait_ge(ht_lo_ready, 2 * RT)

            for n in range(LATENTS):
                c = LAT0 + n
                columns(c, c % SLOTS, n % 4, OUT0 + n - 3 if n >= 4 else 0, ht_hi, ht_lo)

            def gate_round(j):
                for s in range(ROUND):
                    c = BZ0 + ROUND * j + s
                    columns(c, (BZ0 + s) % SLOTS, (LATENTS + s) % 4,
                            OUT0 + LATENTS + ROUND * j + s - 3, ht_hi, ht_lo)

            gate_round(0)
            for which in range(2):
                pe.wait_ge(b_step, SQUARE_STEPS[which])
                nc.tensor.matmul(bank[4 + which][:], ones[:], b_sum[:, which, :], start=True, stop=True
                                 ).then_inc(b_sum_done, 1)
            with pe.Fori(1, ROUNDS) as j:
                gate_round(j)

            def project(p, e, slot):
                bh, bl = bundle_hi[slot], bundle_lo[slot]
                if e == 0:
                    wait(pe, bundle_lo_ready, 2 * p + 2)
                    for half in range(2):
                        wait(pe, proj_lo_ready, 6 * p if half == 0 else 6 * p - 2)
                        for t in range(2):
                            cut = slice((2 * half + t) * P, (2 * half + t + 1) * P)
                            cols = [slice(UV + k * 2 * V_DIM, UV + (k + 1) * 2 * V_DIM) for k in range(KV)]
                            last = product(bank[5 + half][:, t * 2 * V_DIM:(t + 1) * 2 * V_DIM],
                                           [(ckv_hi[:, k, cut], ckv_lo[:, k, cut], bh[:, cols[k]], bl[:, cols[k]])
                                            for k in range(KV)], True, True)
                        last.then_inc(proj_done, 1)
                    wait(pe, proj_lo_ready, 6 * p - 1)
                    cols = [slice(QR + k * 2 * ROPE, QR + (k + 1) * 2 * ROPE) for k in range(KQ)]
                    product(bank[7][:], [(bh[:, cols[k]], bl[:, cols[k]], cq_hi[:, k, :], cq_lo[:, k, :])
                                         for k in range(KQ)], True, True).then_inc(proj_done, 1)
                if e == 0:
                    pe.wait_ge(proj_lo_ready, 6 * p + 1)
                else:
                    pe.wait_ge(proj_hi_ready, 7 * p + 3)
                cols = [slice(UK + k * 2 * NOPE + e * NOPE, UK + k * 2 * NOPE + (e + 1) * NOPE) for k in range(KV)]
                product(bank[PROJ_BANK[3 + 2 * e]][:],
                        [(bh[:, cols[k]], bl[:, cols[k]], ckv_hi[:, k, :], ckv_lo[:, k, :]) for k in range(KV)],
                        True, True).then_inc(proj_done, 1)
                pe.wait_ge(proj_lo_ready, 6 * p + (2 if e == 0 else 3))
                cols = [slice(QN + k * 2 * NOPE + e * NOPE, QN + k * 2 * NOPE + (e + 1) * NOPE) for k in range(KQ)]
                product(bank[PROJ_BANK[4 + 2 * e]][:],
                        [(bh[:, cols[k]], bl[:, cols[k]], cq_hi[:, k, :], cq_lo[:, k, :]) for k in range(KQ)],
                        True, True).then_inc(proj_done, 1)

            def scores(h, p, e, slot):
                pe.wait_ge(proj_lo_ready, 6 * p + 4 + 2 * e)
                pe.wait_ge(qr_lo_ready, p + 1)
                half = slice(e * ROPE, (e + 1) * ROPE)
                for b in range(RT):
                    n = (b + 1) * P
                    cut = slice(b * P, n)
                    wait(pe, masked, RT * h + b - 1)
                    product(bank[b % 2][:, 0:n],
                            [(q_hi[e][:, cut], q_lo[e][:, cut], k_hi[e][:, 0:n], k_lo[e][:, 0:n]),
                             (qr_hi[slot][half, cut], qr_lo[slot][half, cut], kr_hi[half, 0:n], kr_lo[half, 0:n])],
                            True, True).then_inc(scores_done, 1)

            def turn(h):
                for b in range(RT):
                    pe.wait_ge(prob_ready, RT * h + b + 1)
                    wait(pe, pt_lo_ready, RT * h + b - 1)
                    for k in range(b + 1):
                        last = nc.tensor.transpose(bank[2 + b % 2][:, k * P:(k + 1) * P],
                                                   prob[:, (prob_at[b] + k) * P:(prob_at[b] + k + 1) * P], ident[:])
                    last.then_inc(prob_turned, 1)

            def attend(h, e, slot):
                pe.wait_ge(pt_lo_ready, RT * (h + 1))
                wait(pe, gate_ready, h)
                cols = slice(e * V_DIM, (e + 1) * V_DIM)
                for k in range(RT):
                    last = product(bank[4][:, k * P:], [(v_hi[slot][:, k, cols], v_lo[slot][:, k, cols],
                                                        pt_hi[:, k, k * P:], pt_lo[:, k, k * P:])],
                                   k == 0, k == RT - 1)
                last.then_inc(pv_done, 1)

            pe.wait_ge(lat_lo_ready, LATENTS)
            pe.wait_ge(b_var_ready, 2)
            pe.wait_ge(evacuated, OUT0 + LATENTS + N_HEADS)
            project(0, 0, 0)
            scores(0, 0, 0, 0)
            project(0, 1, 0)
            turn(0)

            def head(g, s):
                h = ROUND * g + s
                scores(h, 2 * g + s // 2, s % 2, (s // 2) % 2)
                attend(h - 1, (s - 1) % 2, ((s - 1) // 2) % 2)
                if not (isinstance(h, int) and h == N_HEADS - 1):
                    project(2 * g + (s + 1) // 2, (s + 1) % 2, ((s + 1) // 2) % 2)
                turn(h)

            heads_loop(pe, head)
            attend(N_HEADS - 1, (N_HEADS - 1) % 2, ((N_HEADS - 1) // 2) % 2)
            pe.wait_ge(gate_ready, N_HEADS)
            output_projection(FIN0, None, None, lambda k: fg_hi[k % 4], lambda k: fg_lo[k % 4], 1)


INPUTS = ["x", "positions", "ln_g", "ln_b", "a_w_in", "a_b_in", "a_conv_w", "a_conv_b", "a_norm_g",
          "a_norm_b", "a_w_out", "a_b_out", "kv_w_down", "kv_norm_g", "kv_w_uk", "kv_w_uv", "b_w_in",
          "b_q_norm_g", "b_w_uq", "b_w_out"]


def kernel(**inputs):
    import numpy as _np
    import concourse.bacc as _bacc
    from concourse import mybir as _mybir
    from concourse.bass_utils import run_bass_kernel_spmd as _run

    nc = _bacc.Bacc("TRN2", target_bir_lowering=False, num_devices=1)
    arrays = {f"in_{name}_dram": _np.ascontiguousarray(inputs[name]) for name in INPUTS}
    pair = _np.arange(0, ROPE, 2, dtype=_np.float32) / _np.float32(ROPE)
    table = _np.ones((P, 2), _np.float32)
    table[:, 0] = _np.tile(_np.power(_np.float32(ROPE_THETA), -pair), 4)
    table[:, 1] = _np.tile(_np.repeat(_np.array([-1.0, 1.0], _np.float32), ROPE // 2), 2)
    arrays["in_rope_freq_dram"] = table
    args = [nc.dram_tensor(name, a.shape, _mybir.dt.from_np(a.dtype), kind="ExternalInput").ap()
            for name, a in arrays.items()]
    args.append(nc.dram_tensor("out_0_dram", (1, SEQ, D_MODEL), _mybir.dt.float32, kind="ExternalOutput").ap())
    trunk_kernel(nc, *args)
    return _run(nc, [arrays], core_ids=[0]).results[0]["out_0_dram"]
```

```python
from contextlib import ExitStack

import numpy as np

import concourse.bass as bass
from concourse import mybir

F32 = mybir.dt.float32
F32R = mybir.dt.float32r
I32 = mybir.dt.int32
ALU = mybir.AluOpType
ACT = mybir.ActivationFunctionType

P = 128
BANK = 512
DEPTH = 2
D_MODEL = 1024
SEQ = 512
CONV_WIDTH = 2 * D_MODEL
TAPS = 31
PAD = TAPS - 1
N_HEADS = 16
NOPE = 128
ROPE = 64
V_DIM = 128
KV_RANK = D_MODEL // 4
Q_RANK = D_MODEL // 2
ALPHA = (2.0 * DEPTH) ** 0.25
LN_EPS = 1e-5
RMS_EPS = 1e-6
MASK_VALUE = -1e30
MAX_START = -3e38
SM_SCALE = float((NOPE + ROPE) ** -0.5)
ROPE_THETA = 10000.0

KD = D_MODEL // P
CT = CONV_WIDTH // P
RT = SEQ // P
KQ = Q_RANK // P
KV = KV_RANK // P
PAIRS = N_HEADS // 2
HALVES = D_MODEL // BANK

ROUND = 4
ROUNDS = CT // ROUND

CHUNK = KD * P
Z0 = 2 * CT
OUT0 = Z0 + CT
LAT0 = OUT0 + CT
LATENTS = KV + 1 + KQ
ROPE_CHUNK = LAT0 + KV
BZ0 = LAT0 + LATENTS
FIN0 = BZ0 + N_HEADS
RAW_SLOTS = 2
SLOTS = 4
RESIDENT = SLOTS

UV = 0
QR = UV + KV * 2 * V_DIM
UK = QR + KQ * 2 * ROPE
QN = UK + KV * 2 * NOPE
BUNDLE = QN + KQ * 2 * NOPE
BUNDLE_PARTS = ((UV, UK), (UK, BUNDLE))

V_BIN = 0
V_CONVB = V_BIN + 3 * CT
V_NG = V_CONVB + CT
V_NB = V_NG + CT
V_KVG = V_NB + CT
V_QG = V_KVG + KV
V_ALL = V_QG + KQ

TWO_PI = 2.0 * np.pi
PI_A = 6.28125
PI_B = float(np.float32(np.floor((TWO_PI - PI_A) * 2.0 ** 20) / 2.0 ** 20))
PI_C = float(np.float32(TWO_PI - PI_A - PI_B))
ROUNDER = 1.5 * 2.0 ** 23
PI_SAFE = 3.1415925


def wait(eng, semaphore, value):
    if not isinstance(value, int) or value > 0:
        eng.wait_ge(semaphore, value)


def trunk_kernel(nc, x, positions, ln_g, ln_b, a_w_in, a_b_in, a_conv_w, a_conv_b, a_norm_g,
                 a_norm_b, a_w_out, a_b_out, kv_w_down, kv_norm_g, kv_w_uk, kv_w_uv, b_w_in,
                 b_q_norm_g, b_w_uq, b_w_out, rope_freq, out, only_a=False):
    x_rows = x.rearrange("b (r p) d -> p (b r) d", p=P)
    out_rows = out.rearrange("b (r p) d -> p (b r) d", p=P)
    w_in_a = a_w_in.rearrange("a (k p) n -> p (a k) n", p=P)
    w_out_a = a_w_out.rearrange("a (k p) n -> (a k) p n", p=P)
    w_down = kv_w_down.rearrange("(k p) n -> p k n", p=P)
    w_in_b = b_w_in.rearrange("a (k p) n -> p (a k) n", p=P)
    w_out_b = b_w_out.rearrange("a (k p) n -> (a k) p n", p=P)
    w_uk = kv_w_uk.rearrange("(k p) h d -> p k (h d)", p=P)
    w_uv = kv_w_uv.rearrange("(k p) h d -> p k (h d)", p=P)
    w_uq = b_w_uq.rearrange("a (k p) h d -> p (a k) h d", p=P)

    with ExitStack() as ctx:
        def sem(name):
            return ctx.enter_context(nc.semaphore(name))

        place = [-(-nc.sbuf_base // 32) * 32]

        def region(words):
            at = place[0]
            place[0] = at + -(-words * 4 // 32) * 32
            assert place[0] <= nc.sbuf_usable_end
            return at

        def at(name, base, offset_words, shape, dtype=F32):
            return nc.alloc_sbuf_tensor_at(name, shape, dtype, offset=base + 4 * offset_words)

        def own(name, shape, dtype=F32):
            words = 1
            for n in shape[1:]:
                words *= n
            return at(name, region(words), 0, shape, dtype)

        TILE = SEQ
        reg_x = region(8 * TILE)
        reg_xt = region(16 * TILE)
        reg_u = region(CT * (SEQ + PAD))
        reg_acc = region(CT * TILE)
        reg_z = region(CT * TILE)
        reg_w = region((RAW_SLOTS + 2 * SLOTS) * CHUNK)
        reg_e = region(4 * TILE)

        ident = own("ident", [P, P])
        ones = own("ones", [P, P])
        conv_w = own("conv_w", [P, CT * TAPS])
        conv_w_hi = own("conv_w_hi", [P, CT * TAPS], F32R)
        conv_w_lo = own("conv_w_lo", [P, CT * TAPS], F32R)
        vec = own("vec", [P, V_ALL])
        cos = own("cos", [P, SEQ])
        sin = own("sin", [P, SEQ])
        mask = own("mask", [P, SEQ])
        freq = own("freq", [P, 2])
        bn = own("bn", [P, HALVES, 6])
        mean_var = own("mean_var", [P, 2])
        rstd_row = own("rstd_row", [P, 2])
        minus_half = own("minus_half", [P, 1])
        top = own("top", [P, RT])
        neg_top = own("neg_top", [P, RT])
        denom = own("denom", [P, RT])
        waited = own("waited", [P, RT])
        inv_denom = own("inv_denom", [P, RT])

        w_raw = [at(f"w_raw{i}", reg_w, i * CHUNK, [P, CHUNK]) for i in range(RAW_SLOTS)]
        w_hi = [at(f"w_hi{i}", reg_w, (RAW_SLOTS + i) * CHUNK, [P, CHUNK], F32R) for i in range(SLOTS)]
        w_lo = [at(f"w_lo{i}", reg_w, (RAW_SLOTS + SLOTS + i) * CHUNK, [P, CHUNK], F32R)
                for i in range(SLOTS)]

        x_in = at("x_in", reg_x, 0, [P, RT, D_MODEL])
        val = [at(f"val{i}", reg_x, i * TILE, [P, SEQ]) for i in range(2)]
        sig = [at(f"sig{i}", reg_x, (2 + i) * TILE, [P, SEQ]) for i in range(2)]
        cu_hi = at("cu_hi", reg_x, 4 * TILE, [P, SEQ + PAD], F32R)
        cu_lo = at("cu_lo", reg_x, 4 * TILE + 544, [P, SEQ + PAD], F32R)
        sq = [at(f"sq{i}", reg_x, i * TILE, [P, SEQ]) for i in range(2)]
        var_a = at("var_a", reg_x, 2 * TILE, [P, SEQ])
        std_a = at("std_a", reg_x, 3 * TILE, [P, SEQ])
        rstd_a = at("rstd_a", reg_x, 4 * TILE, [P, SEQ])
        newton_a = at("newton_a", reg_x, 6 * TILE, [P, SEQ])
        xt_hi = at("xt_hi", reg_xt, 0, [P, KD, SEQ], F32R)
        xt_lo = at("xt_lo", reg_xt, KD * SEQ, [P, KD, SEQ], F32R)
        u = at("u", reg_u, 0, [P, CT, SEQ + PAD])
        taps_raw = at("taps_raw", reg_acc, 0, [TAPS, CONV_WIDTH])
        vec_raw = at("vec_raw", reg_acc, 4 * TILE, [V_ALL, P])
        pos_int = at("pos_int", reg_acc, 5 * TILE, [P, SEQ], I32)
        pos = at("pos", reg_acc, 6 * TILE, [P, SEQ])
        angle = at("angle", reg_acc, 7 * TILE, [P, SEQ])
        turns = at("turns", reg_acc, 8 * TILE, [P, SEQ])
        angle_c = at("angle_c", reg_acc, 9 * TILE, [P, SEQ])
        acc = at("acc", reg_acc, 0, [P, CT, SEQ])
        diag_hi = at("diag_hi", reg_z, 0, [P, TAPS, P], F32R)
        diag_lo = at("diag_lo", reg_z, TAPS * P, [P, TAPS, P], F32R)
        z_a = at("z_a", reg_z, 0, [P, CT, SEQ])
        g_hi = at("g_hi", reg_u, 0, [P, CT, SEQ], F32R)
        g_lo = at("g_lo", reg_z, 0, [P, CT, SEQ], F32R)
        csum = at("csum", reg_e, 0, [P, SEQ])
        vsum = at("vsum", reg_e, TILE, [P, SEQ])

        res = at("res", reg_xt, 0, [P, RT, D_MODEL])
        ln_rows = at("ln_rows", reg_xt, 8 * TILE, [P, 3, D_MODEL])
        ln_rows_b = at("ln_rows_b", reg_x, 0, [P, 2, D_MODEL])

        ht_hi = at("ht_hi", reg_acc, 0, [P, KD, SEQ], F32R)
        ht_lo = at("ht_lo", reg_acc, KD * SEQ, [P, KD, SEQ], F32R)
        lat = at("lat", reg_x, 0, [P, LATENTS, SEQ])
        k_swap = at("k_swap", reg_x, LATENTS * TILE, [P, SEQ])
        b_sq = at("b_sq", reg_xt, 8 * TILE, [P, SEQ])
        b_sum = at("b_sum", reg_xt, 9 * TILE, [P, 2, SEQ])
        b_var = at("b_var", reg_xt, 11 * TILE, [P, 2, SEQ])
        b_std = at("b_std", reg_xt, 13 * TILE, [P, 2, SEQ])
        b_newton = at("b_newton", reg_xt, 15 * TILE, [P, SEQ])
        b_rstd = at("b_rstd", reg_e, 0, [P, 2, SEQ])
        cq_hi = at("cq_hi", reg_u, 0, [P, KQ, SEQ], F32R)
        cq_lo = at("cq_lo", reg_u, 4 * TILE, [P, KQ, SEQ], F32R)
        ckv_hi = at("ckv_hi", reg_u, 8 * TILE, [P, KV, SEQ], F32R)
        ckv_lo = at("ckv_lo", reg_u, 10 * TILE, [P, KV, SEQ], F32R)
        kr_hi = at("kr_hi", reg_u, 12 * TILE, [P, SEQ], F32R)
        kr_lo = at("kr_lo", reg_u, 13 * TILE, [P, SEQ], F32R)
        qr_raw = at("qr_raw", reg_u, 14 * TILE, [P, SEQ])
        qr_swap = at("qr_swap", reg_u, 15 * TILE, [P, SEQ])
        gate = at("gate", reg_z, 0, [P, N_HEADS, SEQ])
        k_hi = [at(f"k_hi{i}", reg_acc, (0 + i) * TILE, [P, SEQ], F32R) for i in range(2)]
        k_lo = [at(f"k_lo{i}", reg_acc, (2 + i) * TILE, [P, SEQ], F32R) for i in range(2)]
        q_hi = [at(f"q_hi{i}", reg_acc, (4 + i) * TILE, [P, SEQ], F32R) for i in range(2)]
        q_lo = [at(f"q_lo{i}", reg_acc, (6 + i) * TILE, [P, SEQ], F32R) for i in range(2)]
        v_hi = [at(f"v_hi{i}", reg_acc, (8 + 2 * i) * TILE, [P, RT, 2 * V_DIM], F32R) for i in range(2)]
        v_lo = [at(f"v_lo{i}", reg_acc, (12 + 2 * i) * TILE, [P, RT, 2 * V_DIM], F32R) for i in range(2)]
        qr_hi = [at(f"qr_hi{i}", reg_e, i * TILE, [P, SEQ], F32R) for i in range(2)]
        qr_lo = [at(f"qr_lo{i}", reg_e, (2 + i) * TILE, [P, SEQ], F32R) for i in range(2)]
        bundle_raw = at("bundle_raw", reg_xt, 8 * TILE, [P, BUNDLE])
        bundle_hi = [at(f"bundle_hi{i}", reg_w, i * BUNDLE, [P, BUNDLE], F32R) for i in range(2)]
        bundle_lo = [at(f"bundle_lo{i}", reg_w, (2 + i) * BUNDLE, [P, BUNDLE], F32R) for i in range(2)]
        prob_at = [0, 1, 3, 6]
        prob = at("prob", reg_xt, 8 * TILE + BUNDLE, [P, 10 * P])
        pt_hi = at("pt_hi", reg_x, 0, [P, RT, SEQ], F32R)
        pt_lo = at("pt_lo", reg_x, 4 * TILE, [P, RT, SEQ], F32R)
        fg_hi = [at(f"fg_hi{i}", reg_u, i * TILE, [P, SEQ], F32R) for i in range(4)]
        fg_lo = [at(f"fg_lo{i}", reg_u, (4 + i) * TILE, [P, SEQ], F32R) for i in range(4)]

        bank = [ctx.enter_context(nc.psum_tensor(f"bank{i}", [P, BANK], F32)) for i in range(8)]

        x_landed = [sem(f"x_landed{r}") for r in range(RT)]
        small_landed = sem("small_landed")
        w_landed = [sem(f"w_landed{i}") for i in range(RAW_SLOTS)]
        w_hi_ready, w_lo_ready, w_used = sem("w_hi_ready"), sem("w_lo_ready"), sem("w_used")
        consts_ready = sem("consts_ready")
        vec_turned, taps_turned, vec_ready = sem("vec_turned"), sem("taps_turned"), sem("vec_ready")
        taps_hi_ready, taps_lo_ready, taps_ready = sem("taps_hi_ready"), sem("taps_lo_ready"), sem("taps_ready")
        x_turned, xt_hi_ready, xt_lo_ready = sem("x_turned"), sem("xt_hi_ready"), sem("xt_lo_ready")
        table_step, angles_ready, rope_ready = sem("table_step"), sem("angles_ready"), sem("rope_ready")
        evacuated = sem("evacuated")
        u_ready, pad_ready = sem("u_ready"), sem("pad_ready")
        diag_hi_ready, diag_lo_ready = sem("diag_hi_ready"), sem("diag_lo_ready")
        cu_hi_ready, cu_lo_ready = sem("cu_hi_ready"), sem("cu_lo_ready")
        pe_conv_done, pe_conv_kept = sem("pe_conv_done"), sem("pe_conv_kept")
        tap_done, csum_done, sums_cleared = sem("tap_done"), sem("csum_done"), sem("sums_cleared")
        mean_done, centered, squared, vsum_done, var_done = (
            sem("mean_done"), sem("centered"), sem("squared"), sem("vsum_done"), sem("var_done"))
        var_ready, std_ready, stat_step, rstd_ready = (
            sem("var_ready"), sem("std_ready"), sem("stat_step"), sem("rstd_ready"))
        scaled, silu_done, gated, g_hi_ready, g_lo_ready = (
            sem("scaled"), sem("silu_done"), sem("gated"), sem("g_hi_ready"), sem("g_lo_ready"))
        res_landed, res_scaled, res_ready = sem("res_landed"), sem("res_scaled"), sem("res_ready")
        y_done, y_step, var_row_ready, rstd_row_ready, rstd_step, row_scaled, row_ready = (
            sem("y_done"), sem("y_step"), sem("var_row_ready"), sem("rstd_row_ready"),
            sem("rstd_step"), sem("row_scaled"), sem("row_ready"))
        h_turned, ht_hi_ready, ht_lo_ready = sem("h_turned"), sem("ht_hi_ready"), sem("ht_lo_ready")
        b_step, b_sum_done, b_var_ready, b_std_ready, b_rstd_ready = (
            sem("b_step"), sem("b_sum_done"), sem("b_var_ready"),
            sem("b_std_ready"), sem("b_rstd_ready"))
        lat_scaled, lat_hi_ready, lat_lo_ready = sem("lat_scaled"), sem("lat_hi_ready"), sem("lat_lo_ready")
        k_swapped = sem("k_swapped")
        bundle_landed, bundle_hi_ready, bundle_lo_ready = (
            sem("bundle_landed"), sem("bundle_hi_ready"), sem("bundle_lo_ready"))
        proj_done, proj_hi_ready, proj_lo_ready = sem("proj_done"), sem("proj_hi_ready"), sem("proj_lo_ready")
        q_swapped, rope_step, qr_rotated, qr_hi_ready, qr_lo_ready = (
            sem("q_swapped"), sem("rope_step"), sem("qr_rotated"), sem("qr_hi_ready"), sem("qr_lo_ready"))
        scores_done, masked, neg_top_ready, exp_done, inv_ready, prob_ready = (
            sem("scores_done"), sem("masked"), sem("neg_top_ready"), sem("exp_done"),
            sem("inv_ready"), sem("prob_ready"))
        prob_turned, pt_hi_ready, pt_lo_ready, pv_done, gate_ready = (
            sem("prob_turned"), sem("pt_hi_ready"), sem("pt_lo_ready"), sem("pv_done"), sem("gate_ready"))
        ln_rows_landed = sem("ln_rows_landed")
        stored = sem("stored")

        SMALL_DMAS = 9
        MEAN_AT, VAR_AT = 4, 9
        PROJ_BANK = (7, 5, 6, 7, 5, 5, 6)
        SQUARE_STEPS = (2 * KV - 1, 2 * KV - 1 + 2 * KQ - 1)

        def landed_value(c):
            extra = 16 if isinstance(c, int) and c >= ROPE_CHUNK and (c - ROPE_CHUNK) % RAW_SLOTS == 0 else 0
            return 16 * (c // RAW_SLOTS + 1) + extra

        def heads_loop(eng, step):
            with eng.Fori(0, ROUNDS - 1) as g:
                for s in range(1, ROUND + 1):
                    step(g, s)
            for s in range(1, ROUND):
                step(ROUNDS - 1, s)

        block = ctx.enter_context(nc.Block())

        @block.sync
        def _(sp):
            for r in range(RT):
                sp.dma_start(x_in[:, r, :], x_rows[:, r, :]).then_inc(x_landed[r], 16)
                if r == 0:
                    sp.dma_start(taps_raw[:], a_conv_w[0]).then_inc(small_landed, 16)
                    for row, vector, n in ((V_BIN, a_b_in, 3 * CT), (V_CONVB, a_conv_b, CT),
                                           (V_NG, a_norm_g, CT), (V_NB, a_norm_b, CT),
                                           (V_QG, b_q_norm_g, KQ)):
                        sp.dma_start(vec_raw[row:row + n, :], vector.rearrange("a (n p) -> (a n) p", p=P)
                                     ).then_inc(small_landed, 16)
                    sp.dma_start(vec_raw[V_KVG:V_KVG + KV, :], kv_norm_g.rearrange("(n p) -> n p", p=P)
                                 ).then_inc(small_landed, 16)
                    sp.dma_start(freq[:], rope_freq).then_inc(small_landed, 16)
                    sp.dma_start(pos_int[:], positions.broadcast_to([P, SEQ])).then_inc(small_landed, 16)

            def raw_free(c):
                wait(sp, w_hi_ready, c - RAW_SLOTS + 1)
                wait(sp, w_lo_ready, c - RAW_SLOTS + 1)

            def load_columns(c, slot, source, column, n=P):
                sp.dma_start(w_raw[slot][:].rearrange("p (k m) -> p k m", m=P),
                             source[:, :, bass.ds(column, P)]).then_inc(w_landed[slot], 16)

            def load_value_gate(j):
                for s in range(ROUND):
                    for w in range(2):
                        raw_free(2 * ROUND * j + 2 * s + w)
                        load_columns(None, w, w_in_a, w * CONV_WIDTH + (ROUND * j + s) * P)

            load_value_gate(0)
            with sp.Fori(1, ROUNDS) as j:
                load_value_gate(j)
            with sp.Fori(0, ROUNDS) as j:
                for s in range(ROUND):
                    raw_free(Z0 + ROUND * j + s)
                    load_columns(None, s % 2, w_in_a, 2 * CONV_WIDTH + (ROUND * j + s) * P)

            def load_output_a(k):
                raw_free(OUT0 + k)
                sp.dma_start(w_raw[k % 2][:], w_out_a[k]).then_inc(w_landed[k % 2], 16)

            for k in range(RAW_SLOTS):
                load_output_a(k)
            sp.wait_ge(w_used, OUT0)
            sp.dma_start(res[:], x_rows).then_inc(res_landed, 16)
            sp.dma_start(ln_rows[:, 0, :], ln_g[0:1, :].broadcast_to([P, D_MODEL])).then_inc(res_landed, 16)
            sp.dma_start(ln_rows[:, 1, :], ln_b[0:1, :].broadcast_to([P, D_MODEL])).then_inc(res_landed, 16)
            sp.dma_start(ln_rows[:, 2, :], a_b_out.broadcast_to([P, D_MODEL])).then_inc(res_landed, 16)
            for k in range(RAW_SLOTS, CT):
                load_output_a(k)
            if only_a:
                for r in range(RT):
                    sp.wait_ge(row_ready, r + 1)
                    sp.dma_start(out_rows[:, r, :], res[:, r, :]).then_inc(stored, 16)
                sp.wait_ge(stored, 16 * RT)
                return

            for n in range(LATENTS):
                c = LAT0 + n
                raw_free(c)
                if n < KV:
                    load_columns(c, c % 2, w_down, n * P)
                elif n == KV:
                    halves = w_raw[c % 2][:].rearrange("p (k b m) -> p b k m", b=2, m=ROPE)
                    for b in range(2):
                        sp.dma_start(halves[:, b], w_down[:, :, KV_RANK:KV_RANK + ROPE]
                                     ).then_inc(w_landed[c % 2], 16)
                else:
                    load_columns(c, c % 2, w_in_b, (n - KV - 1) * P)
            for i in range(ROUND):
                raw_free(BZ0 + i)
                load_columns(None, (BZ0 + i) % 2, w_in_b, Q_RANK + i * P)
            sp.wait_ge(evacuated, OUT0 + KV + 1)
            for b in range(4):
                sp.dma_start(k_swap[32 * b:32 * b + 32, :], lat[32 * (b ^ 1):32 * (b ^ 1) + 32, KV, :]
                             ).then_inc(k_swapped, 16)
            with sp.Fori(1, ROUNDS) as j:
                for s in range(ROUND):
                    raw_free(BZ0 + ROUND * j + s)
                    load_columns(None, (BZ0 + s) % 2, w_in_b, Q_RANK + (ROUND * j + s) * P)

            def load_bundle(p):
                wait(sp, bundle_hi_ready, 2 * p)
                wait(sp, bundle_lo_ready, 2 * p)
                for off, source in ((UK, w_uk), (UV, w_uv)):
                    sp.dma_start(bundle_raw[:, off:off + KV * 2 * NOPE].rearrange("p (k m) -> p k m", k=KV),
                                 source[:, :, bass.ds(p * 2 * NOPE, 2 * NOPE)]).then_inc(bundle_landed, 16)
                for e in range(2):
                    qn = bundle_raw[:, QN:BUNDLE].rearrange("p (k e m) -> p e k m", k=KQ, e=2)
                    qr = bundle_raw[:, QR:UK].rearrange("p (k e m) -> p e k m", k=KQ, e=2)
                    sp.dma_start(qn[:, e], w_uq[:, :, bass.ds(2 * p + e, 1), 0:NOPE].rearrange("p k o m -> p k (o m)")
                                 ).then_inc(bundle_landed, 16)
                    sp.dma_start(qr[:, e], w_uq[:, :, bass.ds(2 * p + e, 1), NOPE:NOPE + ROPE].rearrange("p k o m -> p k (o m)")
                                 ).then_inc(bundle_landed, 16)

            def swap_rotary(p):
                sp.wait_ge(proj_hi_ready, 7 * p + 3)
                for b in range(4):
                    sp.dma_start(qr_swap[32 * b:32 * b + 32, :], qr_raw[32 * (b ^ 1):32 * (b ^ 1) + 32, :]
                                 ).then_inc(q_swapped, 16)

            sp.wait_ge(lat_scaled, LATENTS)
            load_bundle(0)
            load_bundle(1)
            swap_rotary(0)
            with sp.Fori(1, PAIRS - 1) as p:
                load_bundle(p + 1)
                swap_rotary(p)
            swap_rotary(PAIRS - 1)

            sp.wait_ge(proj_done, 7 * PAIRS)
            for k in range(CT):
                c = FIN0 + k
                raw_free(c)
                sp.dma_start(w_raw[c % 2][:], w_out_b[k]).then_inc(w_landed[c % 2], 16)
                if k == 1:
                    sp.wait_ge(pv_done, N_HEADS)
                    sp.dma_start(ln_rows_b[:, 0, :], ln_g[1:2, :].broadcast_to([P, D_MODEL])
                                 ).then_inc(ln_rows_landed, 16)
                    sp.dma_start(ln_rows_b[:, 1, :], ln_b[1:2, :].broadcast_to([P, D_MODEL])
                                 ).then_inc(ln_rows_landed, 16)
            for r in range(RT):
                sp.wait_ge(row_ready, RT + r + 1)
                sp.dma_start(out_rows[:, r, :], res[:, r, :]).then_inc(stored, 16)
            sp.wait_ge(stored, 16 * RT)

        @block.gpsimd
        def _(pool):
            nc.gpsimd.memset(ident[:], 0.0).then_inc(consts_ready, 1)
            nc.gpsimd.memset(mask[:], 0.0).then_inc(consts_ready, 1)
            nc.gpsimd.memset(ones[:], 1.0).then_inc(consts_ready, 1)
            nc.gpsimd.memset(minus_half[:], -0.5).then_inc(consts_ready, 1)
            pool.wait_ge(consts_ready, 4)
            nc.gpsimd.affine_select(out=ident[:], in_=ident[:], compare_op=ALU.not_equal, fill=1.0, base=0,
                                    pattern=[[-1, P]], channel_multiplier=1).then_inc(consts_ready, 1)
            nc.gpsimd.affine_select(out=mask[:], in_=mask[:], compare_op=ALU.is_ge, fill=MASK_VALUE,
                                    base=SEQ - P, pattern=[[-1, SEQ]], channel_multiplier=1
                                    ).then_inc(consts_ready, 1)
            nc.gpsimd.memset(u[:, :, 0:PAD], 0.0).then_inc(pad_ready, 1)

            def split_lo(c, raw, slot):
                pool.wait_ge(w_hi_ready, c + 1)
                wait(pool, w_used, c - SLOTS + 1)
                nc.gpsimd.tensor_tensor(w_lo[slot][:], w_raw[raw][:], w_hi[slot][:].bitcast(F32),
                                        ALU.subtract).then_inc(w_lo_ready, 1)

            def glu(t, slot):
                pool.wait_ge(evacuated, 2 * t + 2)
                nc.gpsimd.tensor_tensor(u[:, bass.ds(t, 1), PAD:].rearrange("p o n -> p (o n)"), val[slot][:], sig[slot][:],
                                        ALU.mult).then_inc(u_ready, 1)

            def value_gate(j):
                for s in range(ROUND):
                    t = ROUND * j + s
                    for w in range(2):
                        split_lo(2 * t + w, w, (2 * s + w) % SLOTS)
                    if not isinstance(t, int) or t > 0:
                        glu(t - 1, (s - 1) % 2)
                    if not isinstance(j, int) or j > 0:
                        if s < 2:
                            conv_matrices(j, s)
                        if s == 2:
                            conv_input_lo(j)

            def conv_matrices(j, part):
                pool.wait_ge(w_used, 2 * ROUND * j - 1)
                lo, hi = (0, TAPS // 2) if part == 0 else (TAPS // 2, TAPS)
                n = hi - lo
                taps = conv_w_hi[:, bass.ds(j * (ROUND * TAPS) - TAPS + lo, n)].bitcast(F32)
                nc.gpsimd.tensor_tensor(diag_hi[:, lo:hi, :],
                                        ident[:].unsqueeze(1).broadcast_to([P, n, P]),
                                        taps.unsqueeze(2).broadcast_to([P, n, P]),
                                        ALU.mult).then_inc(diag_hi_ready, 1)

            def conv_input_lo(j):
                pool.wait_ge(cu_hi_ready, j)
                nc.gpsimd.tensor_tensor(cu_lo[:], u[:, bass.ds(ROUND * j - 1, 1), :].rearrange("p o n -> p (o n)"),
                                        cu_hi[:].bitcast(F32), ALU.subtract).then_inc(cu_lo_ready, 1)

            pool.wait_ge(x_turned, 2 * RT)
            value_gate(0)
            pool.wait_ge(taps_hi_ready, 1)
            with pool.Fori(1, ROUNDS) as j:
                value_gate(j)
            for i in range(CT):
                split_lo(Z0 + i, i % 2, i % SLOTS)
                if i == 0:
                    glu(CT - 1, (CT - 1) % 2)
                if i < 2:
                    conv_matrices(ROUNDS, i)
                if i == 2:
                    conv_input_lo(ROUNDS)

            def rstd_of_row(n):
                pool.wait_ge(var_row_ready, n + 1)
                nc.gpsimd.tensor_scalar(rstd_row[:, 0:1], mean_var[:, 1:2], LN_EPS, None, ALU.add
                                        ).then_inc(rstd_step, 1)
                pool.wait_ge(rstd_step, n + 1)
                nc.gpsimd.tensor_tensor(rstd_row[:, 1:2], rstd_row[:, 0:1], minus_half[:], ALU.pow
                                        ).then_inc(rstd_row_ready, 1)

            def add_ln_bias(n, r, rows):
                pool.wait_ge(row_scaled, n + 1)
                nc.gpsimd.tensor_tensor(res[:, r, :], res[:, r, :], rows[:, 1, :], ALU.add
                                        ).then_inc(row_ready, 1)

            for k in range(CT):
                c = OUT0 + k
                split_lo(c, c % 2, c % SLOTS)
                if 4 <= k < 4 + RT:
                    r = k - 4
                    pool.wait_ge(res_scaled, r + 1)
                    nc.gpsimd.tensor_tensor(res[:, r, :], res[:, r, :], ln_rows[:, 2, :], ALU.add
                                            ).then_inc(res_ready, 1)
            for r in range(RT):
                rstd_of_row(r)
                if r > 0:
                    add_ln_bias(r - 1, r - 1, ln_rows)
            if not only_a:
                split_lo(LAT0, LAT0 % 2, LAT0 % SLOTS)
                split_lo(LAT0 + 1, (LAT0 + 1) % 2, (LAT0 + 1) % SLOTS)
            add_ln_bias(RT - 1, RT - 1, ln_rows)
            if only_a:
                return
            for c in range(LAT0 + 2, BZ0 + N_HEADS):
                split_lo(c, c % 2, c % SLOTS)

            def split_bundle_lo(p, slot):
                for part, (lo, hi) in enumerate(BUNDLE_PARTS):
                    pool.wait_ge(bundle_hi_ready, 2 * p + part + 1)
                    nc.gpsimd.tensor_tensor(bundle_lo[slot][:, lo:hi], bundle_raw[:, lo:hi],
                                            bundle_hi[slot][:, lo:hi].bitcast(F32), ALU.subtract
                                            ).then_inc(bundle_lo_ready, 1)

            def rotate(p, slot):
                pool.wait_ge(q_swapped, 64 * (p + 1))
                nc.gpsimd.tensor_tensor(qr_raw[:], qr_raw[:], cos[:], ALU.mult).then_inc(rope_step, 1)
                nc.gpsimd.tensor_tensor(qr_swap[:], qr_swap[:], sin[:], ALU.mult).then_inc(rope_step, 1)
                pool.wait_ge(rope_step, 2 * p + 2)
                nc.gpsimd.tensor_tensor(qr_raw[:], qr_raw[:], qr_swap[:], ALU.add).then_inc(qr_rotated, 1)
                pool.wait_ge(qr_hi_ready, p + 1)
                nc.gpsimd.tensor_tensor(qr_lo[slot][:], qr_raw[:], qr_hi[slot][:].bitcast(F32), ALU.subtract
                                        ).then_inc(qr_lo_ready, 1)

            split_bundle_lo(0, 0)
            split_bundle_lo(1, 1)
            rotate(0, 0)
            with pool.Fori(0, PAIRS // 2 - 1) as i:
                for e in range(2):
                    rotate(2 * i + e + 1, (e + 1) % 2)
                    split_bundle_lo(2 * i + e + 2, e)
            rotate(PAIRS - 1, (PAIRS - 1) % 2)

            pool.wait_ge(proj_done, 7 * PAIRS)
            for k in range(CT):
                c = FIN0 + k
                split_lo(c, c % 2, c % SLOTS)
            for r in range(RT):
                rstd_of_row(RT + r)
                if r > 0:
                    add_ln_bias(RT + r - 1, r - 1, ln_rows_b)
            add_ln_bias(2 * RT - 1, RT - 1, ln_rows_b)

        @block.scalar
        def _(act):
            for q in range(2 * RT):
                r, half = q // 2, q % 2
                act.wait_ge(x_turned, q + 1)
                nc.scalar.activation(xt_hi[:, 4 * half:4 * half + 4, r * P:(r + 1) * P],
                                     bank[q % 4][:].rearrange("p (k n) -> p k n", k=4), ACT.Copy
                                     ).then_inc(xt_hi_ready, 1)
                if q == 1:
                    act.wait_ge(taps_turned, 1)
                    nc.scalar.activation(conv_w_hi[:], bank[4][:, 0:CT * TAPS], ACT.Copy
                                         ).then_inc(taps_hi_ready, 1)
                    act.wait_ge(vec_turned, 1)
                    nc.scalar.activation(vec[:], bank[5][:, 0:V_ALL], ACT.Copy).then_inc(vec_ready, 1)

            def split_hi(c, raw, slot, landed):
                act.wait_ge(w_landed[raw], landed)
                wait(act, w_used, c - SLOTS + 1)
                nc.scalar.activation(w_hi[slot][:], w_raw[raw][:], ACT.Copy).then_inc(w_hi_ready, 1)

            def keep_value_gate(t, s):
                wait(act, u_ready, t - 1)
                act.wait_ge(w_used, 2 * t + 1)
                nc.scalar.activation(val[s % 2][:], bank[2 * s % 4][:], ACT.Identity,
                                     bias=vec[:, bass.ds(V_BIN + t, 1)]).then_inc(evacuated, 1)
                act.wait_ge(w_used, 2 * t + 2)
                nc.scalar.activation(sig[s % 2][:], bank[(2 * s + 1) % 4][:], ACT.Sigmoid,
                                     bias=vec[:, bass.ds(V_BIN + CT + t, 1)]).then_inc(evacuated, 1)

            def value_gate(j):
                for s in range(ROUND):
                    t = ROUND * j + s
                    for w in range(2):
                        split_hi(2 * t + w, w, (2 * s + w) % SLOTS, 16 * (t + 1))
                    if not isinstance(t, int) or t > 0:
                        keep_value_gate(t - 1, s - 1)
                    if not isinstance(j, int) or j > 0:
                        if s < 2:
                            conv_matrices(j, s)
                        if s == 2:
                            conv_input_hi(j)
                        if s == 3:
                            keep_conv(j)

            def conv_matrices(j, part):
                if part == 0:
                    act.wait_ge(w_used, 2 * ROUND * j - 1)
                for k in range(*((0, TAPS // 2) if part == 0 else (TAPS // 2, TAPS))):
                    nc.scalar.activation(
                        diag_lo[:, k, :], ident[:], ACT.Copy,
                        scale=conv_w_lo[:, bass.ds(j * (ROUND * TAPS) - TAPS + k, 1)].bitcast(F32)
                    ).then_inc(diag_lo_ready, 1)

            def conv_input_hi(j):
                act.wait_ge(u_ready, ROUND * j)
                nc.scalar.activation(cu_hi[:], u[:, bass.ds(ROUND * j - 1, 1), :].rearrange("p o n -> p (o n)"),
                                     ACT.Copy).then_inc(cu_hi_ready, 1)

            def keep_conv(j):
                act.wait_ge(pe_conv_done, j)
                nc.scalar.activation(acc[:, bass.ds(ROUND * j - 1, 1), :].rearrange("p o n -> p (o n)"), bank[6][:],
                                     ACT.Identity, bias=vec[:, bass.ds(V_CONVB + ROUND * j - 1, 1)]
                                     ).then_inc(pe_conv_kept, 1)

            act.wait_ge(angles_ready, 1)
            nc.scalar.activation(sin[:], angle[:], ACT.Sin).then_inc(rope_ready, 1)
            nc.scalar.activation(cos[:], angle_c[:], ACT.Sin).then_inc(rope_ready, 1)

            act.wait_ge(x_turned, 2 * RT)
            value_gate(0)
            act.wait_ge(taps_lo_ready, 1)
            act.wait_ge(pad_ready, 1)
            act.wait_ge(rope_ready, 2)
            with act.Fori(1, ROUNDS) as j:
                value_gate(j)

            def keep_z(i):
                act.wait_ge(w_used, Z0 + i + 1)
                nc.scalar.activation(z_a[:, i, :], bank[i % 4][:], ACT.Silu,
                                     bias=vec[:, V_BIN + 2 * CT + i:V_BIN + 2 * CT + i + 1]
                                     ).then_inc(evacuated, 1)

            def z_split(i):
                c = Z0 + i
                split_hi(c, c % 2, c % SLOTS, landed_value(c))

            def square(t):
                act.wait_ge(centered, t + 1)
                wait(act, vsum_done, t - 1)
                nc.scalar.activation(sq[t % 2][:], acc[:, t, :], ACT.Square).then_inc(squared, 1)

            def branch_silu(t):
                act.wait_ge(scaled, t + 1)
                nc.scalar.activation(acc[:, t, :], acc[:, t, :], ACT.Silu,
                                     bias=vec[:, V_NB + t:V_NB + t + 1], scale=vec[:, V_NG + t:V_NG + t + 1]
                                     ).then_inc(silu_done, 1)

            def branch_hi(k):
                act.wait_ge(gated, k + 1)
                nc.scalar.activation(g_hi[:, k, :], acc[:, k, :], ACT.Copy).then_inc(g_hi_ready, 1)

            SILU_AT = VAR_AT + 2
            for i in range(CT):
                z_split(i)
                if i == 0:
                    keep_value_gate(CT - 1, CT - 1)
                if i < 2:
                    conv_matrices(ROUNDS, i)
                if i == 2:
                    conv_input_hi(ROUNDS)
                if i == 3:
                    keep_conv(ROUNDS)
                if i >= 3:
                    keep_z(i - 3)
                if MEAN_AT + 2 <= i < MEAN_AT + 6:
                    for t in range(4 * (i - MEAN_AT - 2), 4 * (i - MEAN_AT - 2) + 4):
                        square(t)
                if i == VAR_AT + 1:
                    act.wait_ge(var_ready, 1)
                    nc.scalar.activation(std_a[:], var_a[:], ACT.Sqrt).then_inc(std_ready, 1)
                if i >= SILU_AT:
                    for t in range(3 * (i - SILU_AT), CT if i == CT - 1 else 3 * (i - SILU_AT) + 3):
                        branch_silu(t)
                if i > SILU_AT:
                    branch_hi(2 * (i - SILU_AT) - 2)
                    branch_hi(2 * (i - SILU_AT) - 1)
            for i in range(CT - 3, CT):
                keep_z(i)
            for k in range(CT):
                c = OUT0 + k
                split_hi(c, c % 2, c % SLOTS, landed_value(c))
                if k < CT - 8:
                    branch_hi(8 + k)
                if 3 <= k < 3 + RT:
                    r = k - 3
                    act.wait_ge(res_landed, 64)
                    nc.scalar.activation(res[:, r, :], res[:, r, :], ACT.Copy, scale=ALPHA
                                         ).then_inc(res_scaled, 1)
            if only_a:
                return

            act.wait_ge(g_lo_ready, CT)
            for q in range(2 * RT):
                r, half = q // 2, q % 2
                act.wait_ge(h_turned, q + 1)
                nc.scalar.activation(ht_hi[:, 4 * half:4 * half + 4, r * P:(r + 1) * P],
                                     bank[q][:].rearrange("p (k n) -> p k n", k=4), ACT.Copy
                                     ).then_inc(ht_hi_ready, 1)
                if q in (4, 5):
                    c = LAT0 + q - 4
                    split_hi(c, c % 2, c % SLOTS, landed_value(c))

            def keep_latent(n):
                act.wait_ge(w_used, LAT0 + n + 1)
                nc.scalar.activation(lat[:, n, :], bank[n % 4][:], ACT.Copy).then_inc(evacuated, 1)

            def keep_gate(i):
                act.wait_ge(w_used, BZ0 + i + 1)
                nc.scalar.activation(gate[:, i, :], bank[(LATENTS + i) % 4][:], ACT.Silu).then_inc(evacuated, 1)

            def latent_hi(m, out_ap, in_ap):
                act.wait_ge(lat_scaled, m + 1)
                nc.scalar.activation(out_ap, in_ap, ACT.Copy).then_inc(lat_hi_ready, 1)

            for n in range(2, LATENTS + N_HEADS):
                c = LAT0 + n
                if n >= SLOTS:
                    m = n - SLOTS
                    if m < LATENTS:
                        keep_latent(m)
                    else:
                        keep_gate(m - LATENTS)
                split_hi(c, c % 2, c % SLOTS, landed_value(c))
                if n == LATENTS + 7:
                    act.wait_ge(b_var_ready, 2)
                    nc.scalar.activation(b_std[:], b_var[:], ACT.Sqrt).then_inc(b_std_ready, 1)
                if n == LATENTS + 10:
                    for k in range(KV):
                        latent_hi(k, ckv_hi[:, k, :], lat[:, k, :])
                    latent_hi(KV, kr_hi[:], lat[:, KV, :])
                if n == LATENTS + 11:
                    for k in range(KQ):
                        latent_hi(KV + 1 + k, cq_hi[:, k, :], lat[:, KV + 1 + k, :])
            for i in range(N_HEADS - 4, N_HEADS):
                keep_gate(i)

            def split_bundle_hi(p, slot):
                act.wait_ge(bundle_landed, 96 * (p + 1))
                wait(act, proj_done, 7 * (p - 1))
                for lo, hi in BUNDLE_PARTS:
                    nc.scalar.activation(bundle_hi[slot][:, lo:hi], bundle_raw[:, lo:hi], ACT.Copy
                                         ).then_inc(bundle_hi_ready, 1)

            def keep_pair(p, slot):
                for half in range(2):
                    act.wait_ge(proj_done, 7 * p + half + 1)
                    nc.scalar.activation(v_hi[slot][:, 2 * half:2 * half + 2, :],
                                         bank[PROJ_BANK[half]][:].rearrange("p (t n) -> p t n", t=2), ACT.Copy
                                         ).then_inc(proj_hi_ready, 1)
                act.wait_ge(proj_done, 7 * p + 3)
                wait(act, qr_lo_ready, p)
                nc.scalar.activation(qr_raw[:], bank[PROJ_BANK[2]][:], ACT.Copy).then_inc(proj_hi_ready, 1)

            def keep_head(p, e):
                for n, tile in ((0, k_hi), (1, q_hi)):
                    act.wait_ge(proj_done, 7 * p + 3 + 2 * e + n + 1)
                    nc.scalar.activation(tile[e][:], bank[PROJ_BANK[3 + 2 * e + n]][:], ACT.Copy
                                         ).then_inc(proj_hi_ready, 1)

            def rotary_hi(p, slot):
                act.wait_ge(qr_rotated, p + 1)
                nc.scalar.activation(qr_hi[slot][:], qr_raw[:], ACT.Copy).then_inc(qr_hi_ready, 1)

            def exps(h):
                act.wait_ge(neg_top_ready, h + 1)
                for b in range(RT):
                    n = (b + 1) * P
                    block_ = prob[:, prob_at[b] * P:prob_at[b] * P + n]
                    nc.scalar.activation(block_, block_, ACT.Exp, bias=neg_top[:, b:b + 1], scale=SM_SCALE,
                                         accum_out=denom[:, b:b + 1]).then_inc(exp_done, 1)

            def transposed_hi(h):
                for b in range(RT):
                    act.wait_ge(prob_turned, RT * h + b + 1)
                    nc.scalar.activation(pt_hi[:, 0:b + 1, b * P:(b + 1) * P],
                                         bank[2 + b % 2][:, 0:(b + 1) * P].rearrange("p (k n) -> p k n", k=b + 1),
                                         ACT.Copy).then_inc(pt_hi_ready, 1)

            act.wait_ge(w_used, FIN0)
            split_bundle_hi(0, 0)
            split_bundle_hi(1, 1)
            keep_pair(0, 0)
            keep_head(0, 0)
            rotary_hi(0, 0)
            keep_head(0, 1)
            exps(0)
            keep_pair(1, 1)
            transposed_hi(0)

            def head(g, s):
                h = ROUND * g + s
                exps(h)
                if s % 2 == 1:
                    p = 2 * g + (s + 1) // 2
                    if not isinstance(p, int) or p < PAIRS:
                        rotary_hi(p, ((s + 1) // 2) % 2)
                        keep_head(p, 0)
                    transposed_hi(h)
                    if not isinstance(p, int) or p < PAIRS - 1:
                        split_bundle_hi(p + 1, ((s + 1) // 2 + 1) % 2)
                else:
                    keep_head(2 * g + s // 2, 1)
                    p = 2 * g + s // 2 + 1
                    if not isinstance(p, int) or p < PAIRS:
                        keep_pair(p, (s // 2 + 1) % 2)
                    transposed_hi(h)

            heads_loop(act, head)

            act.wait_ge(proj_done, 7 * PAIRS)
            for k in range(CT):
                c = FIN0 + k
                split_hi(c, c % 2, c % SLOTS, landed_value(c))
                act.wait_ge(gate_ready, k + 1)
                wait(act, w_used, c - SLOTS + 1)
                nc.scalar.activation(fg_hi[k % 4][:], gate[:, k, :], ACT.Copy).then_inc(g_hi_ready, 1)

        @block.vector
        def _(dve):
            nc.vector.memset(csum[:], 0.0).then_inc(sums_cleared, 1)
            nc.vector.memset(vsum[:], 0.0).then_inc(sums_cleared, 1)
            steps = [0]

            def chained(instruction):
                instruction.then_inc(table_step, 1)
                steps[0] += 1
                dve.wait_ge(table_step, steps[0])

            dve.wait_ge(small_landed, 16 * SMALL_DMAS)
            chained(nc.vector.tensor_copy(pos[:], pos_int[:]))
            chained(nc.vector.tensor_scalar(angle[:], pos[:], freq[:, 0:1], None, ALU.mult))
            chained(nc.vector.tensor_scalar(turns[:], angle[:], 1.0 / TWO_PI, ROUNDER, ALU.mult, ALU.add))
            chained(nc.vector.tensor_scalar(turns[:], turns[:], -ROUNDER, None, ALU.add))
            for part in (PI_A, PI_B, PI_C):
                chained(nc.vector.scalar_tensor_tensor(out=angle[:], in0=turns[:], scalar=-part, in1=angle[:],
                                                       op0=ALU.mult, op1=ALU.add))
            chained(nc.vector.tensor_scalar(angle_c[:], angle[:], 0.5 * np.pi, None, ALU.add))
            chained(nc.vector.tensor_scalar(turns[:], angle_c[:], PI_SAFE, -TWO_PI, ALU.is_gt, ALU.mult))
            chained(nc.vector.tensor_tensor(angle_c[:], angle_c[:], turns[:], ALU.add))
            chained(nc.vector.tensor_scalar(angle_c[:], angle_c[:], PI_SAFE, -PI_SAFE, ALU.min, ALU.max))
            chained(nc.vector.tensor_scalar(angle[:], angle[:], PI_SAFE, -PI_SAFE, ALU.min, ALU.max))
            nc.vector.tensor_scalar(angle[:], angle[:], freq[:, 1:2], None, ALU.mult).then_inc(angles_ready, 1)

            for q in range(2 * RT):
                r, half = q // 2, q % 2
                dve.wait_ge(xt_hi_ready, q + 1)
                cut = (slice(None), slice(4 * half, 4 * half + 4), slice(r * P, (r + 1) * P))
                nc.vector.tensor_tensor(xt_lo[cut], bank[q % 4][:].rearrange("p (k n) -> p k n", k=4),
                                        xt_hi[cut].bitcast(F32), ALU.subtract).then_inc(xt_lo_ready, 1)
                if q == 1:
                    dve.wait_ge(taps_hi_ready, 1)
                    nc.vector.tensor_copy(conv_w[:], bank[4][:, 0:CT * TAPS]).then_inc(taps_ready, 1)
                    nc.vector.tensor_tensor(conv_w_lo[:], bank[4][:, 0:CT * TAPS], conv_w_hi[:].bitcast(F32),
                                            ALU.subtract).then_inc(taps_lo_ready, 1)

            DVE_TILES = ROUND - 1

            def convolve(first, count, done):
                dve.wait_ge(u_ready, first + count)
                for k in range(TAPS):
                    for i in range(count):
                        t = first + i
                        shifted = u[:, bass.ds(t, 1), k:k + SEQ].rearrange("p o n -> p (o n)")
                        acc_t = acc[:, bass.ds(t, 1), :].rearrange("p o n -> p (o n)")
                        tap = conv_w[:, bass.ds(t * TAPS + k, 1)]
                        if k == 0:
                            nc.vector.tensor_scalar(acc_t, shifted, tap, vec[:, bass.ds(V_CONVB + t, 1)],
                                                    ALU.mult, ALU.add).then_inc(tap_done, 1)
                        else:
                            dve.wait_ge(tap_done, done + count * (k - 1) + i + 1)
                            nc.vector.scalar_tensor_tensor(out=acc_t, in0=shifted, scalar=tap, in1=acc_t,
                                                           op0=ALU.mult, op1=ALU.add).then_inc(tap_done, 1)

            def add_to_csum(t, n):
                wait(dve, csum_done, n)
                nc.vector.tensor_tensor(csum[:], csum[:], acc[:, bass.ds(t, 1), :].rearrange("p o n -> p (o n)"),
                                        ALU.add).then_inc(csum_done, 1)

            def convolve_round(j):
                convolve(ROUND * j, DVE_TILES, DVE_TILES * TAPS * j)
                for i in range(DVE_TILES):
                    dve.wait_ge(tap_done, DVE_TILES * TAPS * (j + 1) - DVE_TILES + i + 1)
                    add_to_csum(ROUND * j + i, ROUND * j - 1 + i)
                dve.wait_ge(pe_conv_kept, j)
                add_to_csum(ROUND * j - 1, ROUND * j - 1 + DVE_TILES)

            dve.wait_ge(sums_cleared, 2)
            dve.wait_ge(vec_ready, 1)
            dve.wait_ge(taps_ready, 1)
            dve.wait_ge(pad_ready, 1)
            dve.wait_ge(rope_ready, 2)
            convolve(0, 1, 0)
            convolve(1, DVE_TILES - 1, TAPS)
            dve.wait_ge(tap_done, DVE_TILES * TAPS)
            for i in range(DVE_TILES):
                add_to_csum(i, i)
            with dve.Fori(1, ROUNDS) as j:
                convolve_round(j)
            dve.wait_ge(pe_conv_kept, ROUNDS)
            add_to_csum(CT - 1, CT - 1)

            dve.wait_ge(mean_done, 1)
            for t in range(CT + 2):
                if t < CT:
                    nc.vector.scalar_tensor_tensor(out=acc[:, t, :], in0=bank[7][:], scalar=-1.0 / CONV_WIDTH,
                                                   in1=acc[:, t, :], op0=ALU.mult, op1=ALU.add
                                                   ).then_inc(centered, 1)
                if t >= 2:
                    dve.wait_ge(squared, t - 1)
                    wait(dve, vsum_done, t - 2)
                    nc.vector.tensor_tensor(vsum[:], vsum[:], sq[t % 2][:], ALU.add).then_inc(vsum_done, 1)

            stat_count = [0]

            def stat(instruction):
                instruction.then_inc(stat_step, 1)
                stat_count[0] += 1
                dve.wait_ge(stat_step, stat_count[0])

            def refined_rstd(var, std, t, rstd, ready):
                stat(nc.vector.reciprocal(rstd, std))
                stat(nc.vector.tensor_tensor(t, rstd, rstd, ALU.mult))
                stat(nc.vector.tensor_tensor(t, t, var, ALU.mult))
                stat(nc.vector.tensor_scalar(t, t, -0.5, 1.5, ALU.mult, ALU.add))
                nc.vector.tensor_tensor(rstd, rstd, t, ALU.mult).then_inc(ready, 1)

            dve.wait_ge(var_done, 1)
            nc.vector.tensor_scalar(var_a[:], bank[7][:], 1.0 / CONV_WIDTH, LN_EPS, ALU.mult, ALU.add
                                    ).then_inc(var_ready, 1)
            dve.wait_ge(std_ready, 1)
            refined_rstd(var_a[:], std_a[:], newton_a[:], rstd_a[:], rstd_ready)
            dve.wait_ge(rstd_ready, 1)
            dve.wait_ge(centered, CT)

            def gate_branch(t):
                dve.wait_ge(silu_done, t + 1)
                dve.wait_ge(evacuated, Z0 + t + 1)
                nc.vector.tensor_tensor(acc[:, t, :], acc[:, t, :], z_a[:, t, :], ALU.mult).then_inc(gated, 1)

            def branch_lo(t):
                dve.wait_ge(g_hi_ready, t + 1)
                nc.vector.tensor_tensor(g_lo[:, t, :], acc[:, t, :], g_hi[:, t, :].bitcast(F32), ALU.subtract
                                        ).then_inc(g_lo_ready, 1)

            for t in range(CT + 12):
                if t < CT:
                    nc.vector.tensor_tensor(acc[:, t, :], acc[:, t, :], rstd_a[:], ALU.mult).then_inc(scaled, 1)
                if 3 <= t < CT + 3:
                    gate_branch(t - 3)
                if t >= 12:
                    branch_lo(t - 12)

            def row_norm(n, r, rows, scale):
                dve.wait_ge(y_done, n + 1)
                for half in range(HALVES):
                    cut = res[:, r, half * BANK:(half + 1) * BANK]
                    nc.vector.scalar_tensor_tensor(out=cut, in0=cut, scalar=scale, in1=bank[2 * r + half][:],
                                                   op0=ALU.mult, op1=ALU.add).then_inc(y_step, 1)
                wait(dve, row_scaled, n)
                for half in range(HALVES):
                    dve.wait_ge(y_step, 5 * n + half + 1)
                    nc.vector.bn_stats(bn[:, half, :], res[:, r, half * BANK:(half + 1) * BANK]
                                       ).then_inc(y_step, 1)
                dve.wait_ge(y_step, 5 * n + 4)
                nc.vector.bn_aggr(mean_var[:], bn[:].rearrange("p a b -> p (a b)")).then_inc(var_row_ready, 1)
                dve.wait_ge(rstd_row_ready, n + 1)
                nc.vector.tensor_scalar(res[:, r, :], res[:, r, :], mean_var[:, 0:1], rstd_row[:, 1:2],
                                        ALU.subtract, ALU.mult).then_inc(y_step, 1)
                dve.wait_ge(y_step, 5 * n + 5)
                nc.vector.tensor_tensor(res[:, r, :], res[:, r, :], rows[:, 0, :], ALU.mult
                                        ).then_inc(row_scaled, 1)

            def turned_lo(q):
                r, half = q // 2, q % 2
                cut = (slice(None), slice(4 * half, 4 * half + 4), slice(r * P, (r + 1) * P))
                dve.wait_ge(ht_hi_ready, q + 1)
                nc.vector.tensor_tensor(ht_lo[cut], bank[q][:].rearrange("p (k n) -> p k n", k=4),
                                        ht_hi[cut].bitcast(F32), ALU.subtract).then_inc(ht_lo_ready, 1)

            dve.wait_ge(res_ready, RT)
            for r in range(RT):
                row_norm(r, r, ln_rows, 1.0)
                if r > 0 and not only_a:
                    turned_lo(2 * r - 2)
                    turned_lo(2 * r - 1)
            if only_a:
                return
            turned_lo(2 * RT - 2)
            turned_lo(2 * RT - 1)

            bcount = [0]

            def b_next(instruction):
                instruction.then_inc(b_step, 1)
                bcount[0] += 1
                dve.wait_ge(b_step, bcount[0])

            dve.wait_ge(row_ready, RT)
            for which, tiles in ((0, range(KV)), (1, range(KV + 1, LATENTS))):
                for m in tiles:
                    dve.wait_ge(evacuated, OUT0 + m + 1)
                    if m == tiles[0]:
                        b_next(nc.vector.tensor_tensor(b_sum[:, which, :], lat[:, m, :], lat[:, m, :], ALU.mult))
                    else:
                        b_next(nc.vector.tensor_tensor(b_sq[:], lat[:, m, :], lat[:, m, :], ALU.mult))
                        b_next(nc.vector.tensor_tensor(b_sum[:, which, :], b_sum[:, which, :], b_sq[:], ALU.add))
            dve.wait_ge(k_swapped, 64)
            dve.wait_ge(rope_ready, 2)
            b_next(nc.vector.tensor_tensor(lat[:, KV, :], lat[:, KV, :], cos[:], ALU.mult))
            b_next(nc.vector.tensor_tensor(k_swap[:], k_swap[:], sin[:], ALU.mult))
            for which, rank in ((0, KV_RANK), (1, Q_RANK)):
                dve.wait_ge(b_sum_done, which + 1)
                nc.vector.tensor_scalar(b_var[:, which, :], bank[4 + which][:], 1.0 / rank, RMS_EPS,
                                        ALU.mult, ALU.add).then_inc(b_var_ready, 1)
            dve.wait_ge(b_std_ready, 1)
            dve.wait_ge(b_var_ready, 2)
            for which in range(2):
                refined_rstd(b_var[:, which, :], b_std[:, which, :], b_newton[:], b_rstd[:, which, :], b_rstd_ready)
                dve.wait_ge(b_rstd_ready, which + 1)
            for m in range(LATENTS):
                if m == KV:
                    nc.vector.tensor_tensor(lat[:, KV, :], lat[:, KV, :], k_swap[:], ALU.add).then_inc(lat_scaled, 1)
                    continue
                gain = V_KVG + m if m < KV else V_QG + m - KV - 1
                nc.vector.scalar_tensor_tensor(out=lat[:, m, :], in0=lat[:, m, :], scalar=vec[:, gain:gain + 1],
                                               in1=b_rstd[:, 0 if m < KV else 1, :], op0=ALU.mult, op1=ALU.mult
                                               ).then_inc(lat_scaled, 1)
            for m in range(LATENTS):
                dve.wait_ge(lat_hi_ready, m + 1)
                hi, lo = ((ckv_hi[:, m, :], ckv_lo[:, m, :]) if m < KV else (kr_hi[:], kr_lo[:]) if m == KV
                          else (cq_hi[:, m - KV - 1, :], cq_lo[:, m - KV - 1, :]))
                nc.vector.tensor_tensor(lo, lat[:, m, :], hi.bitcast(F32), ALU.subtract).then_inc(lat_lo_ready, 1)

            def mask_scores(h):
                for b in range(RT):
                    n = (b + 1) * P
                    dve.wait_ge(scores_done, RT * h + b + 1)
                    nc.vector.memset(waited[:, b:b + 1], 0.0)
                    nc.vector.tensor_tensor_reduce(prob[:, prob_at[b] * P:prob_at[b] * P + n], bank[b % 2][:, 0:n],
                                                   mask[:, SEQ - n:SEQ], 1.0, MAX_START, ALU.add, ALU.max,
                                                   top[:, b:b + 1]).then_inc(masked, 1)
                dve.wait_ge(masked, RT * h + RT)
                nc.vector.tensor_scalar(neg_top[:], top[:], -SM_SCALE, None, ALU.mult).then_inc(neg_top_ready, 1)

            def normalise(h):
                dve.wait_ge(exp_done, RT * (h + 1))
                nc.vector.reciprocal(inv_denom[:], denom[:]).then_inc(inv_ready, 1)
                dve.wait_ge(inv_ready, h + 1)
                for b in range(RT):
                    block_ = prob[:, prob_at[b] * P:(prob_at[b] + b + 1) * P]
                    nc.vector.tensor_scalar(block_, block_, inv_denom[:, b:b + 1], None, ALU.mult
                                            ).then_inc(prob_ready, 1)

            def pair_lo(p, slot):
                for half in range(2):
                    dve.wait_ge(proj_hi_ready, 7 * p + half + 1)
                    cut = (slice(None), slice(2 * half, 2 * half + 2), slice(None))
                    nc.vector.tensor_tensor(v_lo[slot][cut], bank[PROJ_BANK[half]][:].rearrange("p (t n) -> p t n", t=2),
                                            v_hi[slot][cut].bitcast(F32), ALU.subtract).then_inc(proj_lo_ready, 1)

            def head_lo(p, e):
                for n, (hi, lo) in enumerate(((k_hi, k_lo), (q_hi, q_lo))):
                    dve.wait_ge(proj_hi_ready, 7 * p + 3 + 2 * e + n + 1)
                    nc.vector.tensor_tensor(lo[e][:], bank[PROJ_BANK[3 + 2 * e + n]][:], hi[e][:].bitcast(F32),
                                            ALU.subtract).then_inc(proj_lo_ready, 1)

            def transposed_lo(h):
                for b in range(RT):
                    dve.wait_ge(pt_hi_ready, RT * h + b + 1)
                    cut = (slice(None), slice(0, b + 1), slice(b * P, (b + 1) * P))
                    nc.vector.tensor_tensor(pt_lo[cut], bank[2 + b % 2][:, 0:(b + 1) * P].rearrange(
                        "p (k n) -> p k n", k=b + 1), pt_hi[cut].bitcast(F32), ALU.subtract
                    ).then_inc(pt_lo_ready, 1)

            def gate_head(h):
                dve.wait_ge(pv_done, h + 1)
                tile = gate[:, bass.ds(h, 1), :].rearrange("p o n -> p (o n)")
                nc.vector.tensor_tensor(tile, bank[4][:], tile, ALU.mult).then_inc(gate_ready, 1)

            dve.wait_ge(consts_ready, 6)
            dve.wait_ge(w_used, FIN0)
            pair_lo(0, 0)
            head_lo(0, 0)
            head_lo(0, 1)
            mask_scores(0)
            normalise(0)
            pair_lo(1, 1)
            transposed_lo(0)

            def head(g, s):
                h = ROUND * g + s
                mask_scores(h)
                gate_head(h - 1)
                normalise(h)
                if s % 2 == 1:
                    p = 2 * g + (s + 1) // 2
                    if not isinstance(p, int) or p < PAIRS:
                        head_lo(p, 0)
                else:
                    head_lo(2 * g + s // 2, 1)
                    p = 2 * g + s // 2 + 1
                    if not isinstance(p, int) or p < PAIRS:
                        pair_lo(p, (s // 2 + 1) % 2)
                transposed_lo(h)

            dve.wait_ge(evacuated, OUT0 + LATENTS + N_HEADS)
            heads_loop(dve, head)
            gate_head(N_HEADS - 1)

            for k in range(CT):
                dve.wait_ge(g_hi_ready, CT + k + 1)
                nc.vector.tensor_tensor(fg_lo[k % 4][:], gate[:, k, :], fg_hi[k % 4][:].bitcast(F32), ALU.subtract
                                        ).then_inc(g_lo_ready, 1)
            dve.wait_ge(ln_rows_landed, 32)
            for r in range(RT):
                row_norm(RT + r, r, ln_rows_b, ALPHA)

        @block.tensor
        def _(pe):
            def product(out_ap, parts, start, stop):
                last = None
                for n, (s_hi, s_lo, m_hi, m_lo) in enumerate(parts):
                    for m, (a, b) in enumerate(((s_lo, m_hi), (s_hi, m_lo), (s_hi, m_hi))):
                        last = nc.tensor.matmul(out_ap, a, b, start=(start and n == 0 and m == 0),
                                                stop=(stop and n == len(parts) - 1 and m == 2))
                return last

            pe.wait_ge(consts_ready, 6)
            for r in range(RT):
                pe.wait_ge(x_landed[r], 16)
                for half in range(2):
                    q = 2 * r + half
                    wait(pe, xt_lo_ready, q - 3)
                    for k in range(4):
                        last = nc.tensor.transpose(bank[q % 4][:, k * P:(k + 1) * P],
                                                   x_in[:, r, (4 * half + k) * P:(4 * half + k + 1) * P], ident[:])
                    last.then_inc(x_turned, 1)
                if r == 0:
                    pe.wait_ge(small_landed, 16 * SMALL_DMAS)
                    for t in range(CT):
                        last = nc.tensor.transpose(bank[4][:, t * TAPS:(t + 1) * TAPS],
                                                   taps_raw[:, t * P:(t + 1) * P], ident[0:TAPS, 0:TAPS])
                    last.then_inc(taps_turned, 1)
                    nc.tensor.transpose(bank[5][:, 0:V_ALL], vec_raw[:], ident[0:V_ALL, 0:V_ALL]
                                        ).then_inc(vec_turned, 1)

            def columns(c, slot, out_bank, bank_free, hi, lo):
                pe.wait_ge(w_hi_ready, c + 1)
                pe.wait_ge(w_lo_ready, c + 1)
                wait(pe, evacuated, bank_free)
                parts = [(w_hi[slot][:, k * P:(k + 1) * P], w_lo[slot][:, k * P:(k + 1) * P],
                          hi[:, k, :], lo[:, k, :]) for k in range(KD)]
                product(bank[out_bank][:], parts, True, True).then_inc(w_used, 1)

            def value_gate(j):
                for s in range(ROUND):
                    for w in range(2):
                        c = 2 * ROUND * j + 2 * s + w
                        columns(c, (2 * s + w) % SLOTS, (2 * s + w) % 4, c - 3, xt_hi, xt_lo)
                    if s == 2 and (not isinstance(j, int) or j > 0):
                        convolve(j)

            def convolve(j):
                pe.wait_ge(diag_hi_ready, 2 * j)
                pe.wait_ge(diag_lo_ready, TAPS * j)
                pe.wait_ge(cu_lo_ready, j)
                pe.wait_ge(evacuated, 2 * ROUND * j)
                parts = [(diag_hi[:, k, :], diag_lo[:, k, :], cu_hi[:, k:k + SEQ], cu_lo[:, k:k + SEQ])
                         for k in range(TAPS)]
                product(bank[6][:], parts, True, True).then_inc(pe_conv_done, 1)

            pe.wait_ge(xt_lo_ready, 2 * RT)
            value_gate(0)
            with pe.Fori(1, ROUNDS) as j:
                value_gate(j)

            for i in range(CT):
                if i == 3:
                    convolve(ROUNDS)
                if i == MEAN_AT:
                    pe.wait_ge(csum_done, CT)
                    nc.tensor.matmul(bank[7][:], ones[:], csum[:], start=True, stop=True).then_inc(mean_done, 1)
                if i == VAR_AT:
                    pe.wait_ge(vsum_done, CT)
                    nc.tensor.matmul(bank[7][:], ones[:], vsum[:], start=True, stop=True).then_inc(var_done, 1)
                columns(Z0 + i, i % SLOTS, i % 4, Z0 + i - 3, xt_hi, xt_lo)

            def output_projection(c0, hi, lo, ring, banks_free):
                def tile(k, r):
                    c = c0 + k
                    cut = slice(r * P, (r + 1) * P)
                    for half in range(HALVES):
                        cols = slice(half * BANK, (half + 1) * BANK)
                        last = product(bank[2 * r + half][:],
                                       [(hi(k)[:, cut], lo(k)[:, cut], w_hi[c % SLOTS][:, cols], w_lo[c % SLOTS][:, cols])],
                                       k == 0, k == CT - 1)
                    return last

                def arrive(k):
                    pe.wait_ge(w_hi_ready, c0 + k + 1)
                    pe.wait_ge(w_lo_ready, c0 + k + 1)
                    pe.wait_ge(g_lo_ready, ring * CT + k + 1)

                for k in range(CT - RESIDENT):
                    arrive(k)
                    for r in range(RT):
                        if k == 0 and r in banks_free:
                            pe.wait_ge(*banks_free[r])
                        last = tile(k, r)
                    last.then_inc(w_used, 1)
                for r in range(RT):
                    for k in range(CT - RESIDENT, CT):
                        if r == 0:
                            arrive(k)
                        last = tile(k, r)
                        if r == RT - 1 and k < CT - 1:
                            last.then_inc(w_used, 1)
                    last.then_inc(y_done, 1)

            output_projection(OUT0, lambda k: g_hi[:, k, :], lambda k: g_lo[:, k, :], 0,
                              {0: (evacuated, OUT0 - 2), 1: (evacuated, OUT0), 3: (var_ready, 1)})
            if only_a:
                return

            for q in range(2 * RT):
                r, half = q // 2, q % 2
                pe.wait_ge(row_ready, r + 1)
                for k in range(4):
                    last = nc.tensor.transpose(bank[q][:, k * P:(k + 1) * P],
                                               res[:, r, (4 * half + k) * P:(4 * half + k + 1) * P], ident[:])
                    if q == k == 0:
                        last.then_inc(w_used, 1)
                last.then_inc(h_turned, 1)
            pe.wait_ge(ht_lo_ready, 2 * RT)

            for n in range(LATENTS):
                c = LAT0 + n
                columns(c, c % SLOTS, n % 4, OUT0 + n - 3 if n >= 4 else 0, ht_hi, ht_lo)

            def gate_round(j):
                for s in range(ROUND):
                    c = BZ0 + ROUND * j + s
                    columns(c, (BZ0 + s) % SLOTS, (LATENTS + s) % 4,
                            OUT0 + LATENTS + ROUND * j + s - 3, ht_hi, ht_lo)

            gate_round(0)
            for which in range(2):
                pe.wait_ge(b_step, SQUARE_STEPS[which])
                nc.tensor.matmul(bank[4 + which][:], ones[:], b_sum[:, which, :], start=True, stop=True
                                 ).then_inc(b_sum_done, 1)
            with pe.Fori(1, ROUNDS) as j:
                gate_round(j)

            def project_pair(p, slot):
                bh, bl = bundle_hi[slot], bundle_lo[slot]
                pe.wait_ge(bundle_lo_ready, 2 * p + 1)
                cols = [slice(UV + k * 2 * V_DIM, UV + (k + 1) * 2 * V_DIM) for k in range(KV)]
                for half in range(2):
                    wait(pe, proj_lo_ready, 6 * p - 3 if half == 0 else 6 * p - 1)
                    for t in range(2):
                        cut = slice((2 * half + t) * P, (2 * half + t + 1) * P)
                        last = product(bank[PROJ_BANK[half]][:, t * 2 * V_DIM:(t + 1) * 2 * V_DIM],
                                       [(ckv_hi[:, k, cut], ckv_lo[:, k, cut], bh[:, cols[k]], bl[:, cols[k]])
                                        for k in range(KV)], True, True)
                    last.then_inc(proj_done, 1)
                wait(pe, proj_lo_ready, 6 * p)
                cols = [slice(QR + k * 2 * ROPE, QR + (k + 1) * 2 * ROPE) for k in range(KQ)]
                product(bank[PROJ_BANK[2]][:], [(bh[:, cols[k]], bl[:, cols[k]], cq_hi[:, k, :], cq_lo[:, k, :])
                                                for k in range(KQ)], True, True).then_inc(proj_done, 1)

            def project_head(p, e, slot):
                bh, bl = bundle_hi[slot], bundle_lo[slot]
                pe.wait_ge(bundle_lo_ready, 2 * p + 2)
                pe.wait_ge(proj_lo_ready, 6 * p + (1 if e == 0 else 4))
                cols = [slice(UK + k * 2 * NOPE + e * NOPE, UK + k * 2 * NOPE + (e + 1) * NOPE) for k in range(KV)]
                product(bank[PROJ_BANK[3 + 2 * e]][:],
                        [(bh[:, cols[k]], bl[:, cols[k]], ckv_hi[:, k, :], ckv_lo[:, k, :]) for k in range(KV)],
                        True, True).then_inc(proj_done, 1)
                if e == 0:
                    pe.wait_ge(proj_lo_ready, 6 * p + 2)
                else:
                    pe.wait_ge(proj_hi_ready, 7 * p + 3)
                cols = [slice(QN + k * 2 * NOPE + e * NOPE, QN + k * 2 * NOPE + (e + 1) * NOPE) for k in range(KQ)]
                product(bank[PROJ_BANK[4 + 2 * e]][:],
                        [(bh[:, cols[k]], bl[:, cols[k]], cq_hi[:, k, :], cq_lo[:, k, :]) for k in range(KQ)],
                        True, True).then_inc(proj_done, 1)

            def scores(h, p, e, slot):
                pe.wait_ge(proj_lo_ready, 6 * p + 4 + 2 * e)
                pe.wait_ge(qr_lo_ready, p + 1)
                half = slice(e * ROPE, (e + 1) * ROPE)
                for b in range(RT):
                    n = (b + 1) * P
                    cut = slice(b * P, n)
                    wait(pe, masked, RT * h + b - 1)
                    product(bank[b % 2][:, 0:n],
                            [(q_hi[e][:, cut], q_lo[e][:, cut], k_hi[e][:, 0:n], k_lo[e][:, 0:n]),
                             (qr_hi[slot][half, cut], qr_lo[slot][half, cut], kr_hi[half, 0:n], kr_lo[half, 0:n])],
                            True, True).then_inc(scores_done, 1)

            def turn(h):
                for b in range(RT):
                    pe.wait_ge(prob_ready, RT * h + b + 1)
                    wait(pe, pt_lo_ready, RT * h + b - 1)
                    for k in range(b + 1):
                        last = nc.tensor.transpose(bank[2 + b % 2][:, k * P:(k + 1) * P],
                                                   prob[:, (prob_at[b] + k) * P:(prob_at[b] + k + 1) * P], ident[:])
                    last.then_inc(prob_turned, 1)

            def attend(h, e, slot):
                pe.wait_ge(pt_lo_ready, RT * (h + 1))
                wait(pe, gate_ready, h)
                cols = slice(e * V_DIM, (e + 1) * V_DIM)
                for k in range(RT):
                    last = product(bank[4][:, k * P:], [(v_hi[slot][:, k, cols], v_lo[slot][:, k, cols],
                                                        pt_hi[:, k, k * P:], pt_lo[:, k, k * P:])],
                                   k == 0, k == RT - 1)
                last.then_inc(pv_done, 1)

            pe.wait_ge(lat_lo_ready, LATENTS)
            pe.wait_ge(b_var_ready, 2)
            pe.wait_ge(evacuated, OUT0 + LATENTS + N_HEADS)
            project_pair(0, 0)
            project_head(0, 0, 0)
            project_head(0, 1, 0)
            scores(0, 0, 0, 0)
            project_pair(1, 1)
            turn(0)

            def head(g, s):
                h = ROUND * g + s
                scores(h, 2 * g + s // 2, s % 2, (s // 2) % 2)
                attend(h - 1, (s - 1) % 2, ((s - 1) // 2) % 2)
                if s % 2 == 1:
                    p = 2 * g + (s + 1) // 2
                    if not isinstance(p, int) or p < PAIRS:
                        project_head(p, 0, ((s + 1) // 2) % 2)
                else:
                    project_head(2 * g + s // 2, 1, (s // 2) % 2)
                    p = 2 * g + s // 2 + 1
                    if not isinstance(p, int) or p < PAIRS:
                        project_pair(p, (s // 2 + 1) % 2)
                turn(h)

            heads_loop(pe, head)
            attend(N_HEADS - 1, (N_HEADS - 1) % 2, ((N_HEADS - 1) // 2) % 2)
            output_projection(FIN0, lambda k: fg_hi[k % 4], lambda k: fg_lo[k % 4], 1,
                              {2: (gate_ready, N_HEADS)})


INPUTS = ["x", "positions", "ln_g", "ln_b", "a_w_in", "a_b_in", "a_conv_w", "a_conv_b", "a_norm_g",
          "a_norm_b", "a_w_out", "a_b_out", "kv_w_down", "kv_norm_g", "kv_w_uk", "kv_w_uv", "b_w_in",
          "b_q_norm_g", "b_w_uq", "b_w_out"]


def kernel(**inputs):
    import numpy as _np
    import concourse.bacc as _bacc
    from concourse import mybir as _mybir
    from concourse.bass_utils import run_bass_kernel_spmd as _run

    nc = _bacc.Bacc("TRN2", target_bir_lowering=False, num_devices=1)
    arrays = {f"in_{name}_dram": _np.ascontiguousarray(inputs[name]) for name in INPUTS}
    pair = _np.arange(0, ROPE, 2, dtype=_np.float32) / _np.float32(ROPE)
    table = _np.ones((P, 2), _np.float32)
    table[:, 0] = _np.tile(_np.power(_np.float32(ROPE_THETA), -pair), 4)
    table[:, 1] = _np.tile(_np.repeat(_np.array([-1.0, 1.0], _np.float32), ROPE // 2), 2)
    arrays["in_rope_freq_dram"] = table
    args = [nc.dram_tensor(name, a.shape, _mybir.dt.from_np(a.dtype), kind="ExternalInput").ap()
            for name, a in arrays.items()]
    args.append(nc.dram_tensor("out_0_dram", (1, SEQ, D_MODEL), _mybir.dt.float32, kind="ExternalOutput").ap())
    trunk_kernel(nc, *args)
    return _run(nc, [arrays], core_ids=[0]).results[0]["out_0_dram"]
```

```python
from contextlib import ExitStack

import numpy as np

import concourse.bass as bass
from concourse import mybir

F32 = mybir.dt.float32
F32R = mybir.dt.float32r
I32 = mybir.dt.int32
ALU = mybir.AluOpType
ACT = mybir.ActivationFunctionType

P = 128
BANK = 512
DEPTH = 2
D_MODEL = 1024
SEQ = 512
CONV_WIDTH = 2 * D_MODEL
TAPS = 31
PAD = TAPS - 1
N_HEADS = 16
NOPE = 128
ROPE = 64
V_DIM = 128
KV_RANK = D_MODEL // 4
Q_RANK = D_MODEL // 2
ALPHA = (2.0 * DEPTH) ** 0.25
LN_EPS = 1e-5
RMS_EPS = 1e-6
MASK_VALUE = -1e30
MAX_START = -3e38
SM_SCALE = float((NOPE + ROPE) ** -0.5)
ROPE_THETA = 10000.0

KD = D_MODEL // P
CT = CONV_WIDTH // P
RT = SEQ // P
KQ = Q_RANK // P
KV = KV_RANK // P
PAIRS = N_HEADS // 2
HALVES = D_MODEL // BANK

ROUND = 4
ROUNDS = CT // ROUND

CHUNK = KD * P
Z0 = 2 * CT
OUT0 = Z0 + CT
LAT0 = OUT0 + CT
LATENTS = KV + 1 + KQ
ROPE_CHUNK = LAT0 + KV
BZ0 = LAT0 + LATENTS
FIN0 = BZ0 + N_HEADS
RAW_SLOTS = 2
SLOTS = 4
RESIDENT = SLOTS

UV = 0
QR = UV + KV * 2 * V_DIM
UK = QR + KQ * 2 * ROPE
QN = UK + KV * 2 * NOPE
BUNDLE = QN + KQ * 2 * NOPE
BUNDLE_PARTS = ((UV, UK), (UK, BUNDLE))

V_BIN = 0
V_CONVB = V_BIN + 3 * CT
V_NG = V_CONVB + CT
V_NB = V_NG + CT
V_KVG = V_NB + CT
V_QG = V_KVG + KV
V_ALL = V_QG + KQ

TWO_PI = 2.0 * np.pi
PI_A = 6.28125
PI_B = float(np.float32(np.floor((TWO_PI - PI_A) * 2.0 ** 20) / 2.0 ** 20))
PI_C = float(np.float32(TWO_PI - PI_A - PI_B))
ROUNDER = 1.5 * 2.0 ** 23
PI_SAFE = 3.1415925


def wait(eng, semaphore, value):
    if not isinstance(value, int) or value > 0:
        eng.wait_ge(semaphore, value)


def trunk_kernel(nc, x, positions, ln_g, ln_b, a_w_in, a_b_in, a_conv_w, a_conv_b, a_norm_g,
                 a_norm_b, a_w_out, a_b_out, kv_w_down, kv_norm_g, kv_w_uk, kv_w_uv, b_w_in,
                 b_q_norm_g, b_w_uq, b_w_out, rope_freq, out):
    x_rows = x.rearrange("b (r p) d -> p (b r) d", p=P)
    out_rows = out.rearrange("b (r p) d -> p (b r) d", p=P)
    w_in_a = a_w_in.rearrange("a (k p) n -> p (a k) n", p=P)
    w_out_a = a_w_out.rearrange("a (k p) n -> (a k) p n", p=P)
    w_down = kv_w_down.rearrange("(k p) n -> p k n", p=P)
    w_in_b = b_w_in.rearrange("a (k p) n -> p (a k) n", p=P)
    w_out_b = b_w_out.rearrange("a (k p) n -> (a k) p n", p=P)
    w_uk = kv_w_uk.rearrange("(k p) h d -> p k (h d)", p=P)
    w_uv = kv_w_uv.rearrange("(k p) h d -> p k (h d)", p=P)
    w_uq = b_w_uq.rearrange("a (k p) h d -> p (a k) h d", p=P)

    with ExitStack() as ctx:
        def sem(name):
            return ctx.enter_context(nc.semaphore(name))

        place = [-(-nc.sbuf_base // 32) * 32]

        def region(words):
            at = place[0]
            place[0] = at + -(-words * 4 // 32) * 32
            assert place[0] <= nc.sbuf_usable_end
            return at

        def at(name, base, offset_words, shape, dtype=F32):
            return nc.alloc_sbuf_tensor_at(name, shape, dtype, offset=base + 4 * offset_words)

        def own(name, shape, dtype=F32):
            words = 1
            for n in shape[1:]:
                words *= n
            return at(name, region(words), 0, shape, dtype)

        TILE = SEQ
        reg_x = region(8 * TILE)
        reg_xt = region(16 * TILE)
        reg_u = region(CT * (SEQ + PAD))
        reg_acc = region(CT * TILE)
        reg_z = region(CT * TILE)
        reg_w = region((RAW_SLOTS + 2 * SLOTS) * CHUNK)
        reg_e = region(4 * TILE)

        ident = own("ident", [P, P])
        ones = own("ones", [P, P])
        conv_w = own("conv_w", [P, CT * TAPS])
        conv_w_hi = own("conv_w_hi", [P, CT * TAPS], F32R)
        conv_w_lo = own("conv_w_lo", [P, CT * TAPS], F32R)
        vec = own("vec", [P, V_ALL])
        cos = own("cos", [P, SEQ])
        sin = own("sin", [P, SEQ])
        mask = own("mask", [P, SEQ])
        freq = own("freq", [P, 2])
        bn = own("bn", [P, RT, HALVES, 6])
        mean_var = own("mean_var", [P, RT, 2])
        rstd_row = own("rstd_row", [P, RT, 2])
        var_cols = own("var_cols", [P, RT])
        rstd_cols = own("rstd_cols", [P, RT])
        minus_half = own("minus_half", [P, RT])
        top = own("top", [P, RT])
        neg_top = own("neg_top", [P, RT])
        denom = own("denom", [P, RT])
        waited = own("waited", [P, RT])
        inv_denom = own("inv_denom", [P, RT])

        w_raw = [at(f"w_raw{i}", reg_w, i * CHUNK, [P, CHUNK]) for i in range(RAW_SLOTS)]
        w_hi = [at(f"w_hi{i}", reg_w, (RAW_SLOTS + i) * CHUNK, [P, CHUNK], F32R) for i in range(SLOTS)]
        w_lo = [at(f"w_lo{i}", reg_w, (RAW_SLOTS + SLOTS + i) * CHUNK, [P, CHUNK], F32R)
                for i in range(SLOTS)]

        x_in = at("x_in", reg_x, 0, [P, RT, D_MODEL])
        val = [at(f"val{i}", reg_x, i * TILE, [P, SEQ]) for i in range(2)]
        sig = [at(f"sig{i}", reg_x, (2 + i) * TILE, [P, SEQ]) for i in range(2)]
        cu_hi = at("cu_hi", reg_x, 4 * TILE, [P, SEQ + PAD], F32R)
        cu_lo = at("cu_lo", reg_x, 4 * TILE + 544, [P, SEQ + PAD], F32R)
        sq = [at(f"sq{i}", reg_x, place * TILE, [P, SEQ]) for i, place in enumerate((0, 1, 4, 5))]
        rstd_diag = at("rstd_diag", reg_x, 2 * TILE, [P, SEQ])
        rstd_a = at("rstd_a", reg_x, 3 * TILE, [P, SEQ])
        xt_hi = at("xt_hi", reg_xt, 0, [P, KD, SEQ], F32R)
        xt_lo = at("xt_lo", reg_xt, KD * SEQ, [P, KD, SEQ], F32R)
        u = at("u", reg_u, 0, [P, CT, SEQ + PAD])
        taps_raw = at("taps_raw", reg_acc, 0, [TAPS, CONV_WIDTH])
        vec_raw = at("vec_raw", reg_acc, 4 * TILE, [V_ALL, P])
        pos_int = at("pos_int", reg_acc, 5 * TILE, [P, SEQ], I32)
        pos = at("pos", reg_acc, 6 * TILE, [P, SEQ])
        angle = at("angle", reg_acc, 7 * TILE, [P, SEQ])
        turns = at("turns", reg_acc, 8 * TILE, [P, SEQ])
        angle_c = at("angle_c", reg_acc, 9 * TILE, [P, SEQ])
        acc = at("acc", reg_acc, 0, [P, CT, SEQ])
        diag_hi = at("diag_hi", reg_z, 0, [P, TAPS, P], F32R)
        diag_lo = at("diag_lo", reg_z, TAPS * P, [P, TAPS, P], F32R)
        z_a = at("z_a", reg_z, 0, [P, CT, SEQ])
        g_hi = at("g_hi", reg_u, 0, [P, CT, SEQ], F32R)
        g_lo = at("g_lo", reg_z, 0, [P, CT, SEQ], F32R)
        csum = at("csum", reg_e, 0, [P, SEQ])
        vsum = at("vsum", reg_e, TILE, [P, SEQ])
        vsum_odd = at("vsum_odd", reg_e, 2 * TILE, [P, SEQ])
        tap_product = [at(f"tap_product{i}", reg_e, (2 + i) * TILE, [P, SEQ]) for i in range(2)]

        res = at("res", reg_xt, 0, [P, RT, D_MODEL])
        ln_rows = at("ln_rows", reg_xt, 8 * TILE, [P, 3, D_MODEL])
        ln_rows_b = at("ln_rows_b", reg_x, 0, [P, 2, D_MODEL])

        ht_hi = at("ht_hi", reg_acc, 0, [P, KD, SEQ], F32R)
        ht_copy = at("ht_copy", reg_x, 4 * TILE, [P, RT, SEQ])
        ht_lo = at("ht_lo", reg_acc, KD * SEQ, [P, KD, SEQ], F32R)
        lat = at("lat", reg_x, 0, [P, LATENTS, SEQ])
        k_swap = at("k_swap", reg_x, LATENTS * TILE, [P, SEQ])
        b_sq = at("b_sq", reg_xt, 8 * TILE, [P, SEQ])
        b_sum = at("b_sum", reg_xt, 9 * TILE, [P, 2, SEQ])
        b_var = at("b_var", reg_xt, 11 * TILE, [P, 2, SEQ])
        b_std = at("b_std", reg_xt, 13 * TILE, [P, 2, SEQ])
        b_newton = at("b_newton", reg_xt, 15 * TILE, [P, SEQ])
        b_rstd = at("b_rstd", reg_e, 0, [P, 2, SEQ])
        cq_hi = at("cq_hi", reg_u, 0, [P, KQ, SEQ], F32R)
        cq_lo = at("cq_lo", reg_u, 4 * TILE, [P, KQ, SEQ], F32R)
        ckv_hi = at("ckv_hi", reg_u, 8 * TILE, [P, KV, SEQ], F32R)
        ckv_lo = at("ckv_lo", reg_u, 10 * TILE, [P, KV, SEQ], F32R)
        kr_hi = at("kr_hi", reg_u, 12 * TILE, [P, SEQ], F32R)
        kr_lo = at("kr_lo", reg_u, 13 * TILE, [P, SEQ], F32R)
        qr_raw = at("qr_raw", reg_u, 14 * TILE, [P, SEQ])
        qr_swap = at("qr_swap", reg_u, 15 * TILE, [P, SEQ])
        gate = at("gate", reg_z, 0, [P, N_HEADS, SEQ])
        k_hi = [at(f"k_hi{i}", reg_acc, (0 + i) * TILE, [P, SEQ], F32R) for i in range(2)]
        k_lo = [at(f"k_lo{i}", reg_acc, (2 + i) * TILE, [P, SEQ], F32R) for i in range(2)]
        q_hi = [at(f"q_hi{i}", reg_acc, (4 + i) * TILE, [P, SEQ], F32R) for i in range(2)]
        q_lo = [at(f"q_lo{i}", reg_acc, (6 + i) * TILE, [P, SEQ], F32R) for i in range(2)]
        v_hi = [at(f"v_hi{i}", reg_acc, (8 + 2 * i) * TILE, [P, RT, 2 * V_DIM], F32R) for i in range(2)]
        v_lo = [at(f"v_lo{i}", reg_acc, (12 + 2 * i) * TILE, [P, RT, 2 * V_DIM], F32R) for i in range(2)]
        qr_lo = at("qr_lo", reg_u, 15 * TILE, [P, SEQ], F32R)
        qr_stack = [[at(f"qr_stack{i}_{e}", reg_e, (2 * i + e) * TILE, [P, SEQ], F32R) for e in range(2)]
                    for i in range(2)]
        head_rows = (slice(0, ROPE), slice(ROPE, 2 * ROPE))
        bundle_raw = at("bundle_raw", reg_xt, 8 * TILE, [P, BUNDLE])
        prob_at = [0, 1, 3, 6]

        def bundle_tiles(name, slot, places):
            return [at(f"{name}{slot}_{n}", base, offset, [P, hi - lo], F32R)
                    for n, ((base, offset), (lo, hi)) in enumerate(zip(places, BUNDLE_PARTS))]

        FIRST = 2
        bundle_hi = [bundle_tiles("bundle_hi", i, [(reg_w, i * BUNDLE), (reg_w, i * BUNDLE + UK)])
                     for i in range(2)]
        bundle_lo = [bundle_tiles("bundle_lo", i, [(reg_w, (2 + i) * BUNDLE), (reg_w, (2 + i) * BUNDLE + UK)])
                     for i in range(2)]
        bundle_hi.append(bundle_tiles("bundle_hi", FIRST, [(reg_x, 2 * (BUNDLE - UK)), (reg_x, 0)]))
        bundle_lo.append(bundle_tiles("bundle_lo", FIRST, [(reg_xt, 8 * TILE + BUNDLE), (reg_x, BUNDLE - UK)]))

        def piece(parts, lo, hi):
            n = 0 if hi <= UK else 1
            return parts[n][:, lo - BUNDLE_PARTS[n][0]:hi - BUNDLE_PARTS[n][0]]

        score_order = (3, 2, 1, 0)
        score_bank = (0, 3, 1, 0)
        turn_groups = ((3, ((3, 0),), 1), (1, ((1, 0),), 3), (2, ((2, 0), (0, 3 * P)), 4))
        prob = at("prob", reg_xt, 8 * TILE + BUNDLE, [P, 10 * P])
        pt_hi = at("pt_hi", reg_x, 0, [P, RT, SEQ], F32R)
        pt_lo = at("pt_lo", reg_x, 4 * TILE, [P, RT, SEQ], F32R)
        fg_hi = [at(f"fg_hi{i}", reg_u, i * TILE, [P, SEQ], F32R) for i in range(4)]
        fg_lo = [at(f"fg_lo{i}", reg_u, (4 + i) * TILE, [P, SEQ], F32R) for i in range(4)]

        bank = [ctx.enter_context(nc.psum_tensor(f"bank{i}", [P, BANK], F32)) for i in range(8)]

        x_landed = [sem(f"x_landed{r}") for r in range(RT)]
        small_landed = sem("small_landed")
        w_landed = [sem(f"w_landed{i}") for i in range(RAW_SLOTS)]
        w_hi_ready, w_lo_ready, w_used = sem("w_hi_ready"), sem("w_lo_ready"), sem("w_used")
        ident_ready, consts_ready = sem("ident_ready"), sem("consts_ready")
        vec_turned, taps_turned, vec_ready = sem("vec_turned"), sem("taps_turned"), sem("vec_ready")
        taps_hi_ready, taps_lo_ready, taps_ready = sem("taps_hi_ready"), sem("taps_lo_ready"), sem("taps_ready")
        x_turned, xt_hi_ready, xt_lo_ready = sem("x_turned"), sem("xt_hi_ready"), sem("xt_lo_ready")
        table_step, angles_ready, rope_ready = sem("table_step"), sem("angles_ready"), sem("rope_ready")
        evacuated = sem("evacuated")
        u_ready, pad_ready = sem("u_ready"), sem("pad_ready")
        diag_hi_ready, diag_lo_ready = sem("diag_hi_ready"), sem("diag_lo_ready")
        cu_hi_ready, cu_lo_ready = sem("cu_hi_ready"), sem("cu_lo_ready")
        pe_conv_done, pe_conv_kept = sem("pe_conv_done"), sem("pe_conv_kept")
        product_ready, product_added = sem("product_ready"), sem("product_added")
        tap_done, csum_done, sums_cleared = sem("tap_done"), sem("csum_done"), sem("sums_cleared")
        mean_done, centered, squared, vsum_done, vsum_odd_done, var_done = (
            sem("mean_done"), sem("centered"), sem("squared"), sem("vsum_done"), sem("vsum_odd_done"),
            sem("var_done"))
        var_ready, rstd_cols_ready, rstd_diag_ready, rstd_spread, rstd_ready, stat_step = (
            sem("var_ready"), sem("rstd_cols_ready"), sem("rstd_diag_ready"), sem("rstd_spread"), sem("rstd_ready"),
            sem("stat_step"))
        scaled, silu_done, gated, g_hi_ready, g_lo_ready = (
            sem("scaled"), sem("silu_done"), sem("gated"), sem("g_hi_ready"), sem("g_lo_ready"))
        res_landed, res_scaled, res_ready = sem("res_landed"), sem("res_scaled"), sem("res_ready")
        y_done, y_step, var_row_ready, rstd_row_ready, rstd_step, row_ready = (
            sem("y_done"), sem("y_step"), sem("var_row_ready"), sem("rstd_row_ready"),
            sem("rstd_step"), sem("row_ready"))
        h_turned, ht_copied, ht_hi_ready, ht_lo_ready, ht_lo_pool = (
            sem("h_turned"), sem("ht_copied"), sem("ht_hi_ready"), sem("ht_lo_ready"), sem("ht_lo_pool"))
        b_step, b_sum_done, b_var_ready, b_std_ready, b_rstd_ready = (
            sem("b_step"), sem("b_sum_done"), sem("b_var_ready"),
            sem("b_std_ready"), sem("b_rstd_ready"))
        lat_scaled, lat_hi_ready, lat_lo_ready = sem("lat_scaled"), sem("lat_hi_ready"), sem("lat_lo_ready")
        k_swapped = sem("k_swapped")
        bundle_landed, bundle_hi_ready, bundle_lo_ready = (
            sem("bundle_landed"), sem("bundle_hi_ready"), sem("bundle_lo_ready"))
        proj_done, proj_hi_ready, proj_lo_ready = sem("proj_done"), sem("proj_hi_ready"), sem("proj_lo_ready")
        qr_kept, q_swapped, rope_step, qr_rotated, qr_hi_ready, qr_split, qr_lo_ready = (
            sem("qr_kept"), sem("q_swapped"), sem("rope_step"), sem("qr_rotated"), sem("qr_hi_ready"),
            sem("qr_split"), sem("qr_lo_ready"))
        scores_done, masked, neg_top_ready, exp_done, inv_ready, prob_ready = (
            sem("scores_done"), sem("masked"), sem("neg_top_ready"), sem("exp_done"),
            sem("inv_ready"), sem("prob_ready"))
        prob_turned, pt_hi_ready, pt_lo_ready, pv_done, gate_ready = (
            sem("prob_turned"), sem("pt_hi_ready"), sem("pt_lo_ready"), sem("pv_done"), sem("gate_ready"))
        ln_rows_landed = sem("ln_rows_landed")
        stored = sem("stored")

        SMALL_DMAS = 9
        SHARED_TILE = 2
        SHARES = (1, 1, 3, 5)
        assert sum(SHARES) * (ROUNDS - 1) == TAPS - 1 and sum(SHARES) % 2 == 0
        MEAN_AT, VAR_AT = 11, 14
        PROJ_BANK = (7, 5, 6, 7, 5, 5, 6)
        SQUARE_STEPS = (2 * KV - 1, 2 * KV - 1 + 2 * KQ - 1)

        def landed_value(c):
            extra = 16 if isinstance(c, int) and c >= ROPE_CHUNK and (c - ROPE_CHUNK) % RAW_SLOTS == 0 else 0
            return 16 * (c // RAW_SLOTS + 1) + extra

        def step_taps(j, s):
            return [(sum(SHARES) * (j - 1) + 1 + i, (1 + i) % 2)
                    for i in range(sum(SHARES[:s]), sum(SHARES[:s + 1]))]

        def heads_loop(eng, step):
            with eng.Fori(0, ROUNDS - 1) as g:
                for s in range(1, ROUND + 1):
                    step(g, s)
            for s in range(1, ROUND):
                step(ROUNDS - 1, s)

        block = ctx.enter_context(nc.Block())

        @block.sync
        def _(sp):
            def raw_free(c):
                wait(sp, w_hi_ready, c - RAW_SLOTS + 1)
                wait(sp, w_lo_ready, c - RAW_SLOTS + 1)

            def load_columns(slot, source, column):
                sp.dma_start(w_raw[slot][:].rearrange("p (k m) -> p k m", m=P),
                             source[:, :, bass.ds(column, P)]).then_inc(w_landed[slot], 16)

            def load_value_gate(j, first=0):
                for s in range(first, ROUND):
                    for w in range(2):
                        raw_free(2 * ROUND * j + 2 * s + w)
                        load_columns(w, w_in_a, w * CONV_WIDTH + (ROUND * j + s) * P)

            for r in range(RT):
                sp.dma_start(x_in[:, r, :], x_rows[:, r, :]).then_inc(x_landed[r], 16)
                if r % 2 == 1:
                    w = r // 2
                    load_columns(w, w_in_a, w * CONV_WIDTH)
            sp.dma_start(taps_raw[:], a_conv_w[0]).then_inc(small_landed, 16)
            for row, vector, n in ((V_BIN, a_b_in, 3 * CT), (V_CONVB, a_conv_b, CT),
                                   (V_NG, a_norm_g, CT), (V_NB, a_norm_b, CT), (V_QG, b_q_norm_g, KQ)):
                sp.dma_start(vec_raw[row:row + n, :], vector.rearrange("a (n p) -> (a n) p", p=P)
                             ).then_inc(small_landed, 16)
            sp.dma_start(vec_raw[V_KVG:V_KVG + KV, :], kv_norm_g.rearrange("(n p) -> n p", p=P)
                         ).then_inc(small_landed, 16)
            sp.dma_start(freq[:], rope_freq).then_inc(small_landed, 16)
            sp.dma_start(pos_int[:], positions.broadcast_to([P, SEQ])).then_inc(small_landed, 16)
            load_value_gate(0, 1)
            with sp.Fori(1, ROUNDS) as j:
                load_value_gate(j)
            with sp.Fori(0, ROUNDS) as j:
                for s in range(ROUND):
                    raw_free(Z0 + ROUND * j + s)
                    load_columns(s % 2, w_in_a, 2 * CONV_WIDTH + (ROUND * j + s) * P)

            def load_output_a(k):
                raw_free(OUT0 + k)
                sp.dma_start(w_raw[k % 2][:], w_out_a[k]).then_inc(w_landed[k % 2], 16)

            for k in range(SLOTS):
                load_output_a(k)
            sp.wait_ge(w_used, OUT0)
            sp.dma_start(res[:], x_rows).then_inc(res_landed, 16)
            sp.dma_start(ln_rows[:, 0, :], ln_g[0:1, :].broadcast_to([P, D_MODEL])).then_inc(res_landed, 16)
            sp.dma_start(ln_rows[:, 1, :], ln_b[0:1, :].broadcast_to([P, D_MODEL])).then_inc(res_landed, 16)
            sp.dma_start(ln_rows[:, 2, :], a_b_out.broadcast_to([P, D_MODEL])).then_inc(res_landed, 16)
            for k in range(SLOTS, CT):
                load_output_a(k)
            for n in range(LATENTS):
                c = LAT0 + n
                raw_free(c)
                if n < KV:
                    load_columns(c % 2, w_down, n * P)
                elif n == KV:
                    halves = w_raw[c % 2][:].rearrange("p (k b m) -> p b k m", b=2, m=ROPE)
                    for b in range(2):
                        sp.dma_start(halves[:, b], w_down[:, :, KV_RANK:KV_RANK + ROPE]
                                     ).then_inc(w_landed[c % 2], 16)
                else:
                    load_columns(c % 2, w_in_b, (n - KV - 1) * P)
            for i in range(ROUND):
                raw_free(BZ0 + i)
                load_columns((BZ0 + i) % 2, w_in_b, Q_RANK + i * P)
            sp.wait_ge(evacuated, OUT0 + KV + 1)
            for b in range(4):
                sp.dma_start(k_swap[32 * b:32 * b + 32, :], lat[32 * (b ^ 1):32 * (b ^ 1) + 32, KV, :]
                             ).then_inc(k_swapped, 16)
            with sp.Fori(1, ROUNDS - 1) as j:
                for s in range(ROUND):
                    raw_free(BZ0 + ROUND * j + s)
                    load_columns((BZ0 + s) % 2, w_in_b, Q_RANK + (ROUND * j + s) * P)

            def load_bundle(p):
                wait(sp, bundle_hi_ready, 2 * p)
                wait(sp, bundle_lo_ready, 2 * p)
                for off, source in ((UK, w_uk), (UV, w_uv)):
                    sp.dma_start(bundle_raw[:, off:off + KV * 2 * NOPE].rearrange("p (k m) -> p k m", k=KV),
                                 source[:, :, bass.ds(p * 2 * NOPE, 2 * NOPE)]).then_inc(bundle_landed, 16)
                for e in range(2):
                    qn = bundle_raw[:, QN:BUNDLE].rearrange("p (k e m) -> p e k m", k=KQ, e=2)
                    qr = bundle_raw[:, QR:UK].rearrange("p (k e m) -> p e k m", k=KQ, e=2)
                    sp.dma_start(qn[:, e], w_uq[:, :, bass.ds(2 * p + e, 1), 0:NOPE].rearrange("p k o m -> p k (o m)")
                                 ).then_inc(bundle_landed, 16)
                    sp.dma_start(qr[:, e], w_uq[:, :, bass.ds(2 * p + e, 1), NOPE:NOPE + ROPE].rearrange("p k o m -> p k (o m)")
                                 ).then_inc(bundle_landed, 16)

            def swap_rotary(p):
                sp.wait_ge(qr_kept, p + 1)
                for b in range(4):
                    sp.dma_start(qr_swap[32 * b:32 * b + 32, :], qr_raw[32 * (b ^ 1):32 * (b ^ 1) + 32, :]
                                 ).then_inc(q_swapped, 16)

            for i in range(N_HEADS - ROUND, N_HEADS):
                if i == N_HEADS - 2:
                    sp.wait_ge(lat_scaled, LATENTS)
                    load_bundle(0)
                raw_free(BZ0 + i)
                load_columns((BZ0 + i) % 2, w_in_b, Q_RANK + i * P)
            def move_rotary_lo(p, slot):
                sp.wait_ge(qr_split, 2 * p + 2)
                for e in range(2):
                    sp.dma_start(qr_stack[slot][e][head_rows[1 - e], :].bitcast(F32), qr_lo[head_rows[e], :].bitcast(F32)
                                 ).then_inc(qr_lo_ready, 16)

            load_bundle(1)
            swap_rotary(0)
            move_rotary_lo(0, 0)
            with sp.Fori(0, PAIRS // 2 - 1) as i:
                for e in range(1, 3):
                    load_bundle(2 * i + e + 1)
                    swap_rotary(2 * i + e)
                    move_rotary_lo(2 * i + e, e % 2)
            swap_rotary(PAIRS - 1)
            move_rotary_lo(PAIRS - 1, (PAIRS - 1) % 2)

            sp.wait_ge(proj_done, 7 * (PAIRS - 1))
            for k in range(CT):
                c = FIN0 + k
                raw_free(c)
                sp.dma_start(w_raw[c % 2][:], w_out_b[k]).then_inc(w_landed[c % 2], 16)
                if k == 1:
                    sp.wait_ge(pv_done, N_HEADS)
                    sp.dma_start(ln_rows_b[:, 0, :], ln_g[1:2, :].broadcast_to([P, D_MODEL])
                                 ).then_inc(ln_rows_landed, 16)
                    sp.dma_start(ln_rows_b[:, 1, :], ln_b[1:2, :].broadcast_to([P, D_MODEL])
                                 ).then_inc(ln_rows_landed, 16)
            for r in range(RT):
                for half in range(HALVES):
                    cols = slice(half * BANK, (half + 1) * BANK)
                    sp.wait_ge(row_ready, HALVES * (RT + r) + half + 1)
                    sp.dma_start(out_rows[:, r, cols], res[:, r, cols]).then_inc(stored, 16)
            sp.wait_ge(stored, 16 * RT * HALVES)

        @block.gpsimd
        def _(pool):
            nc.gpsimd.memset(ident[:], 0.0).then_inc(ident_ready, 1)
            pool.wait_ge(ident_ready, 1)
            nc.gpsimd.affine_select(out=ident[:], in_=ident[:], compare_op=ALU.not_equal, fill=1.0, base=0,
                                    pattern=[[-1, P]], channel_multiplier=1).then_inc(ident_ready, 1)
            nc.gpsimd.memset(mask[:], 0.0).then_inc(consts_ready, 1)
            nc.gpsimd.memset(ones[:], 1.0).then_inc(consts_ready, 1)
            nc.gpsimd.memset(minus_half[:], -0.5).then_inc(consts_ready, 1)
            pool.wait_ge(consts_ready, 3)
            nc.gpsimd.affine_select(out=mask[:], in_=mask[:], compare_op=ALU.is_ge, fill=MASK_VALUE,
                                    base=SEQ - P, pattern=[[-1, SEQ]], channel_multiplier=1
                                    ).then_inc(consts_ready, 1)
            nc.gpsimd.memset(u[:, :, 0:PAD], 0.0).then_inc(pad_ready, 1)

            def split_lo(c, raw, slot):
                pool.wait_ge(w_hi_ready, c + 1)
                wait(pool, w_used, c - SLOTS + 1)
                nc.gpsimd.tensor_tensor(w_lo[slot][:], w_raw[raw][:], w_hi[slot][:].bitcast(F32),
                                        ALU.subtract).then_inc(w_lo_ready, 1)

            def glu(t, slot):
                pool.wait_ge(evacuated, 2 * t + 2)
                nc.gpsimd.tensor_tensor(u[:, bass.ds(t, 1), PAD:].rearrange("p o n -> p (o n)"), val[slot][:], sig[slot][:],
                                        ALU.mult).then_inc(u_ready, 1)

            def value_gate(j):
                for s in range(ROUND):
                    t = ROUND * j + s
                    for w in range(2):
                        split_lo(2 * t + w, w, (2 * s + w) % SLOTS)
                    if not isinstance(t, int) or t > 0:
                        glu(t - 1, (s - 1) % 2)
                    if not isinstance(j, int) or j > 0:
                        if s < 2:
                            conv_matrices(j, s)
                        if s == 2:
                            conv_input_lo(j)
                        for k, slot in step_taps(j, s):
                            add_product(k, slot)

            def add_product(k, slot):
                pool.wait_ge(product_ready, k + 1)
                pool.wait_ge(product_added, k + 1)
                nc.gpsimd.tensor_tensor(acc[:, SHARED_TILE, :], acc[:, SHARED_TILE, :], tap_product[slot][:], ALU.add
                                        ).then_inc(product_added, 1)

            def conv_matrices(j, part):
                pool.wait_ge(w_used, 2 * ROUND * j - 1)
                lo, hi = (0, TAPS // 2) if part == 0 else (TAPS // 2, TAPS)
                n = hi - lo
                taps = conv_w_hi[:, bass.ds(j * (ROUND * TAPS) - TAPS + lo, n)].bitcast(F32)
                nc.gpsimd.tensor_tensor(diag_hi[:, lo:hi, :],
                                        ident[:].unsqueeze(1).broadcast_to([P, n, P]),
                                        taps.unsqueeze(2).broadcast_to([P, n, P]),
                                        ALU.mult).then_inc(diag_hi_ready, 1)

            def conv_input_lo(j):
                pool.wait_ge(cu_hi_ready, j)
                nc.gpsimd.tensor_tensor(cu_lo[:], u[:, bass.ds(ROUND * j - 1, 1), :].rearrange("p o n -> p (o n)"),
                                        cu_hi[:].bitcast(F32), ALU.subtract).then_inc(cu_lo_ready, 1)

            value_gate(0)
            pool.wait_ge(taps_hi_ready, 1)
            pool.wait_ge(taps_turned, 1)
            nc.gpsimd.memset(acc[:, SHARED_TILE, :], 0.0).then_inc(product_added, 1)
            add_product(0, 0)
            with pool.Fori(1, ROUNDS) as j:
                value_gate(j)
            def add_odd_square(t):
                pool.wait_ge(squared, t + 1)
                if t == 1:
                    nc.gpsimd.tensor_copy(vsum_odd[:], sq[t % 4][:]).then_inc(vsum_odd_done, 1)
                else:
                    pool.wait_ge(vsum_odd_done, t // 2)
                    nc.gpsimd.tensor_tensor(vsum_odd[:], vsum_odd[:], sq[t % 4][:], ALU.add
                                            ).then_inc(vsum_odd_done, 1)

            for i in range(CT):
                split_lo(Z0 + i, i % 2, i % SLOTS)
                if i == 0:
                    glu(CT - 1, (CT - 1) % 2)
                if i >= CT - 2:
                    for t in range(*((1, 10, 2) if i == CT - 2 else (11, CT, 2))):
                        add_odd_square(t)
            pool.wait_ge(var_ready, 1)
            nc.gpsimd.tensor_tensor(rstd_cols[:], var_cols[:], minus_half[:], ALU.pow).then_inc(rstd_cols_ready, 1)

            def rstd_of_row(n, r):
                pool.wait_ge(var_row_ready, n + 1)
                nc.gpsimd.tensor_scalar(rstd_row[:, r, 0:1], mean_var[:, r, 1:2], LN_EPS, None, ALU.add
                                        ).then_inc(rstd_step, 1)
                pool.wait_ge(rstd_step, n + 1)
                nc.gpsimd.tensor_tensor(rstd_row[:, r, 1:2], rstd_row[:, r, 0:1], minus_half[:, 0:1], ALU.pow
                                        ).then_inc(rstd_row_ready, 1)

            for k in range(CT):
                c = OUT0 + k
                split_lo(c, c % 2, c % SLOTS)
                if 6 <= k < 6 + RT:
                    r = k - 6
                    pool.wait_ge(res_scaled, r + 1)
                    nc.gpsimd.tensor_tensor(res[:, r, :], res[:, r, :], ln_rows[:, 2, :], ALU.add
                                            ).then_inc(res_ready, 1)
            def turned_lo(q):
                r, half = q // 2, q % 2
                cut = (slice(None), slice(4 * half, 4 * half + 4), slice(r * P, (r + 1) * P))
                pool.wait_ge(ht_hi_ready, q + 1)
                pool.wait_ge(ht_copied, q + 1)
                nc.gpsimd.tensor_tensor(ht_lo[cut], ht_copy[:, q, :].rearrange("p (k n) -> p k n", k=4),
                                        ht_hi[cut].bitcast(F32), ALU.subtract).then_inc(ht_lo_pool, 1)

            def split_bundle_lo(p, slot, part):
                lo, hi = BUNDLE_PARTS[part]
                pool.wait_ge(bundle_hi_ready, 2 * p + part + 1)
                nc.gpsimd.tensor_tensor(bundle_lo[slot][part][:], bundle_raw[:, lo:hi],
                                        bundle_hi[slot][part][:].bitcast(F32), ALU.subtract
                                        ).then_inc(bundle_lo_ready, 1)

            rstd_of_row(0, 0)
            rstd_of_row(1, 1)
            turned_lo(0)
            rstd_of_row(2, 2)
            turned_lo(1)
            turned_lo(2)
            turned_lo(3)
            split_lo(LAT0, LAT0 % 2, LAT0 % SLOTS)
            rstd_of_row(3, 3)
            for c in range(LAT0 + 1, FIN0):
                split_lo(c, c % 2, c % SLOTS)
                if c == FIN0 - 3:
                    split_bundle_lo(0, FIRST, 0)
            split_bundle_lo(0, FIRST, 1)

            def rotate(p):
                pool.wait_ge(q_swapped, 64 * (p + 1))
                nc.gpsimd.tensor_tensor(qr_raw[:], qr_raw[:], cos[:], ALU.mult).then_inc(rope_step, 1)
                nc.gpsimd.tensor_tensor(qr_swap[:], qr_swap[:], sin[:], ALU.mult).then_inc(rope_step, 1)
                pool.wait_ge(rope_step, 2 * p + 2)
                nc.gpsimd.tensor_tensor(qr_raw[:], qr_raw[:], qr_swap[:], ALU.add).then_inc(qr_rotated, 1)

            rotate(0)
            for part in range(2):
                split_bundle_lo(1, 1, part)
            with pool.Fori(0, PAIRS // 2 - 1) as i:
                for e in range(2):
                    rotate(2 * i + e + 1)
                    for part in range(2):
                        split_bundle_lo(2 * i + e + 2, e, part)
            rotate(PAIRS - 1)

            pool.wait_ge(proj_done, 7 * PAIRS)
            for k in range(CT):
                c = FIN0 + k
                split_lo(c, c % 2, c % SLOTS)
            for r in range(RT):
                rstd_of_row(RT + r, r)

        @block.scalar
        def _(act):
            def split_hi(c, raw, slot, landed):
                act.wait_ge(w_landed[raw], landed)
                wait(act, w_used, c - SLOTS + 1)
                nc.scalar.activation(w_hi[slot][:], w_raw[raw][:], ACT.Copy).then_inc(w_hi_ready, 1)

            def keep_value_gate(t, s):
                wait(act, u_ready, t - 1)
                act.wait_ge(w_used, 2 * t + 1)
                nc.scalar.activation(val[s % 2][:], bank[2 * s % 4][:], ACT.Identity,
                                     bias=vec[:, bass.ds(V_BIN + t, 1)]).then_inc(evacuated, 1)
                act.wait_ge(w_used, 2 * t + 2)
                nc.scalar.activation(sig[s % 2][:], bank[(2 * s + 1) % 4][:], ACT.Sigmoid,
                                     bias=vec[:, bass.ds(V_BIN + CT + t, 1)]).then_inc(evacuated, 1)

            def value_gate(j):
                for s in range(ROUND):
                    t = ROUND * j + s
                    if not isinstance(t, int) or t > 0:
                        for w in range(2):
                            split_hi(2 * t + w, w, (2 * s + w) % SLOTS, 16 * (t + 1))
                    if not isinstance(t, int) or t > 0:
                        keep_value_gate(t - 1, s - 1)
                    if not isinstance(j, int) or j > 0:
                        if s < 2:
                            conv_matrices(j, s)
                        if s == 2:
                            conv_input_hi(j)
                        for k, slot in step_taps(j, s):
                            tap_times_u(k, slot)
                        if s == 3:
                            keep_conv(j)

            def tap_times_u(k, slot):
                column = V_CONVB + SHARED_TILE
                bias = {"bias": vec[:, column:column + 1]} if isinstance(k, int) and k == 0 else {}
                wait(act, product_added, k)
                nc.scalar.activation(tap_product[slot][:], u[:, SHARED_TILE, bass.ds(k, SEQ)],
                                     ACT.Identity if bias else ACT.Copy,
                                     scale=conv_w[:, bass.ds(k + SHARED_TILE * TAPS, 1)], **bias).then_inc(product_ready, 1)

            def conv_matrices(j, part):
                if part == 0:
                    act.wait_ge(w_used, 2 * ROUND * j - 1)
                for k in range(*((0, TAPS // 2) if part == 0 else (TAPS // 2, TAPS))):
                    nc.scalar.activation(
                        diag_lo[:, k, :], ident[:], ACT.Copy,
                        scale=conv_w_lo[:, bass.ds(j * (ROUND * TAPS) - TAPS + k, 1)].bitcast(F32)
                    ).then_inc(diag_lo_ready, 1)

            def conv_input_hi(j):
                act.wait_ge(u_ready, ROUND * j)
                nc.scalar.activation(cu_hi[:], u[:, bass.ds(ROUND * j - 1, 1), :].rearrange("p o n -> p (o n)"),
                                     ACT.Copy).then_inc(cu_hi_ready, 1)

            def keep_conv(j):
                act.wait_ge(pe_conv_done, j)
                nc.scalar.activation(acc[:, bass.ds(ROUND * j - 1, 1), :].rearrange("p o n -> p (o n)"), bank[6][:],
                                     ACT.Identity, bias=vec[:, bass.ds(V_CONVB + ROUND * j - 1, 1)]
                                     ).then_inc(pe_conv_kept, 1)

            for q in range(2 * RT):
                r, half = q // 2, q % 2
                act.wait_ge(x_turned, q + 1)
                nc.scalar.activation(xt_hi[:, 4 * half:4 * half + 4, r * P:(r + 1) * P],
                                     bank[q % 4][:].rearrange("p (k n) -> p k n", k=4), ACT.Copy
                                     ).then_inc(xt_hi_ready, 1)
                if q % 4 == 3:
                    split_hi(q // 4, q // 4, q // 4, 16)
            act.wait_ge(taps_turned, 1)
            nc.scalar.activation(conv_w_hi[:], bank[4][:, 0:CT * TAPS], ACT.Copy).then_inc(taps_hi_ready, 1)
            act.wait_ge(vec_turned, 1)
            nc.scalar.activation(vec[:], bank[5][:, 0:V_ALL], ACT.Copy).then_inc(vec_ready, 1)
            act.wait_ge(vec_ready, 1)
            value_gate(0)
            act.wait_ge(angles_ready, 1)
            nc.scalar.activation(sin[:], angle[:], ACT.Sin).then_inc(rope_ready, 1)
            nc.scalar.activation(cos[:], angle_c[:], ACT.Sin).then_inc(rope_ready, 1)
            act.wait_ge(ident_ready, 2)
            act.wait_ge(taps_lo_ready, 1)
            act.wait_ge(pad_ready, 1)
            act.wait_ge(rope_ready, 2)
            act.wait_ge(taps_ready, 1)
            act.wait_ge(u_ready, SHARED_TILE + 1)
            tap_times_u(0, 0)
            with act.Fori(1, ROUNDS) as j:
                value_gate(j)

            def keep_z(i):
                act.wait_ge(w_used, Z0 + i + 1)
                nc.scalar.activation(z_a[:, i, :], bank[i % 4][:], ACT.Silu,
                                     bias=vec[:, V_BIN + 2 * CT + i:V_BIN + 2 * CT + i + 1]
                                     ).then_inc(evacuated, 1)

            def z_split(i):
                c = Z0 + i
                split_hi(c, c % 2, c % SLOTS, landed_value(c))

            def square(t):
                act.wait_ge(centered, t + 1)
                wait(act, (vsum_done, vsum_odd_done)[t % 2], t // 2 - 1)
                nc.scalar.activation(sq[t % 4][:], acc[:, t, :], ACT.Square).then_inc(squared, 1)

            def branch_silu(t):
                act.wait_ge(scaled, t + 1)
                nc.scalar.activation(acc[:, t, :], acc[:, t, :], ACT.Silu,
                                     bias=vec[:, V_NB + t:V_NB + t + 1], scale=vec[:, V_NG + t:V_NG + t + 1]
                                     ).then_inc(silu_done, 1)

            def branch_hi(k):
                act.wait_ge(gated, k + 1)
                nc.scalar.activation(g_hi[:, k, :], acc[:, k, :], ACT.Copy).then_inc(g_hi_ready, 1)

            for i in range(CT):
                z_split(i)
                if i == 0:
                    keep_value_gate(CT - 1, CT - 1)
                if i >= CT - 2:
                    for t in range(*((0, 10) if i == CT - 2 else (10, CT))):
                        square(t)
                if i >= 3:
                    keep_z(i - 3)

            def output_split(k):
                c = OUT0 + k
                split_hi(c, c % 2, c % SLOTS, landed_value(c))

            for k in range(2):
                output_split(k)
                keep_z(CT - 3 + k)
            act.wait_ge(rstd_spread, 1)
            nc.scalar.activation(rstd_a[:], bank[7][:], ACT.Copy).then_inc(rstd_ready, 1)
            for t in range(CT + 3):
                if t in (3, 9):
                    output_split(2 + t // 9)
                if t == 5:
                    keep_z(CT - 1)
                if t < CT:
                    branch_silu(t)
                if t >= 3:
                    branch_hi(t - 3)
            for k in range(SLOTS, CT):
                output_split(k)
                if 5 <= k < 5 + RT:
                    r = k - 5
                    act.wait_ge(res_landed, 64)
                    nc.scalar.activation(res[:, r, :], res[:, r, :], ACT.Copy, scale=ALPHA
                                         ).then_inc(res_scaled, 1)

            act.wait_ge(g_lo_ready, CT)
            for q in range(2 * RT):
                r, half = q // 2, q % 2
                if q >= 2 * RT - SLOTS:
                    c = LAT0 + q - (2 * RT - SLOTS)
                    split_hi(c, c % 2, c % SLOTS, landed_value(c))
                act.wait_ge(h_turned, q + 1)
                nc.scalar.activation(ht_hi[:, 4 * half:4 * half + 4, r * P:(r + 1) * P],
                                     bank[q][:].rearrange("p (k n) -> p k n", k=4), ACT.Copy
                                     ).then_inc(ht_hi_ready, 1)
                if q < RT:
                    nc.scalar.activation(ht_copy[:, q, :], bank[q][:], ACT.Copy).then_inc(ht_copied, 1)

            def keep_latent(n):
                act.wait_ge(w_used, LAT0 + n + 1)
                nc.scalar.activation(lat[:, n, :], bank[n % 4][:], ACT.Copy).then_inc(evacuated, 1)

            def keep_gate(i):
                act.wait_ge(w_used, BZ0 + i + 1)
                nc.scalar.activation(gate[:, i, :], bank[(LATENTS + i) % 4][:], ACT.Silu).then_inc(evacuated, 1)

            def latent_hi(m, out_ap, in_ap):
                act.wait_ge(lat_scaled, m + 1)
                nc.scalar.activation(out_ap, in_ap, ACT.Copy).then_inc(lat_hi_ready, 1)

            def split_bundle_hi(p, slot, part):
                lo, hi = BUNDLE_PARTS[part]
                act.wait_ge(bundle_landed, 96 * (p + 1))
                wait(act, proj_done, 7 * (p - 1))
                nc.scalar.activation(bundle_hi[slot][part][:], bundle_raw[:, lo:hi], ACT.Copy
                                     ).then_inc(bundle_hi_ready, 1)

            def keep_rotary(p):
                act.wait_ge(proj_done, 7 * p + 1)
                wait(act, qr_lo_ready, 32 * p)
                nc.scalar.activation(qr_raw[:], bank[PROJ_BANK[0]][:], ACT.Copy).then_inc(qr_kept, 1)

            def rotary_hi(p, slot):
                act.wait_ge(qr_rotated, p + 1)
                for e in range(2):
                    rows = head_rows[e]
                    nc.scalar.activation(qr_stack[slot][e][rows, :], qr_raw[rows, :], ACT.Copy
                                         ).then_inc(qr_hi_ready, 1)

            for n in range(SLOTS, LATENTS + N_HEADS):
                c = LAT0 + n
                m = n - SLOTS
                if m < LATENTS:
                    keep_latent(m)
                else:
                    keep_gate(m - LATENTS)
                split_hi(c, c % 2, c % SLOTS, landed_value(c))
                if n == LATENTS + 7:
                    act.wait_ge(b_var_ready, 2)
                    nc.scalar.activation(b_std[:], b_var[:], ACT.Sqrt).then_inc(b_std_ready, 1)
                if n == LATENTS + 10:
                    for k in range(KV):
                        latent_hi(k, ckv_hi[:, k, :], lat[:, k, :])
                    latent_hi(KV, kr_hi[:], lat[:, KV, :])
                if n == LATENTS + 11:
                    for k in range(KQ):
                        latent_hi(KV + 1 + k, cq_hi[:, k, :], lat[:, KV + 1 + k, :])
                part = n - (LATENTS + N_HEADS - 3)
                if part == 0:
                    act.wait_ge(lat_lo_ready, LATENTS)
                if part in (0, 1):
                    split_bundle_hi(0, FIRST, part)
            keep_rotary(0)
            rotary_hi(0, 0)
            for i in range(N_HEADS - 4, N_HEADS):
                keep_gate(i)

            def keep_values(p, slot):
                for half in range(2):
                    act.wait_ge(proj_done, 7 * p + half + 2)
                    nc.scalar.activation(v_hi[slot][:, 2 * half:2 * half + 2, :],
                                         bank[PROJ_BANK[1 + half]][:].rearrange("p (t n) -> p t n", t=2), ACT.Copy
                                         ).then_inc(proj_hi_ready, 1)

            def keep_head(p, e):
                for n, tile in ((0, k_hi), (1, q_hi)):
                    act.wait_ge(proj_done, 7 * p + 3 + 2 * e + n + 1)
                    nc.scalar.activation(tile[e][:], bank[PROJ_BANK[3 + 2 * e + n]][:], ACT.Copy
                                         ).then_inc(proj_hi_ready, 1)

            def exps(h):
                for i, b in enumerate(score_order):
                    if i % 2 == 0:
                        act.wait_ge(neg_top_ready, 2 * h + i // 2 + 1)
                    n = (b + 1) * P
                    block_ = prob[:, prob_at[b] * P:prob_at[b] * P + n]
                    nc.scalar.activation(block_, block_, ACT.Exp, bias=neg_top[:, b:b + 1], scale=SM_SCALE,
                                         accum_out=denom[:, b:b + 1]).then_inc(exp_done, 1)

            def transposed_hi(h):
                for g, (from_bank, group, _) in enumerate(turn_groups):
                    act.wait_ge(prob_turned, 3 * h + g + 1)
                    for b, first in group:
                        nc.scalar.activation(pt_hi[:, 0:b + 1, b * P:(b + 1) * P],
                                             bank[from_bank][:, first:first + (b + 1) * P].rearrange(
                                                 "p (k n) -> p k n", k=b + 1), ACT.Copy).then_inc(pt_hi_ready, 1)

            act.wait_ge(w_used, FIN0)
            keep_values(0, 0)
            keep_head(0, 0)
            for part in range(2):
                split_bundle_hi(1, 1, part)
            keep_head(0, 1)
            exps(0)
            keep_rotary(1)
            keep_values(1, 1)
            transposed_hi(0)

            def head(g, s):
                h = ROUND * g + s
                exps(h)
                if s % 2 == 1:
                    p = 2 * g + (s + 1) // 2
                    if not isinstance(p, int) or p < PAIRS:
                        rotary_hi(p, ((s + 1) // 2) % 2)
                        keep_head(p, 0)
                    transposed_hi(h)
                    if not isinstance(p, int) or p < PAIRS - 1:
                        for part in range(2):
                            split_bundle_hi(p + 1, ((s + 1) // 2 + 1) % 2, part)
                else:
                    keep_head(2 * g + s // 2, 1)
                    p = 2 * g + s // 2 + 1
                    if not isinstance(p, int) or p < PAIRS:
                        keep_rotary(p)
                        keep_values(p, (s // 2 + 1) % 2)
                    transposed_hi(h)

            heads_loop(act, head)

            act.wait_ge(proj_done, 7 * PAIRS)
            for k in range(CT):
                c = FIN0 + k
                split_hi(c, c % 2, c % SLOTS, landed_value(c))
                act.wait_ge(gate_ready, k + 1)
                wait(act, w_used, c - SLOTS + 1)
                nc.scalar.activation(fg_hi[k % 4][:], gate[:, k, :], ACT.Copy).then_inc(g_hi_ready, 1)

        @block.vector
        def _(dve):
            nc.vector.memset(csum[:], 0.0).then_inc(sums_cleared, 1)
            nc.vector.memset(vsum[:], 0.0).then_inc(sums_cleared, 1)
            for q in range(2 * RT):
                r, half = q // 2, q % 2
                dve.wait_ge(xt_hi_ready, q + 1)
                cut = (slice(None), slice(4 * half, 4 * half + 4), slice(r * P, (r + 1) * P))
                nc.vector.tensor_tensor(xt_lo[cut], bank[q % 4][:].rearrange("p (k n) -> p k n", k=4),
                                        xt_hi[cut].bitcast(F32), ALU.subtract).then_inc(xt_lo_ready, 1)

            steps = [0]

            def chained(instruction):
                instruction.then_inc(table_step, 1)
                steps[0] += 1
                dve.wait_ge(table_step, steps[0])

            dve.wait_ge(small_landed, 16 * SMALL_DMAS)
            chained(nc.vector.tensor_copy(pos[:], pos_int[:]))
            chained(nc.vector.tensor_scalar(angle[:], pos[:], freq[:, 0:1], None, ALU.mult))
            chained(nc.vector.tensor_scalar(turns[:], angle[:], 1.0 / TWO_PI, ROUNDER, ALU.mult, ALU.add))
            chained(nc.vector.tensor_scalar(turns[:], turns[:], -ROUNDER, None, ALU.add))
            for part in (PI_A, PI_B, PI_C):
                chained(nc.vector.scalar_tensor_tensor(out=angle[:], in0=turns[:], scalar=-part, in1=angle[:],
                                                       op0=ALU.mult, op1=ALU.add))
            chained(nc.vector.tensor_scalar(angle_c[:], angle[:], 0.5 * np.pi, None, ALU.add))
            chained(nc.vector.tensor_scalar(turns[:], angle_c[:], PI_SAFE, -TWO_PI, ALU.is_gt, ALU.mult))
            chained(nc.vector.tensor_tensor(angle_c[:], angle_c[:], turns[:], ALU.add))
            chained(nc.vector.tensor_scalar(angle_c[:], angle_c[:], PI_SAFE, -PI_SAFE, ALU.min, ALU.max))
            chained(nc.vector.tensor_scalar(angle[:], angle[:], PI_SAFE, -PI_SAFE, ALU.min, ALU.max))
            nc.vector.tensor_scalar(angle[:], angle[:], freq[:, 1:2], None, ALU.mult).then_inc(angles_ready, 1)

            dve.wait_ge(taps_hi_ready, 1)
            nc.vector.tensor_copy(conv_w[:], bank[4][:, 0:CT * TAPS]).then_inc(taps_ready, 1)
            nc.vector.tensor_tensor(conv_w_lo[:], bank[4][:, 0:CT * TAPS], conv_w_hi[:].bitcast(F32),
                                    ALU.subtract).then_inc(taps_lo_ready, 1)

            DVE_TILES = ROUND - 1

            def convolve(first, starts, done):
                taken, last_of, pos = [0] * len(starts), [0] * len(starts), 0
                while min(taken) < TAPS:
                    for i, begin in enumerate(starts):
                        if pos < begin or taken[i] == TAPS:
                            continue
                        t, k = first + i, taken[i]
                        shifted = u[:, bass.ds(t, 1), k:k + SEQ].rearrange("p o n -> p (o n)")
                        acc_t = acc[:, bass.ds(t, 1), :].rearrange("p o n -> p (o n)")
                        tap = conv_w[:, bass.ds(t * TAPS + k, 1)]
                        if k == 0:
                            dve.wait_ge(u_ready, t + 1)
                            nc.vector.tensor_scalar(acc_t, shifted, tap, vec[:, bass.ds(V_CONVB + t, 1)],
                                                    ALU.mult, ALU.add).then_inc(tap_done, 1)
                        else:
                            dve.wait_ge(tap_done, done + last_of[i])
                            nc.vector.scalar_tensor_tensor(out=acc_t, in0=shifted, scalar=tap, in1=acc_t,
                                                           op0=ALU.mult, op1=ALU.add).then_inc(tap_done, 1)
                        taken[i] += 1
                        pos += 1
                        last_of[i] = pos

            def add_to_csum(t, n):
                wait(dve, csum_done, n)
                nc.vector.tensor_tensor(csum[:], csum[:], acc[:, bass.ds(t, 1), :].rearrange("p o n -> p (o n)"),
                                        ALU.add).then_inc(csum_done, 1)

            def convolve_round(j, count):
                done = DVE_TILES * TAPS * j - TAPS
                convolve(ROUND * j, (0, 9, 26, 66)[:count], done)
                dve.wait_ge(tap_done, done + count * TAPS)
                for i in range(count):
                    add_to_csum(ROUND * j + i, ROUND * j - 2 + i)
                dve.wait_ge(pe_conv_kept, j)
                add_to_csum(ROUND * j - 1, ROUND * j - 2 + count)

            dve.wait_ge(sums_cleared, 2)
            dve.wait_ge(vec_ready, 1)
            dve.wait_ge(taps_ready, 1)
            dve.wait_ge(pad_ready, 1)
            convolve(0, (0, 14), 0)
            dve.wait_ge(tap_done, 2 * TAPS)
            for i in range(2):
                add_to_csum(i, i)
            dve.wait_ge(rope_ready, 2)
            with dve.Fori(1, ROUNDS - 1) as j:
                convolve_round(j, DVE_TILES)
            convolve_round(ROUNDS - 1, ROUND)
            dve.wait_ge(product_added, TAPS + 1)
            add_to_csum(SHARED_TILE, CT - 1)

            dve.wait_ge(mean_done, 1)
            for t in range(CT + 2):
                if t < CT:
                    nc.vector.scalar_tensor_tensor(out=acc[:, t, :], in0=bank[7][:], scalar=-1.0 / CONV_WIDTH,
                                                   in1=acc[:, t, :], op0=ALU.mult, op1=ALU.add
                                                   ).then_inc(centered, 1)
                if t >= 2 and t % 2 == 0:
                    dve.wait_ge(squared, t - 1)
                    wait(dve, vsum_done, t // 2 - 1)
                    nc.vector.tensor_tensor(vsum[:], vsum[:], sq[(t - 2) % 4][:], ALU.add).then_inc(vsum_done, 1)

            stat_count = [0]

            def stat(instruction):
                instruction.then_inc(stat_step, 1)
                stat_count[0] += 1
                dve.wait_ge(stat_step, stat_count[0])

            def refined_rstd(var, std, t, rstd, ready):
                stat(nc.vector.reciprocal(rstd, std))
                stat(nc.vector.tensor_tensor(t, rstd, rstd, ALU.mult))
                stat(nc.vector.tensor_tensor(t, t, var, ALU.mult))
                stat(nc.vector.tensor_scalar(t, t, -0.5, 1.5, ALU.mult, ALU.add))
                nc.vector.tensor_tensor(rstd, rstd, t, ALU.mult).then_inc(ready, 1)

            dve.wait_ge(var_done, 1)
            nc.vector.tensor_scalar(var_cols[:], bank[7][:, 0:RT], 1.0 / CONV_WIDTH, LN_EPS, ALU.mult, ALU.add
                                    ).then_inc(var_ready, 1)
            dve.wait_ge(rstd_cols_ready, 1)
            for b in range(RT):
                nc.vector.tensor_scalar(rstd_diag[:, b * P:(b + 1) * P], ident[:], rstd_cols[:, b:b + 1], None,
                                        ALU.mult).then_inc(rstd_diag_ready, 1)
            dve.wait_ge(rstd_ready, 1)
            dve.wait_ge(centered, CT)

            def gate_branch(t):
                dve.wait_ge(silu_done, t + 1)
                dve.wait_ge(evacuated, Z0 + t + 1)
                nc.vector.tensor_tensor(acc[:, t, :], acc[:, t, :], z_a[:, t, :], ALU.mult).then_inc(gated, 1)

            def branch_lo(t):
                dve.wait_ge(g_hi_ready, t + 1)
                nc.vector.tensor_tensor(g_lo[:, t, :], acc[:, t, :], g_hi[:, t, :].bitcast(F32), ALU.subtract
                                        ).then_inc(g_lo_ready, 1)

            for t in range(CT + 6):
                if t < CT:
                    nc.vector.tensor_tensor(acc[:, t, :], acc[:, t, :], rstd_a[:], ALU.mult).then_inc(scaled, 1)
                if 3 <= t < CT + 3:
                    gate_branch(t - 3)
                if t >= 6:
                    branch_lo(t - 6)

            def row_norm(n, r, rows, scale, meanwhile=None):
                halves = [res[:, r, half * BANK:(half + 1) * BANK] for half in range(HALVES)]
                cols = [slice(half * BANK, (half + 1) * BANK) for half in range(HALVES)]
                for half in range(HALVES):
                    dve.wait_ge(y_done, HALVES * n + half + 1)
                    nc.vector.scalar_tensor_tensor(out=halves[half], in0=halves[half], scalar=scale,
                                                   in1=bank[2 * r + half][:], op0=ALU.mult, op1=ALU.add
                                                   ).then_inc(y_step, 1)
                    dve.wait_ge(y_step, 6 * n + 2 * half + 1)
                    nc.vector.bn_stats(bn[:, r, half, :], halves[half]).then_inc(y_step, 1)
                if meanwhile:
                    meanwhile()
                dve.wait_ge(y_step, 6 * n + 4)
                nc.vector.bn_aggr(mean_var[:, r, :], bn[:, r].rearrange("p a b -> p (a b)")).then_inc(var_row_ready, 1)
                dve.wait_ge(var_row_ready, n + 1)
                for half in range(HALVES):
                    nc.vector.scalar_tensor_tensor(out=halves[half], in0=halves[half], scalar=mean_var[:, r, 0:1],
                                                   in1=rows[:, 0, cols[half]], op0=ALU.subtract, op1=ALU.mult
                                                   ).then_inc(y_step, 1)
                dve.wait_ge(rstd_row_ready, n + 1)
                for half in range(HALVES):
                    dve.wait_ge(y_step, 6 * n + 5 + half)
                    nc.vector.scalar_tensor_tensor(out=halves[half], in0=halves[half], scalar=rstd_row[:, r, 1:2],
                                                   in1=rows[:, 1, cols[half]], op0=ALU.mult, op1=ALU.add
                                                   ).then_inc(row_ready, 1)

            dve.wait_ge(res_ready, RT)
            def turned_lo(r):
                for q in (2 * r, 2 * r + 1):
                    cut = (slice(None), slice(4 * (q % 2), 4 * (q % 2) + 4), slice(r * P, (r + 1) * P))
                    dve.wait_ge(ht_hi_ready, q + 1)
                    nc.vector.tensor_tensor(ht_lo[cut], bank[q][:].rearrange("p (k n) -> p k n", k=4),
                                            ht_hi[cut].bitcast(F32), ALU.subtract).then_inc(ht_lo_ready, 1)

            for r in range(RT):
                row_norm(r, r, ln_rows, 1.0, (lambda: turned_lo(RT - 2)) if r == RT - 1 else None)
            turned_lo(RT - 1)

            bcount = [0]

            def b_next(instruction):
                instruction.then_inc(b_step, 1)
                bcount[0] += 1
                dve.wait_ge(b_step, bcount[0])

            dve.wait_ge(row_ready, 2 * RT)
            for which, tiles in ((0, range(KV)), (1, range(KV + 1, LATENTS))):
                for m in tiles:
                    dve.wait_ge(evacuated, OUT0 + m + 1)
                    if m == tiles[0]:
                        b_next(nc.vector.tensor_tensor(b_sum[:, which, :], lat[:, m, :], lat[:, m, :], ALU.mult))
                    else:
                        b_next(nc.vector.tensor_tensor(b_sq[:], lat[:, m, :], lat[:, m, :], ALU.mult))
                        b_next(nc.vector.tensor_tensor(b_sum[:, which, :], b_sum[:, which, :], b_sq[:], ALU.add))
            dve.wait_ge(k_swapped, 64)
            dve.wait_ge(rope_ready, 2)
            b_next(nc.vector.tensor_tensor(lat[:, KV, :], lat[:, KV, :], cos[:], ALU.mult))
            b_next(nc.vector.tensor_tensor(k_swap[:], k_swap[:], sin[:], ALU.mult))
            for which, rank in ((0, KV_RANK), (1, Q_RANK)):
                dve.wait_ge(b_sum_done, which + 1)
                nc.vector.tensor_scalar(b_var[:, which, :], bank[4 + which][:], 1.0 / rank, RMS_EPS,
                                        ALU.mult, ALU.add).then_inc(b_var_ready, 1)
            dve.wait_ge(b_std_ready, 1)
            dve.wait_ge(b_var_ready, 2)
            for which in range(2):
                refined_rstd(b_var[:, which, :], b_std[:, which, :], b_newton[:], b_rstd[:, which, :], b_rstd_ready)
                dve.wait_ge(b_rstd_ready, which + 1)
            for m in range(LATENTS):
                if m == KV:
                    nc.vector.tensor_tensor(lat[:, KV, :], lat[:, KV, :], k_swap[:], ALU.add).then_inc(lat_scaled, 1)
                    continue
                gain = V_KVG + m if m < KV else V_QG + m - KV - 1
                nc.vector.scalar_tensor_tensor(out=lat[:, m, :], in0=lat[:, m, :], scalar=vec[:, gain:gain + 1],
                                               in1=b_rstd[:, 0 if m < KV else 1, :], op0=ALU.mult, op1=ALU.mult
                                               ).then_inc(lat_scaled, 1)
            for m in range(LATENTS):
                dve.wait_ge(lat_hi_ready, m + 1)
                hi, lo = ((ckv_hi[:, m, :], ckv_lo[:, m, :]) if m < KV else (kr_hi[:], kr_lo[:]) if m == KV
                          else (cq_hi[:, m - KV - 1, :], cq_lo[:, m - KV - 1, :]))
                nc.vector.tensor_tensor(lo, lat[:, m, :], hi.bitcast(F32), ALU.subtract).then_inc(lat_lo_ready, 1)

            def mask_scores(h):
                for i, b in enumerate(score_order):
                    n = (b + 1) * P
                    dve.wait_ge(scores_done, RT * h + i + 1)
                    nc.vector.memset(waited[:, b:b + 1], 0.0)
                    nc.vector.tensor_tensor_reduce(prob[:, prob_at[b] * P:prob_at[b] * P + n], bank[score_bank[i]][:, 0:n],
                                                   mask[:, SEQ - n:SEQ], 1.0, MAX_START, ALU.add, ALU.max,
                                                   top[:, b:b + 1]).then_inc(masked, 1)
                    if i % 2 == 1:
                        dve.wait_ge(masked, RT * h + i + 1)
                        nc.vector.tensor_scalar(neg_top[:, b:b + 2], top[:, b:b + 2], -SM_SCALE, None, ALU.mult
                                                ).then_inc(neg_top_ready, 1)

            def normalise(h):
                for half, blocks in enumerate((score_order[:2], score_order[2:])):
                    dve.wait_ge(exp_done, RT * h + 2 * half + 2)
                    pair = slice(min(blocks), min(blocks) + 2)
                    nc.vector.reciprocal(inv_denom[:, pair], denom[:, pair]).then_inc(inv_ready, 1)
                    dve.wait_ge(inv_ready, 2 * h + half + 1)
                    for b in blocks:
                        block_ = prob[:, prob_at[b] * P:(prob_at[b] + b + 1) * P]
                        nc.vector.tensor_scalar(block_, block_, inv_denom[:, b:b + 1], None, ALU.mult
                                                ).then_inc(prob_ready, 1)

            def rotary_lo(p, slot):
                for e in range(2):
                    rows = head_rows[e]
                    dve.wait_ge(qr_hi_ready, 2 * p + e + 1)
                    nc.vector.tensor_tensor(qr_lo[rows, :], qr_raw[rows, :], qr_stack[slot][e][rows, :].bitcast(F32),
                                            ALU.subtract).then_inc(qr_split, 1)

            def pair_lo(p, slot):
                for half in range(2):
                    dve.wait_ge(proj_hi_ready, 6 * p + half + 1)
                    cut = (slice(None), slice(2 * half, 2 * half + 2), slice(None))
                    nc.vector.tensor_tensor(v_lo[slot][cut], bank[PROJ_BANK[1 + half]][:].rearrange("p (t n) -> p t n", t=2),
                                            v_hi[slot][cut].bitcast(F32), ALU.subtract).then_inc(proj_lo_ready, 1)

            def head_lo(p, e):
                for n, (hi, lo) in enumerate(((k_hi, k_lo), (q_hi, q_lo))):
                    dve.wait_ge(proj_hi_ready, 6 * p + 2 + 2 * e + n + 1)
                    nc.vector.tensor_tensor(lo[e][:], bank[PROJ_BANK[3 + 2 * e + n]][:], hi[e][:].bitcast(F32),
                                            ALU.subtract).then_inc(proj_lo_ready, 1)

            def transposed_lo(h):
                n = 0
                for from_bank, group, _ in turn_groups:
                    n += len(group)
                    dve.wait_ge(pt_hi_ready, RT * h + n)
                    for b, first in group:
                        cut = (slice(None), slice(0, b + 1), slice(b * P, (b + 1) * P))
                        nc.vector.tensor_tensor(pt_lo[cut], bank[from_bank][:, first:first + (b + 1) * P].rearrange(
                            "p (k n) -> p k n", k=b + 1), pt_hi[cut].bitcast(F32), ALU.subtract
                        ).then_inc(pt_lo_ready, 1)

            def gate_head(h):
                dve.wait_ge(pv_done, h + 1)
                tile = gate[:, bass.ds(h, 1), :].rearrange("p o n -> p (o n)")
                nc.vector.tensor_tensor(tile, bank[4][:], tile, ALU.mult).then_inc(gate_ready, 1)

            dve.wait_ge(consts_ready, 4)
            rotary_lo(0, 0)
            dve.wait_ge(w_used, FIN0)
            pair_lo(0, 0)
            head_lo(0, 0)
            head_lo(0, 1)
            mask_scores(0)
            normalise(0)
            pair_lo(1, 1)
            transposed_lo(0)

            def head(g, s):
                h = ROUND * g + s
                mask_scores(h)
                if s % 2 == 1:
                    normalise(h)
                    p = 2 * g + (s + 1) // 2
                    if not isinstance(p, int) or p < PAIRS:
                        rotary_lo(p, ((s + 1) // 2) % 2)
                        head_lo(p, 0)
                    gate_head(h - 1)
                else:
                    gate_head(h - 1)
                    normalise(h)
                    head_lo(2 * g + s // 2, 1)
                    p = 2 * g + s // 2 + 1
                    if not isinstance(p, int) or p < PAIRS:
                        pair_lo(p, (s // 2 + 1) % 2)
                transposed_lo(h)

            dve.wait_ge(evacuated, OUT0 + LATENTS + N_HEADS)
            heads_loop(dve, head)
            for k in range(CT):
                if k == 2:
                    gate_head(N_HEADS - 1)
                dve.wait_ge(g_hi_ready, CT + k + 1)
                nc.vector.tensor_tensor(fg_lo[k % 4][:], gate[:, k, :], fg_hi[k % 4][:].bitcast(F32), ALU.subtract
                                        ).then_inc(g_lo_ready, 1)
            dve.wait_ge(ln_rows_landed, 32)
            for r in range(RT):
                row_norm(RT + r, r, ln_rows_b, ALPHA)

        @block.tensor
        def _(pe):
            def product(out_ap, parts, start, stop):
                last = None
                for n, (s_hi, s_lo, m_hi, m_lo) in enumerate(parts):
                    for m, (a, b) in enumerate(((s_lo, m_hi), (s_hi, m_lo), (s_hi, m_hi))):
                        last = nc.tensor.matmul(out_ap, a, b, start=(start and n == 0 and m == 0),
                                                stop=(stop and n == len(parts) - 1 and m == 2))
                return last

            pe.wait_ge(ident_ready, 2)
            for r in range(RT):
                pe.wait_ge(x_landed[r], 16)
                for half in range(2):
                    q = 2 * r + half
                    wait(pe, xt_lo_ready, q - 3)
                    for k in range(4):
                        last = nc.tensor.transpose(bank[q % 4][:, k * P:(k + 1) * P],
                                                   x_in[:, r, (4 * half + k) * P:(4 * half + k + 1) * P], ident[:])
                    last.then_inc(x_turned, 1)

            def small_transposes():
                pe.wait_ge(small_landed, 16 * SMALL_DMAS)
                for t in range(CT):
                    last = nc.tensor.transpose(bank[4][:, t * TAPS:(t + 1) * TAPS],
                                               taps_raw[:, t * P:(t + 1) * P], ident[0:TAPS, 0:TAPS])
                last.then_inc(taps_turned, 1)
                nc.tensor.transpose(bank[5][:, 0:V_ALL], vec_raw[:], ident[0:V_ALL, 0:V_ALL]
                                    ).then_inc(vec_turned, 1)

            def columns(c, slot, out_bank, bank_free, hi, lo):
                pe.wait_ge(w_hi_ready, c + 1)
                pe.wait_ge(w_lo_ready, c + 1)
                wait(pe, evacuated, bank_free)
                parts = [(w_hi[slot][:, k * P:(k + 1) * P], w_lo[slot][:, k * P:(k + 1) * P],
                          hi[:, k, :], lo[:, k, :]) for k in range(KD)]
                product(bank[out_bank][:], parts, True, True).then_inc(w_used, 1)

            def value_gate(j):
                for s in range(ROUND):
                    for w in range(2):
                        c = 2 * ROUND * j + 2 * s + w
                        columns(c, (2 * s + w) % SLOTS, (2 * s + w) % 4, c - 3, xt_hi, xt_lo)
                        if isinstance(c, int) and c == 0:
                            small_transposes()
                    if s == 2 and (not isinstance(j, int) or j > 0):
                        convolve(j)

            def convolve(j):
                pe.wait_ge(diag_hi_ready, 2 * j)
                pe.wait_ge(diag_lo_ready, TAPS * j)
                pe.wait_ge(cu_lo_ready, j)
                pe.wait_ge(evacuated, 2 * ROUND * j)
                parts = [(diag_hi[:, k, :], diag_lo[:, k, :], cu_hi[:, k:k + SEQ], cu_lo[:, k:k + SEQ])
                         for k in range(TAPS)]
                product(bank[6][:], parts, True, True).then_inc(pe_conv_done, 1)

            pe.wait_ge(xt_lo_ready, 2 * RT)
            value_gate(0)
            with pe.Fori(1, ROUNDS) as j:
                value_gate(j)

            for i in range(CT):
                if i == MEAN_AT:
                    pe.wait_ge(consts_ready, 4)
                    pe.wait_ge(csum_done, CT)
                    nc.tensor.matmul(bank[7][:], ones[:], csum[:], start=True, stop=True).then_inc(mean_done, 1)
                if i == VAR_AT:
                    pe.wait_ge(vsum_done, CT // 2)
                    pe.wait_ge(vsum_odd_done, CT // 2)
                    for b in range(RT):
                        for n, part in enumerate((vsum, vsum_odd)):
                            last = nc.tensor.matmul(bank[7][:, b:b + 1], part[:, b * P:(b + 1) * P], ones[:, 0:1],
                                                    start=n == 0, stop=n == 1)
                    last.then_inc(var_done, 1)
                if i == VAR_AT + 1:
                    pe.wait_ge(rstd_diag_ready, RT)
                    nc.tensor.matmul(bank[7][:], ones[:], rstd_diag[:], start=True, stop=True).then_inc(rstd_spread, 1)
                columns(Z0 + i, i % SLOTS, i % 4, Z0 + i - 3, xt_hi, xt_lo)

            def output_projection(c0, hi, lo, ring, banks_free, after=None):
                def tile(k, r, half):
                    c = c0 + k
                    cut = slice(r * P, (r + 1) * P)
                    cols = slice(half * BANK, (half + 1) * BANK)
                    return product(bank[2 * r + half][:],
                                   [(hi(k)[:, cut], lo(k)[:, cut], w_hi[c % SLOTS][:, cols], w_lo[c % SLOTS][:, cols])],
                                   k == 0, k == CT - 1)

                def arrive(k):
                    pe.wait_ge(w_hi_ready, c0 + k + 1)
                    pe.wait_ge(w_lo_ready, c0 + k + 1)
                    pe.wait_ge(g_lo_ready, ring * CT + k + 1)

                for k in range(CT - RESIDENT):
                    arrive(k)
                    for r in range(RT):
                        if k == 0 and r in banks_free:
                            pe.wait_ge(*banks_free[r])
                        for half in range(HALVES):
                            last = tile(k, r, half)
                    last.then_inc(w_used, 1)
                for r in range(RT):
                    early = CT - 1 if r == 0 else CT - RESIDENT
                    for half in range(HALVES):
                        for k in range(CT - RESIDENT, early):
                            if half == 0:
                                arrive(k)
                            tile(k, r, half)
                    for half in range(HALVES):
                        for k in range(early, CT):
                            if r == half == 0:
                                arrive(k)
                            last = tile(k, r, half)
                            if r == RT - 1 and half == HALVES - 1 and k < CT - 1:
                                last.then_inc(w_used, 1)
                        last.then_inc(y_done, 1)
                        if after:
                            after(r, half)

            def turn_h(q):
                r, half = q // 2, q % 2
                pe.wait_ge(row_ready, 2 * r + 2)
                for k in range(4):
                    last = nc.tensor.transpose(bank[q][:, k * P:(k + 1) * P],
                                               res[:, r, (4 * half + k) * P:(4 * half + k + 1) * P], ident[:])
                    if q == 2 * (RT - 2) and k == 0:
                        last.then_inc(w_used, 1)
                last.then_inc(h_turned, 1)

            def turn_early(r, half):
                if (r, half) == (RT - 2, HALVES - 1):
                    turn_h(0)
                    turn_h(1)
                if (r, half) == (RT - 1, 0):
                    turn_h(2)
                    turn_h(3)

            output_projection(OUT0, lambda k: g_hi[:, k, :], lambda k: g_lo[:, k, :], 0,
                              {0: (evacuated, OUT0 - 2), 1: (evacuated, OUT0), 3: (rstd_ready, 1)},
                              turn_early)

            turn_h(4)
            turn_h(5)
            most, rest = slice(0, (RT - 1) * P), slice((RT - 1) * P, SEQ)

            def latent(n, cut):
                c = LAT0 + n
                pe.wait_ge(w_hi_ready, c + 1)
                pe.wait_ge(w_lo_ready, c + 1)
                parts = [(w_hi[c % SLOTS][:, k * P:(k + 1) * P], w_lo[c % SLOTS][:, k * P:(k + 1) * P],
                          ht_hi[:, k, cut], ht_lo[:, k, cut]) for k in range(KD)]
                return product(bank[n][:, cut], parts, True, True)

            pe.wait_ge(ht_lo_pool, 4)
            pe.wait_ge(ht_lo_ready, 2)
            latent(0, most)
            turn_h(6)
            turn_h(7)
            latent(1, most)
            pe.wait_ge(ht_lo_ready, 4)
            for n in range(2):
                latent(n, rest).then_inc(w_used, 1)
            for n in range(2, LATENTS):
                c = LAT0 + n
                columns(c, c % SLOTS, n % 4, OUT0 + n - 3 if n >= 4 else 0, ht_hi, ht_lo)

            def gate_round(j):
                for s in range(ROUND):
                    c = BZ0 + ROUND * j + s
                    columns(c, (BZ0 + s) % SLOTS, (LATENTS + s) % 4,
                            OUT0 + LATENTS + ROUND * j + s - 3, ht_hi, ht_lo)

            gate_round(0)
            for which in range(2):
                pe.wait_ge(b_step, SQUARE_STEPS[which])
                nc.tensor.matmul(bank[4 + which][:], ones[:], b_sum[:, which, :], start=True, stop=True
                                 ).then_inc(b_sum_done, 1)
            with pe.Fori(1, ROUNDS - 1) as j:
                gate_round(j)

            def project_pair(p, slot):
                bh, bl = bundle_hi[slot], bundle_lo[slot]
                pe.wait_ge(bundle_lo_ready, 2 * p + 1)
                wait(pe, proj_lo_ready, 6 * p - 3)
                cols = [(QR + k * 2 * ROPE, QR + (k + 1) * 2 * ROPE) for k in range(KQ)]
                product(bank[PROJ_BANK[0]][:], [(piece(bh, *cols[k]), piece(bl, *cols[k]), cq_hi[:, k, :], cq_lo[:, k, :])
                                                for k in range(KQ)], True, True).then_inc(proj_done, 1)
                cols = [(UV + k * 2 * V_DIM, UV + (k + 1) * 2 * V_DIM) for k in range(KV)]
                for half in range(2):
                    wait(pe, proj_lo_ready, 6 * p - 1 + half)
                    for t in range(2):
                        cut = slice((2 * half + t) * P, (2 * half + t + 1) * P)
                        last = product(bank[PROJ_BANK[1 + half]][:, t * 2 * V_DIM:(t + 1) * 2 * V_DIM],
                                       [(ckv_hi[:, k, cut], ckv_lo[:, k, cut], piece(bh, *cols[k]), piece(bl, *cols[k]))
                                        for k in range(KV)], True, True)
                    last.then_inc(proj_done, 1)

            def project_head(p, e, slot):
                bh, bl = bundle_hi[slot], bundle_lo[slot]
                pe.wait_ge(bundle_lo_ready, 2 * p + 2)
                if e == 0:
                    pe.wait_ge(qr_kept, p + 1)
                else:
                    pe.wait_ge(proj_lo_ready, 6 * p + 4)
                cols = [(UK + k * 2 * NOPE + e * NOPE, UK + k * 2 * NOPE + (e + 1) * NOPE) for k in range(KV)]
                product(bank[PROJ_BANK[3 + 2 * e]][:],
                        [(piece(bh, *cols[k]), piece(bl, *cols[k]), ckv_hi[:, k, :], ckv_lo[:, k, :]) for k in range(KV)],
                        True, True).then_inc(proj_done, 1)
                pe.wait_ge(proj_lo_ready, 6 * p + 1 + e)
                cols = [(QN + k * 2 * NOPE + e * NOPE, QN + k * 2 * NOPE + (e + 1) * NOPE) for k in range(KQ)]
                product(bank[PROJ_BANK[4 + 2 * e]][:],
                        [(piece(bh, *cols[k]), piece(bl, *cols[k]), cq_hi[:, k, :], cq_lo[:, k, :]) for k in range(KQ)],
                        True, True).then_inc(proj_done, 1)

            def scores(h, p, e, slot):
                pe.wait_ge(proj_lo_ready, 6 * p + 4 + 2 * e)
                half, stack = head_rows[e], qr_stack[slot][e]
                for i, b in enumerate(score_order):
                    n = (b + 1) * P
                    cut = slice(b * P, n)
                    if i in (0, 3):
                        wait(pe, masked, RT * h + (0, None, None, 1)[i])
                    else:
                        wait(pe, pt_lo_ready, RT * (h - 1) + i)
                    product(bank[score_bank[i]][:, 0:n],
                            [(q_hi[e][:, cut], q_lo[e][:, cut], k_hi[e][:, 0:n], k_lo[e][:, 0:n])], True, False)
                    if i == 0:
                        pe.wait_ge(qr_lo_ready, 32 * p + 32)
                    nc.tensor.matmul(bank[score_bank[i]][:, 0:n], stack[half, cut], kr_lo[half, 0:n], start=False, stop=False)
                    nc.tensor.matmul(bank[score_bank[i]][:, 0:n], stack[:, cut], kr_hi[:, 0:n], start=False, stop=True
                                     ).then_inc(scores_done, 1)

            def turn(h):
                for to_bank, group, normalised in turn_groups:
                    pe.wait_ge(prob_ready, RT * h + normalised)
                    for b, first in group:
                        for k in range(b + 1):
                            last = nc.tensor.transpose(bank[to_bank][:, first + k * P:first + (k + 1) * P],
                                                       prob[:, (prob_at[b] + k) * P:(prob_at[b] + k + 1) * P],
                                                       ident[:])
                    last.then_inc(prob_turned, 1)

            def attend(h, e, slot):
                pe.wait_ge(pt_lo_ready, RT * (h + 1))
                wait(pe, gate_ready, h)
                cols = slice(e * V_DIM, (e + 1) * V_DIM)
                for k in range(RT):
                    last = product(bank[4][:, k * P:], [(v_hi[slot][:, k, cols], v_lo[slot][:, k, cols],
                                                        pt_hi[:, k, k * P:], pt_lo[:, k, k * P:])],
                                   k == 0, k == RT - 1)
                last.then_inc(pv_done, 1)

            pe.wait_ge(lat_lo_ready, LATENTS)
            pe.wait_ge(b_var_ready, 2)
            project_pair(0, FIRST)
            gate_round(ROUNDS - 1)
            project_head(0, 0, FIRST)
            project_head(0, 1, FIRST)
            pe.wait_ge(evacuated, OUT0 + LATENTS + N_HEADS)
            scores(0, 0, 0, 0)
            project_pair(1, 1)
            turn(0)

            def head(g, s):
                h = ROUND * g + s
                scores(h, 2 * g + s // 2, s % 2, (s // 2) % 2)
                if s % 2 == 1:
                    p = 2 * g + (s + 1) // 2
                    if not isinstance(p, int) or p < PAIRS:
                        project_head(p, 0, ((s + 1) // 2) % 2)
                    attend(h - 1, (s - 1) % 2, ((s - 1) // 2) % 2)
                else:
                    attend(h - 1, (s - 1) % 2, ((s - 1) // 2) % 2)
                    project_head(2 * g + s // 2, 1, (s // 2) % 2)
                    p = 2 * g + s // 2 + 1
                    if not isinstance(p, int) or p < PAIRS:
                        project_pair(p, (s // 2 + 1) % 2)
                turn(h)

            heads_loop(pe, head)
            attend(N_HEADS - 1, (N_HEADS - 1) % 2, ((N_HEADS - 1) // 2) % 2)
            output_projection(FIN0, lambda k: fg_hi[k % 4], lambda k: fg_lo[k % 4], 1,
                              {2: (gate_ready, N_HEADS)})


INPUTS = ["x", "positions", "ln_g", "ln_b", "a_w_in", "a_b_in", "a_conv_w", "a_conv_b", "a_norm_g",
          "a_norm_b", "a_w_out", "a_b_out", "kv_w_down", "kv_norm_g", "kv_w_uk", "kv_w_uv", "b_w_in",
          "b_q_norm_g", "b_w_uq", "b_w_out"]


def kernel(**inputs):
    import numpy as _np
    import concourse.bacc as _bacc
    from concourse import mybir as _mybir
    from concourse.bass_utils import run_bass_kernel_spmd as _run

    nc = _bacc.Bacc("TRN2", target_bir_lowering=False, num_devices=1)
    arrays = {f"in_{name}_dram": _np.ascontiguousarray(inputs[name]) for name in INPUTS}
    pair = _np.arange(0, ROPE, 2, dtype=_np.float32) / _np.float32(ROPE)
    table = _np.ones((P, 2), _np.float32)
    table[:, 0] = _np.tile(_np.power(_np.float32(ROPE_THETA), -pair), 4)
    table[:, 1] = _np.tile(_np.repeat(_np.array([-1.0, 1.0], _np.float32), ROPE // 2), 2)
    arrays["in_rope_freq_dram"] = table
    args = [nc.dram_tensor(name, a.shape, _mybir.dt.from_np(a.dtype), kind="ExternalInput").ap()
            for name, a in arrays.items()]
    args.append(nc.dram_tensor("out_0_dram", (1, SEQ, D_MODEL), _mybir.dt.float32, kind="ExternalOutput").ap())
    trunk_kernel(nc, *args)
    return _run(nc, [arrays], core_ids=[0]).results[0]["out_0_dram"]
```
